# Optimizing a Trainium2 kernel written in Bass

```python
import jax, jax.numpy as jnp
from jax import lax
import numpy as np

D_MODEL = 1024
BATCH = 1
SEQ = 256
DEPTH = 2

GRID_W = 64
CTX_LEN = 256
LN_EPS = 1e-5
D_CONV = 512
CONV_WIDTH = 31
N_Q_HEADS = 8
N_KV_HEADS = 2
HEAD_DIM = 64
WINDOW = 128
BLOCK = 128
ROPE_BASE = 10000.0
D_ATTN = N_Q_HEADS * HEAD_DIM
D_KV = N_KV_HEADS * HEAD_DIM
N_MLSTM_HEADS = 4
MLSTM_HEAD_DIM = 128
D_MLSTM = N_MLSTM_HEADS * MLSTM_HEAD_DIM
CHUNK = 64
N_GATE_COLS = 2 * 2 * N_MLSTM_HEADS
N_BRANCHES = 3
IN_SPLITS = (2 * D_CONV, D_ATTN, D_KV, D_KV, D_MLSTM, D_MLSTM, D_MLSTM, D_MLSTM, N_GATE_COLS, N_BRANCHES * D_MODEL)
D_IN = 2 * D_CONV + D_ATTN + 2 * D_KV + 4 * D_MLSTM + N_GATE_COLS + N_BRANCHES * D_MODEL
N_EXPERTS = 16
N_GROUPS = 4
EXPERTS_PER_GROUP = N_EXPERTS // N_GROUPS
TOP_K = 2
D_EXPERT = 512

kernel_name = "hybrid_conv_swa_mlstm_moe_dit"

def layer_norm(x, g, b):
    xf = x.astype(jnp.float32)
    mu = xf.mean(-1, keepdims=True)
    var = jnp.square(xf - mu).mean(-1, keepdims=True)
    y = (xf - mu) * lax.rsqrt(var + LN_EPS)
    return (y * g.astype(jnp.float32) + b.astype(jnp.float32)).astype(x.dtype)

def split_in(p):
    offs, acc = [], 0
    for s in IN_SPLITS[:-1]:
        acc += s
        offs.append(acc)
    return jnp.split(p, offs, axis=-1)

def conv_module(a_in, w, b, g, beta):
    val, gate = jnp.split(a_in, 2, axis=-1)
    u = val * jax.nn.sigmoid(gate)
    pad = CONV_WIDTH // 2
    y = lax.conv_general_dilated(u, w[:, None, :], window_strides=(1,), padding=[(pad, pad)],
                                 dimension_numbers=("NWC", "WIO", "NWC"), feature_group_count=D_CONV) + b
    return jax.nn.silu(layer_norm(y, g, b * 0 + beta) if False else layer_norm(y, g, beta))

def rope_half(u, pos):
    nf = u.shape[-1] // 2
    inv = ROPE_BASE ** (-jnp.arange(nf, dtype=jnp.float32) / nf)
    ang = pos.astype(jnp.float32)[:, None] * inv[None, :]
    cos = jnp.cos(ang)[None, :, None, :]
    sin = jnp.sin(ang)[None, :, None, :]
    u1 = u[..., :nf].astype(jnp.float32)
    u2 = u[..., nf:].astype(jnp.float32)
    return jnp.concatenate([u1 * cos - u2 * sin, u1 * sin + u2 * cos], axis=-1).astype(u.dtype)

def axial_rope(t, row_pos, col_pos):
    half = t.shape[-1] // 2
    return jnp.concatenate([rope_half(t[..., :half], row_pos), rope_half(t[..., half:], col_pos)], axis=-1)

def sink_softmax(scores, sink):
    m = sink
    for s in scores:
        m = jnp.maximum(m, s.max(-1, keepdims=True))
    ex = [jnp.exp(s - m) for s in scores]
    denom = jnp.exp(sink - m)
    for e in ex:
        denom = denom + e.sum(-1, keepdims=True)
    return [e / denom for e in ex]

def banded_attention(q, k, v, kc, vc, sink):
    B, S, H, Dh = q.shape
    G = H // N_KV_HEADS
    nb = S // BLOCK
    scale = Dh ** -0.5
    qb = q.reshape(B, nb, BLOCK, N_KV_HEADS, G, Dh)

    def band(t):
        tb = t.reshape(B, nb, BLOCK, N_KV_HEADS, Dh)
        tp = jnp.pad(tb, ((0, 0), (1, 1), (0, 0), (0, 0), (0, 0)))
        return jnp.concatenate([tp[:, :-2], tp[:, 1:-1], tp[:, 2:]], axis=2)

    kb, vb = band(k), band(v)
    s_loc = jnp.einsum("bnqhgd,bnkhd->bnhgqk", qb, kb).astype(jnp.float32) * scale
    blk = jnp.arange(nb)[:, None]
    qpos = blk * BLOCK + jnp.arange(BLOCK)[None, :]
    kpos = blk * BLOCK - BLOCK + jnp.arange(3 * BLOCK)[None, :]
    valid = ((jnp.abs(qpos[:, :, None] - kpos[:, None, :]) <= WINDOW)
             & (kpos[:, None, :] >= 0) & (kpos[:, None, :] < S))
    s_loc = jnp.where(valid[None, :, None, None], s_loc, -jnp.inf)
    s_ctx = jnp.einsum("bnqhgd,blhd->bnhgql", qb, kc).astype(jnp.float32) * scale
    sink_l = jnp.broadcast_to(sink.astype(jnp.float32).reshape(1, 1, N_KV_HEADS, G, 1, 1), s_loc.shape[:-1] + (1,))
    p_loc, p_ctx = sink_softmax([s_loc, s_ctx], sink_l)
    o = (jnp.einsum("bnhgqk,bnkhd->bnqhgd", p_loc.astype(v.dtype), vb)
         + jnp.einsum("bnhgql,blhd->bnqhgd", p_ctx.astype(vc.dtype), vc))
    return o.reshape(B, S, H * Dh)

def context_attention(qc, kc, vc, sink):
    B, L, H, Dh = qc.shape
    G = H // N_KV_HEADS
    qg = qc.reshape(B, L, N_KV_HEADS, G, Dh)
    s = jnp.einsum("bqhgd,bkhd->bhgqk", qg, kc).astype(jnp.float32) * (Dh ** -0.5)
    sink_l = jnp.broadcast_to(sink.astype(jnp.float32).reshape(1, N_KV_HEADS, G, 1, 1), s.shape[:-1] + (1,))
    (p,) = sink_softmax([s], sink_l)
    o = jnp.einsum("bhgqk,bkhd->bqhgd", p.astype(vc.dtype), vc)
    return o.reshape(B, L, H * Dh)

def mlstm_scan(q, k, v, ig, lf, state):
    B, T, H, dh = q.shape
    nc = T // CHUNK
    tril = jnp.tril(jnp.ones((CHUNK, CHUNK), dtype=bool))

    def to_chunks(t):
        return jnp.moveaxis(t.reshape((B, nc, CHUNK) + t.shape[2:]), 1, 0)

    def step(carry, inp):
        C, n, m = carry
        qc, kc, vc, igc, lfc = inp
        b = jnp.cumsum(lfc, axis=1)
        log_d = b[:, :, None, :] - b[:, None, :, :] + igc[:, None, :, :]
        log_d = jnp.where(tril[None, :, :, None], log_d, -jnp.inf)
        inter = b + m[:, None, :]
        m_out = jnp.maximum(inter, log_d.max(axis=2))
        w_intra = jnp.exp(log_d - m_out[:, :, None, :])
        w_inter = jnp.exp(inter - m_out)
        qk = jnp.einsum("bjhd,bshd->bjsh", qc, kc) * w_intra
        num = jnp.einsum("bjsh,bshe->bjhe", qk, vc) + w_inter[..., None] * jnp.einsum("bjhd,bhde->bjhe", qc, C)
        den = qk.sum(axis=2) + w_inter * jnp.einsum("bjhd,bhd->bjh", qc, n)
        h = num / jnp.maximum(jnp.abs(den), jnp.exp(-m_out))[..., None]
        b_last = b[:, -1, :]
        log_w = b_last[:, None, :] - b + igc
        m_new = jnp.maximum(b_last + m, log_w.max(axis=1))
        w_s = jnp.exp(log_w - m_new[:, None, :])
        decay = jnp.exp(b_last + m - m_new)
        C_new = decay[..., None, None] * C + jnp.einsum("bsh,bshd,bshe->bhde", w_s, kc, vc)
        n_new = decay[..., None] * n + jnp.einsum("bsh,bshd->bhd", w_s, kc)
        return (C_new, n_new, m_new), h

    xs = (to_chunks(q), to_chunks(k), to_chunks(v), to_chunks(ig), to_chunks(lf))
    state, h = lax.scan(step, state, xs)
    h = jnp.moveaxis(h, 0, 1).reshape(B, T, H, dh)
    return h, state

def mlstm_bidir(q, k, v, gates, init_fwd, init_bwd):
    ig_f, lf_f = gates[:, :, 0, 0], jax.nn.log_sigmoid(gates[:, :, 0, 1])
    ig_b, lf_b = gates[:, :, 1, 0], jax.nn.log_sigmoid(gates[:, :, 1, 1])
    h_f, st_f = mlstm_scan(q, k, v, ig_f, lf_f, init_fwd)
    fl = lambda t: jnp.flip(t, axis=1)
    h_b, st_b = mlstm_scan(fl(q), fl(k), fl(v), fl(ig_b), fl(lf_b), init_bwd)
    return h_f + fl(h_b), st_f, st_b

def head_norm(h, g):
    mu = h.mean(-1, keepdims=True)
    var = jnp.square(h - mu).mean(-1, keepdims=True)
    y = (h - mu) * lax.rsqrt(var + LN_EPS)
    return y.reshape(h.shape[:2] + (-1,)) * g.astype(jnp.float32)

def token_mixer(u, uc, row_pos, col_pos, w_in, conv_w, conv_b, conv_ln_g, conv_ln_b, w_a_out, attn_sink,
                w_b_out, mlstm_gate_b, mlstm_norm_g, w_c_out, w_out, need_ctx_out):
    B, S, _ = u.shape
    L = uc.shape[1]
    a_in, q, k, v, mq, mk, mv, mo, mg, bg = split_in(u @ w_in)
    a_in_c, q_c, k_c, v_c, mq_c, mk_c, mv_c, mo_c, mg_c, bg_c = split_in(uc @ w_in)

    qh = axial_rope(q.reshape(B, S, N_Q_HEADS, HEAD_DIM), row_pos, col_pos)
    kh = axial_rope(k.reshape(B, S, N_KV_HEADS, HEAD_DIM), row_pos, col_pos)
    vh = v.reshape(B, S, N_KV_HEADS, HEAD_DIM)
    kch = k_c.reshape(B, L, N_KV_HEADS, HEAD_DIM)
    vch = v_c.reshape(B, L, N_KV_HEADS, HEAD_DIM)
    y_b = banded_attention(qh, kh, vh, kch, vch, attn_sink)

    def heads(t, T):
        return t.reshape(B, T, N_MLSTM_HEADS, MLSTM_HEAD_DIM).astype(jnp.float32)
    k_scale = MLSTM_HEAD_DIM ** -0.5
    gb = mlstm_gate_b.astype(jnp.float32)
    g_lat = mg.astype(jnp.float32).reshape(B, S, 2, 2, N_MLSTM_HEADS) + gb
    g_ctx = mg_c.astype(jnp.float32).reshape(B, L, 2, 2, N_MLSTM_HEADS) + gb
    zero = (jnp.zeros((B, N_MLSTM_HEADS, MLSTM_HEAD_DIM, MLSTM_HEAD_DIM), jnp.float32),
            jnp.zeros((B, N_MLSTM_HEADS, MLSTM_HEAD_DIM), jnp.float32),
            jnp.zeros((B, N_MLSTM_HEADS), jnp.float32))
    h_ctx, st_f, st_b = mlstm_bidir(heads(mq_c, L), heads(mk_c, L) * k_scale, heads(mv_c, L), g_ctx, zero, zero)
    h_lat, _, _ = mlstm_bidir(heads(mq, S), heads(mk, S) * k_scale, heads(mv, S), g_lat, st_f, st_b)
    y_c = (jax.nn.sigmoid(mo.astype(jnp.float32)) * head_norm(h_lat, mlstm_norm_g)).astype(u.dtype)

    def merge(ya, yb, yc, gates):
        ga, gbr, gc = jnp.split(jax.nn.sigmoid(gates), N_BRANCHES, axis=-1)
        return (ga * (ya @ w_a_out) + gbr * (yb @ w_b_out) + gc * (yc @ w_c_out)) @ w_out

    y_a = conv_module(a_in, conv_w, conv_b, conv_ln_g, conv_ln_b)
    y = merge(y_a, y_b, y_c, bg)
    if need_ctx_out:
        y_a_c = conv_module(a_in_c, conv_w, conv_b, conv_ln_g, conv_ln_b)
        y_b_c = context_attention(q_c.reshape(B, L, N_Q_HEADS, HEAD_DIM), kch, vch, attn_sink)
        y_c_c = (jax.nn.sigmoid(mo_c.astype(jnp.float32)) * head_norm(h_ctx, mlstm_norm_g)).astype(uc.dtype)
        y_ctx = merge(y_a_c, y_b_c, y_c_c, bg_c)
    else:
        y_ctx = None
    return y, y_ctx

def grouped_moe(t, w_router, b_router, w_gu, w_dn):
    N, D = t.shape
    scores = jax.nn.sigmoid((t @ w_router).astype(jnp.float32))
    sel = (scores + b_router.astype(jnp.float32)).reshape(N, N_GROUPS, EXPERTS_PER_GROUP)
    group_score = lax.top_k(sel, TOP_K)[0].sum(-1)
    g_idx = jnp.argmax(group_score, axis=-1)
    idx = jnp.broadcast_to(g_idx[:, None, None], (N, 1, EXPERTS_PER_GROUP))
    in_group = jnp.take_along_axis(sel, idx, axis=1)[:, 0]
    _, loc = lax.top_k(in_group, TOP_K)
    e_idx = g_idx[:, None] * EXPERTS_PER_GROUP + loc
    w = jnp.take_along_axis(scores, e_idx, axis=1)
    w = w / w.sum(-1, keepdims=True)
    gates = jnp.sum(jax.nn.one_hot(e_idx, N_EXPERTS, dtype=jnp.float32) * w[..., None], axis=1)
    out = jnp.zeros((N, D), jnp.float32)
    for e in range(N_EXPERTS):
        g_, u_ = jnp.split(t @ w_gu[e], 2, axis=-1)
        out = out + gates[:, e:e + 1] * ((jax.nn.silu(g_) * u_) @ w_dn[e]).astype(jnp.float32)
    return out.astype(t.dtype)

def setup_inputs(seed: int = 0) -> dict:
    key = jax.random.key(seed)
    ks = iter(jax.random.split(key, 40))
    f32 = jnp.float32

    def nrm(shape, scale):
        return jax.random.normal(next(ks), shape, f32) * scale

    D = D_MODEL
    beta = (8.0 * DEPTH) ** -0.25
    f_bias = jnp.linspace(3.0, 6.0, N_MLSTM_HEADS, dtype=f32)
    ig_b = nrm((DEPTH, 2, N_MLSTM_HEADS), 0.1)
    fg_b = f_bias + nrm((DEPTH, 2, N_MLSTM_HEADS), 0.1)
    return {
        "x": nrm((BATCH, SEQ, D), 1.0),
        "c": nrm((BATCH, D), 1.0),
        "ctx": nrm((BATCH, CTX_LEN, D), 1.0),
        "c_ctx": nrm((D,), 1.0),
        "ln_in_g": 1.0 + nrm((D,), 0.02),
        "ln_in_b": nrm((D,), 0.02),
        "w_router": nrm((D, N_EXPERTS), D ** -0.5),
        "b_router": nrm((N_EXPERTS,), 0.01),
        "w_mod": nrm((DEPTH, D, 6 * D), D ** -0.5),
        "b_mod": nrm((DEPTH, 6 * D), 0.02),
        "w_in": nrm((DEPTH, D, D_IN), D ** -0.5),
        "conv_w": nrm((DEPTH, CONV_WIDTH, D_CONV), CONV_WIDTH ** -0.5),
        "conv_b": nrm((DEPTH, D_CONV), 0.02),
        "conv_ln_g": 1.0 + nrm((DEPTH, D_CONV), 0.02),
        "conv_ln_b": nrm((DEPTH, D_CONV), 0.02),
        "w_a_out": nrm((DEPTH, D_CONV, D), D_CONV ** -0.5),
        "attn_sink": nrm((DEPTH, N_Q_HEADS), 0.5),
        "w_b_out": nrm((DEPTH, D_ATTN, D), D_ATTN ** -0.5),
        "mlstm_gate_b": jnp.stack([ig_b, fg_b], axis=2),
        "mlstm_norm_g": 1.0 + nrm((DEPTH, D_MLSTM), 0.02),
        "w_c_out": nrm((DEPTH, D_MLSTM, D), D_MLSTM ** -0.5),
        "w_out": nrm((DEPTH, D, D), beta * D ** -0.5),
        "ln1_g": 1.0 + nrm((DEPTH, D), 0.02),
        "ln1_b": nrm((DEPTH, D), 0.02),
        "moe_w_gu": nrm((DEPTH, N_EXPERTS, D, 2 * D_EXPERT), D ** -0.5),
        "moe_w_dn": nrm((DEPTH, N_EXPERTS, D_EXPERT, D), beta * D_EXPERT ** -0.5),
        "ln2_g": 1.0 + nrm((DEPTH, D), 0.02),
        "ln2_b": nrm((DEPTH, D), 0.02),
    }

def reference(x, c, ctx, c_ctx, ln_in_g, ln_in_b, w_router, b_router, w_mod, b_mod, w_in, conv_w, conv_b,
              conv_ln_g, conv_ln_b, w_a_out, attn_sink, w_b_out, mlstm_gate_b, mlstm_norm_g, w_c_out, w_out,
              ln1_g, ln1_b, moe_w_gu, moe_w_dn, ln2_g, ln2_b):
    B, S, D = x.shape
    L = ctx.shape[1]
    alpha = (2.0 * DEPTH) ** 0.25
    rows = S // GRID_W
    row_pos = jnp.repeat(jnp.arange(rows), GRID_W)
    col_pos = jnp.arange(rows * GRID_W) % GRID_W

    h = layer_norm(x, ln_in_g, ln_in_b)
    hc = layer_norm(ctx, ln_in_g, ln_in_b)
    silu_c = jax.nn.silu(c)
    silu_cc = jax.nn.silu(c_ctx)
    for l in range(DEPTH):
        need_ctx = l < DEPTH - 1
        sh1, sc1, g1, sh2, sc2, g2 = [t[:, None, :] for t in jnp.split(silu_c @ w_mod[l] + b_mod[l], 6, axis=-1)]
        csh1, csc1, cg1, csh2, csc2, cg2 = jnp.split(silu_cc @ w_mod[l] + b_mod[l], 6, axis=-1)

        u = h * (1 + sc1) + sh1
        uc = hc * (1 + csc1) + csh1
        y, y_ctx = token_mixer(u, uc, row_pos, col_pos, w_in[l], conv_w[l], conv_b[l], conv_ln_g[l], conv_ln_b[l],
                               w_a_out[l], attn_sink[l], w_b_out[l], mlstm_gate_b[l], mlstm_norm_g[l], w_c_out[l],
                               w_out[l], need_ctx)
        h = layer_norm(alpha * h + g1 * y, ln1_g[l], ln1_b[l])

        u2 = h * (1 + sc2) + sh2
        if need_ctx:
            hc = layer_norm(alpha * hc + cg1 * y_ctx, ln1_g[l], ln1_b[l])
            uc2 = hc * (1 + csc2) + csh2
            tokens = jnp.concatenate([u2.reshape(B * S, D), uc2.reshape(B * L, D)], axis=0)
            f = grouped_moe(tokens, w_router, b_router, moe_w_gu[l], moe_w_dn[l])
            f_lat = f[:B * S].reshape(B, S, D)
            f_ctx = f[B * S:].reshape(B, L, D)
            hc = layer_norm(alpha * hc + cg2 * f_ctx, ln2_g[l], ln2_b[l])
        else:
            f_lat = grouped_moe(u2.reshape(B * S, D), w_router, b_router, moe_w_gu[l], moe_w_dn[l]).reshape(B, S, D)
        h = layer_norm(alpha * h + g2 * f_lat, ln2_g[l], ln2_b[l])
    return h


_drawn_inputs = setup_inputs


def setup_inputs(seed=0):
    import zlib

    import numpy as np

    out = dict(_drawn_inputs(seed))
    spreads = {}
    factors = {'conv_b': 6.042,
     'conv_ln_g': 7.382,
     'conv_ln_b': 8.0,
     'attn_sink': 22.82,
     'mlstm_norm_g': 7.351}
    for name, (base, spread) in spreads.items():
        noise = np.random.default_rng([zlib.crc32(name.encode()), seed]).standard_normal(out[name].shape)
        drawn = base * np.exp(spread * noise) if base else spread * noise
        out[name] = __import__('jax').numpy.asarray(drawn.astype(out[name].dtype))
    for name, factor in factors.items():
        out[name] = (out[name] * factor).astype(out[name].dtype)
    return out
```

```python
from contextlib import ExitStack

import numpy as np

import concourse.bass as bass
from concourse import mybir

F32 = mybir.dt.float32
ALU = mybir.AluOpType
ACT = mybir.ActivationFunctionType
AX_X = mybir.AxisListType.X

P = 128
D = 1024
KD = D // P
DEPTH = 2
S_LAT, S_CTX = 256, 256
T = S_LAT + S_CTX
TT = T // P
D_CONV, TAPS = 512, 31
PAD = TAPS // 2
CT = D_CONV // P
NQ, NKV, DH = 8, 2, 64
NH, MH = 4, 128
WINDOW, GRID_W, ROPE_BASE = 128, 64, 10000.0
NE, NG, EPG, DE = 16, 4, 4, 512
FT = DE // P
EPS = 1e-5
ALPHA = (2.0 * DEPTH) ** 0.25
A_SCALE = DH ** -0.5
K_SCALE = MH ** -0.5
NEG = -1e30
NS = 6
SLOT = KD * 256
BANKS = 8

C_A, C_Q, C_K, C_V = 0, 1024, 1536, 1664
C_MQ, C_MK, C_MV, C_MO, C_MG, C_BG = 1792, 2304, 2816, 3328, 3840, 3856
SH1, SC1, G1, SH2, SC2, G2 = 0, 8, 16, 24, 32, 40
N_MOD = 6 * KD

UNITS = [(h, d) for h in range(NH) for d in range(2)]


def token_tiles(layer):
    return TT if layer < DEPTH - 1 else S_LAT // P


def attention_units(layer):
    return [(qt, h) for qt in range(token_tiles(layer)) for h in range(NQ)]


def key_range(qt):
    return (0, T) if qt < S_LAT // P else (S_LAT, T)


def scan_ranges(s, d, n):
    lat, ctx = (0, 2 * P), None
    if s == 0:
        full = [(P, 2 * P)] if d == 0 else []
    elif s == 1:
        full = [] if d == 0 else [(0, P)]
    elif s == 2:
        full = [lat, (3 * P, 4 * P)] if d == 0 else [lat]
    else:
        full = [lat] if d == 0 else [lat, (2 * P, 3 * P)]
    return [r for r in full if r[1] <= n]


def scan_tiles(t, d):
    return [s for s in range(TT) if s == t or any(a <= t * P < b for a, b in scan_ranges(s, d, T))]


def joined(ranges):
    out = []
    for a, b in sorted(ranges):
        if out and out[-1][1] == a:
            out[-1] = (out[-1][0], b)
        else:
            out.append((a, b))
    return out


def psum_order():
    order = [("prep",)]
    for l in range(DEPTH):
        nt = token_tiles(l)
        order += [("mod", l)]
        order += [("tr1", l, k) for k in range(KD)]
        for j in range(CT):
            order += [("val", l, j), ("gate", l, j)]
        order += [("v", l), ("ig", l)]
        order += [("qk", l, t) for t in (4, 5, 0, 1, 2, 3)]
        order += [("perm", l, t) for t in range(6)]
        order += [("mqk", l, t) for t in range(8)]
        order += [("mv", l, c, h) for c in range(2) for h in range(TT // 2)]
        order += [("mo", l, c, h) for c in range(2) for h in range(nt // 2)]
        order += [("mean", l), ("var", l), ("cols", l)]
        n = len(attention_units(l))
        for i in range(n + 3):
            order += [("S", l, i)] if i < n else []
            order += [("PT", l, i - 2)] if 0 <= i - 2 < n else []
            order += [("PV", l, i - 3)] if 0 <= i - 3 < n else []
        n = len(UNITS)
        for i in range(n + 2):
            order += [("bm", l, i)] if i < n else []
            order += [("st", l, i - 1, s) for s in range(TT)] if 0 <= i - 1 < n else []
            order += [("hv", l, i - 2, t) for t in range(nt // 2)] if 0 <= i - 2 < n else []
        order += [("yc", l, h) for h in range(NH)]
        order += [(b, l, j) for j in range(KD) for b in ("bga", "bgb", "bgc", "ya", "yb", "yc_")]
        order += [("g1", l, c) for c in range(4)]
        order += [("out", l, c, h) for c in range(4) for h in range(nt // 2)]
        order += [("tr2", l, k) for k in range(KD)]
        order += [("router", l)]
        order += [("moe", l, b, x) for b in range(2)
                  for x in [(g, j) for j in range(FT) for g in "gu"]
                  + [("o", c, t) for c in range(2) for t in range(nt)]]
        order += [("g2", l, c) for c in range(4)]
    place, n = {}, 0
    for key in order:
        if key == ("moe", key[1] if len(key) > 1 else 0, 0, ("g", 0)):
            body = sum(k[0] == "moe" and k[1] == key[1] for k in order)
            assert body % BANKS == 0
        place[key] = (n % BANKS, n // BANKS)
        n += 1
        if key[0] == "moe" and (key[2], key[3]) == (1, ("o", 1, token_tiles(key[1]) - 1)):
            n += body * (NE // 2 - 1)
    return order, place


def host_constants():
    nf = DH // 4
    inv = ROPE_BASE ** (-np.arange(nf, dtype=np.float32) / np.float32(nf))
    pos = np.arange(S_LAT)
    row, col = pos // GRID_W, pos % GRID_W
    d = np.arange(P) % DH
    ang = np.where((d < DH // 2)[:, None], row[None, :], col[None, :]).astype(np.float32) * inv[d % nf][:, None]
    second = (d % (2 * nf)) >= nf
    cos, sin = np.cos(ang), np.where(second[:, None], np.sin(ang), -np.sin(ang))
    partner = np.arange(P) + np.where(second, -nf, nf)
    perm = np.zeros((P, P), np.float32)
    perm[partner, np.arange(P)] = 1.0
    q = np.arange(S_LAT).reshape(2, P, 1)
    k = np.arange(T).reshape(1, 1, T)
    band = np.where((np.abs(q - k) <= WINDOW) | (k >= S_LAT), 0.0, NEG).astype(np.float32).transpose(1, 0, 2)
    s, t = np.arange(P)[:, None], np.arange(P)[None, :]
    tri = np.stack([np.where(s <= t, 0.0, NEG), np.where(s >= t, 0.0, NEG)], 1).astype(np.float32)
    return {
        "k_ident": np.eye(P, dtype=np.float32),
        "k_perm": perm,
        "k_rope": np.stack([cos, sin], 1).astype(np.float32),
        "k_band": np.ascontiguousarray(band),
        "k_tri": np.ascontiguousarray(tri),
    }


def build(nc, a, out):
    order, place = psum_order()

    with ExitStack() as ctx:
        def sb(name, shape):
            return ctx.enter_context(nc.sbuf_tensor(name, shape, F32))

        H = sb("H", [P, TT, D])
        uT = sb("uT", [P, KD, T])
        ring = sb("ring", [P, NS, SLOT])
        arena = sb("arena", [P, KD, T])
        upad = sb("upad", [P, CT, 2, S_LAT + 2 * PAD])
        convT = sb("convT", [P, CT, T])
        qkT = sb("qkT", [P, 6, T])
        v_tok = sb("v_tok", [P, TT, NKV * DH])
        mqk = sb("mqk", [P, 8, T])
        mv_tok = sb("mv_tok", [P, TT, NH, MH + 1])
        mo_tok = sb("mo_tok", [P, TT, NH, MH])
        yab = sb("yab", [P, 8, T])
        wgate = sb("wgate", [P, KD, P])
        wrouter = sb("wrouter", [P, KD, NE])
        ident = sb("ident", [P, P])
        perm = sb("perm", [P, P])
        rope = sb("rope", [P, 2, S_LAT])
        band = sb("band", [P, 2, T])
        tri = sb("tri", [P, 2, P])
        ones_mean = sb("ones_mean", [P, P])
        small_rows = sb("small_rows", [N_MOD + 12, DEPTH, P])
        c_rows = sb("c_rows", [16, P])
        smallT = sb("smallT", [P, DEPTH, N_MOD + 12])
        cT = sb("cT", [P, KD, 2])
        cwT = sb("cwT", [P, DEPTH, CT, TAPS])
        modT = sb("modT", [P, DEPTH, N_MOD, 2])
        gate_bias = sb("gate_bias", [P, DEPTH])
        sink = sb("sink", [P, DEPTH, NQ])
        norm_g = sb("norm_g", [P, DEPTH, NH * MH])
        b_router = sb("b_router", [P, NE])
        negM_tok = sb("negM_tok", [64, T])
        gate_cols = sb("gate_cols", [P, 8, 64])
        eps = sb("eps", [P, 1])
        ones_row = sb("ones_row", [64, T])
        st = sb("st", [P, TT, 12])
        mv = sb("mv", [P, TT, 2])
        sd = sb("sd", [P, TT])
        rstd = sb("rstd", [P, TT])
        a_max = sb("a_max", [P, 3, 2])
        a_sum = sb("a_sum", [P, 3, 4])
        den = sb("den", [P, 3, 2])
        hstat = sb("hstat", [P, 4, TT * NH])
        r_sc = sb("r_sc", [P, TT, NE])
        r_sel = sb("r_sel", [P, TT, NE])
        r_rank = sb("r_rank", [P, TT, NE])
        r_cmp = sb("r_cmp", [P, TT, NE])
        r_hi = sb("r_hi", [P, TT, NG, 4])
        r_gs = sb("r_gs", [P, TT, NG])
        r_grank = sb("r_grank", [P, TT, NG])
        r_gcmp = sb("r_gcmp", [P, TT, NG])
        r_sum = sb("r_sum", [P, TT])
        gates = sb("gates", [P, TT, NE])

        cw_rows = arena[0:TAPS, 0:DEPTH, :]
        flat = arena[:, :, :].rearrange("p a b -> p (a b)")
        sq = flat[:, 0:CT * T].rearrange("p (a b) -> p a b", a=CT)
        grow = arena
        s_buf = arena
        w_buf = arena
        merged = arena
        acc = flat.rearrange("p (a b) -> p a b", a=TT)
        uflat = uT[:, :, :].rearrange("p a b -> p (a b)")
        ln_g, ln_b = uflat[:, 0:D], uflat[:, D:2 * D]
        g_rows = uflat[:, 2 * D:4 * D].rearrange("p (c d) -> p c d", c=2)
        tri_buf = upad[:, :, :, :].rearrange("p a b c -> p (a b c)")[:, 0:2 * TT * P]\
            .rearrange("p (u s t) -> p u s t", u=2, s=TT)
        hacc = convT[:, :, :].rearrange("p t (h d) -> p t h d", h=NH)
        hsq = arena[:, 0:TT, :].rearrange("p t (h d) -> p t h d", h=NH)
        yc = qkT
        sig = mqk
        psum = [ctx.enter_context(nc.psum_tensor(f"psum{b}", [P, 512], F32)) for b in range(BANKS)]

        def sem(name):
            return ctx.enter_context(nc.semaphore(name))

        ready = [sem(f"psum_ready{b}") for b in range(BANKS)]
        drained = [sem(f"psum_drained{b}") for b in range(BANKS)]
        loaded = [sem(f"slot_loaded{s}") for s in range(NS)]
        k_copy_loaded = sem("k_copy_loaded")
        setup_loaded = sem("setup_loaded")
        x_loaded = sem("x_loaded")
        ln_loaded = sem("ln_rows_loaded")
        wgate_loaded = sem("wgate_loaded")
        wgate_cleared = sem("wgate_cleared")
        consts_set = sem("consts_set")
        c_ready = sem("c_ready")
        mod_slot_used = sem("mod_slot_used")
        h_ready = sem("h_ready")
        ln_var, ln_std = sem("ln_var"), sem("ln_std")
        conv_ready, sq_ready, scaled_ready, ya_ready = (sem("conv_ready"), sem("conv_squares"), sem("conv_scaled"),
                                                        sem("ya_ready"))
        rope_ready = sem("rope_ready")
        gate_x, gate_l, gate_m, gate_em = sem("gate_negabs"), sem("gate_softplus"), sem("gate_m"), sem("gate_exp_m")
        s_ready, p_exp, p_ready = sem("scores_ready"), sem("probs_exp"), sem("probs_ready")
        tri_ready = sem("tri_ready")
        hc_ready, hsq_ready, hvar, hstd, hn_ready = (sem("head_centered"), sem("head_squares"), sem("head_var"),
                                                     sem("head_std"), sem("head_normed"))
        merged_ready = sem("merged_ready")
        dve_chain, act_chain, out_sent = sem("dve_chain"), sem("act_chain"), sem("out_sent")

        def bank(*key):
            return psum[place[key][0]]

        def wait_ready(eng, *key):
            eng.wait_ge(ready[place[key][0]], place[key][1] + 1)

        def wait_bank(pe, *key):
            if place[key][1] > 0:
                pe.wait_ge(drained[place[key][0]], place[key][1])

        def wait_drained(eng, *key):
            eng.wait_ge(drained[place[key][0]], place[key][1] + 1)

        def ready_of(*key):
            return ready[place[key][0]]

        def drained_of(*key):
            return drained[place[key][0]]

        def moe_round(l):
            return sum(k[0] == "moe" and k[1] == l for k in order) // BANKS

        win = [a["w_in"][l].rearrange("(k p) n -> p k n", p=P) for l in range(DEPTH)]
        wmod = [a["w_mod"][l].rearrange("(k p) n -> p k n", p=P) for l in range(DEPTH)]
        wout = [a["w_out"][l].rearrange("(k p) n -> p k n", p=P) for l in range(DEPTH)]
        wbr = [[a[n][l].rearrange("(k p) n -> p k n", p=P) for n in ("w_a_out", "w_b_out", "w_c_out")]
               for l in range(DEPTH)]

        def slot8(s):
            return ring[:, s, :].rearrange("p (k n) -> p k n", k=KD)

        def slot4(s):
            return ring[:, s, :].rearrange("p (k n) -> p k n", k=FT)

        stream = []
        for l in range(DEPTH):
            nt = token_tiles(l)

            def used(key, last):
                stream.append((key, ready_of(*last), place[last][1] + 1))
            for n in range(N_MOD // 2 - 1):
                stream.append((("mod", l, n), mod_slot_used, l * (N_MOD // 2 - 1) + n + 1))
            used(("mod", l, N_MOD // 2 - 1), ("mod", l))
            for j in range(CT):
                used(("a", l, j), ("gate", l, j))
            used(("v", l), ("v", l))
            used(("kk", l), ("qk", l, 5))
            for c in range(2):
                used(("q", l, c), ("qk", l, 2 * c + 1))
            for c in range(4):
                used(("mqk", l, c), ("mqk", l, 2 * c + 1))
            for c in range(2):
                used(("mv", l, c), ("mv", l, c, TT // 2 - 1))
            for c in range(2):
                used(("mo", l, c), ("mo", l, c, nt // 2 - 1))
            for j in range(KD // 2):
                last = 2 * j + 1
                used(("bga", l, j), ("bga", l, last))
                used(("bgb", l, j), ("bgb", l, last))
                used(("bgc", l, j), ("bgc", l, last))
                used(("yab", l, j), ("yb", l, last))
                used(("yc", l, j), ("yc_", l, last))
            for c in range(4):
                used(("out", l, c), ("out", l, c, nt // 2 - 1))
            for e in range(NE):
                b = e % 2
                for x in [("u", j) for j in range(FT)] + [("o", c, nt - 1) for c in range(2)]:
                    key = ("moe", l, b, x)
                    stream.append((("moe", l, e, x), ready_of(*key),
                                   place[key][1] + 1 + (e // 2) * moe_round(l)))
        index = {key: n for n, (key, _, _) in enumerate(stream)}

        def slot_of(*key):
            return index[key] % NS

        def wait_slot(eng, *key):
            eng.wait_ge(loaded[index[key] % NS], 32 * (index[key] // NS + 1))

        block = ctx.enter_context(nc.Block())

        @block.sync
        def _(sp):
            def load(key, offset=None):
                s = index[key] % NS
                w8, w4 = slot8(s), slot4(s)
                kind, l = key[0], key[1]
                if kind == "mod":
                    n = key[2] if offset is None else offset
                    src = wmod[l][:, :, bass.ds(n * 256, 256)]
                    pairs = [(w8[:, 0:4, :], src[:, 0:4, :]), (w8[:, 4:8, :], src[:, 4:8, :])]
                elif kind == "a":
                    j = key[2]
                    pairs = [(w8[:, :, g * P:(g + 1) * P],
                              win[l][:, :, C_A + g * D_CONV + j * P:C_A + g * D_CONV + (j + 1) * P]) for g in range(2)]
                elif kind == "v":
                    pairs = [(w8[:, 4 * g:4 * g + 4, 0:P], win[l][:, 4 * g:4 * g + 4, C_V:C_V + P]) for g in range(2)]
                elif kind == "kk":
                    copies = [(w8[:, :, (2 * g + r) * DH:(2 * g + r + 1) * DH],
                               win[l][:, :, C_K + g * DH:C_K + (g + 1) * DH]) for r in range(2) for g in range(NKV)]
                    pairs = copies[0:2]
                    for dst, src in copies[2:4]:
                        sp.dma_start(dst, src).then_inc(k_copy_loaded, 16)
                elif kind in ("q", "mqk", "mv", "mo"):
                    c0 = {"q": C_Q, "mqk": C_MQ, "mv": C_MV, "mo": C_MO}[kind] + 256 * key[2]
                    pairs = [(w8[:, 4 * g:4 * g + 4, :], win[l][:, 4 * g:4 * g + 4, c0:c0 + 256]) for g in range(2)]
                elif kind in ("bga", "bgb", "bgc"):
                    c0 = C_BG + "abc".index(kind[2]) * D + 256 * key[2]
                    pairs = [(w8[:, 4 * g:4 * g + 4, :], win[l][:, 4 * g:4 * g + 4, c0:c0 + 256]) for g in range(2)]
                elif kind == "yab":
                    c = slice(256 * key[2], 256 * key[2] + 256)
                    pairs = [(w8[:, 4 * g:4 * g + 4, :], wbr[l][g][:, :, c]) for g in range(2)]
                elif kind == "yc":
                    c = slice(256 * key[2], 256 * key[2] + 256)
                    pairs = [(w8[:, 2 * g:2 * g + 2, :], wbr[l][2][:, 2 * g:2 * g + 2, c]) for g in range(2)]
                elif kind == "out":
                    c = slice(256 * key[2], 256 * key[2] + 256)
                    pairs = [(w8[:, 4 * g:4 * g + 4, :], wout[l][:, 4 * g:4 * g + 4, c]) for g in range(2)]
                else:
                    e, x = (key[2] if offset is None else offset), key[3]
                    if x[0] == "u":
                        src = a["moe_w_gu"][l, e].rearrange("(k p) n -> p k n", p=P)
                        j = x[1]
                        pairs = [(w8[:, :, g * P:(g + 1) * P], src[:, :, g * DE + j * P:g * DE + (j + 1) * P])
                                 for g in range(2)]
                    else:
                        src = a["moe_w_dn"][l, e].rearrange("(k p) n -> p k n", p=P)
                        c = slice(512 * x[1], 512 * x[1] + 512)
                        pairs = [(w4[:, 2 * g:2 * g + 2, :], src[:, 2 * g:2 * g + 2, c]) for g in range(2)]
                for dst, src in pairs:
                    sp.dma_start(dst, src).then_inc(loaded[s], 16)

            def load_when_free(key):
                n = index[key]
                if n >= NS:
                    sp.wait_ge(stream[n - NS][1], stream[n - NS][2])
                load(key)

            keys = [key for key, _, _ in stream]
            at = 0
            while at < len(keys):
                key = keys[at]
                l = key[1]
                if key[0] == "mod":
                    for n in range(NS):
                        load_when_free(("mod", l, n))
                    with sp.Fori(1, N_MOD // 2 // NS) as i:
                        for n in range(NS):
                            sp.wait_ge(mod_slot_used, (i - 1) * NS + (l * (N_MOD // 2 - 1) + n + 1))
                            load(("mod", l, n), i * NS + n)
                    at += N_MOD // 2
                elif key[0] == "moe":
                    pair = keys[at:at + 12]
                    for k in pair:
                        load_when_free(k)
                    with sp.Fori(1, NE // 2) as i:
                        for n, k in enumerate(pair):
                            _, free, value = stream[index[k] + 12 - NS]
                            sp.wait_ge(free, (i - 1) * moe_round(l) + value)
                            load(k, i * 2 + k[2])
                    at += 6 * NE
                else:
                    load_when_free(key)
                    at += 1
            sp.wait_ge(h_ready, TT + sum(2 * token_tiles(l) for l in range(DEPTH)))
            sp.dma_start(out.rearrange("b (t p) d -> p (b t) d", p=P), H[:, 0:2, :]).then_inc(out_sent, 16)
            sp.wait_ge(out_sent, 16)

        setup = []

        def row_pairs():
            setup.append((ident[:, :], a["k_ident"]))
            for l in range(DEPTH):
                setup.append((small_rows[0:N_MOD, l, :], a["b_mod"][l].rearrange("(r c) -> r c", c=P)))
                for i, n in enumerate(("conv_b", "conv_ln_g", "conv_ln_b")):
                    setup.append((small_rows[N_MOD + 4 * i:N_MOD + 4 * i + 4, l, :],
                                  a[n][l].rearrange("(r c) -> r c", c=P)))
                setup.append((cw_rows[:, l, :], a["conv_w"][l]))
            setup.append((c_rows[0:8, :], a["c"][0].rearrange("(r c) -> r c", c=P)))
            setup.append((c_rows[8:16, :], a["c_ctx"].rearrange("(r c) -> r c", c=P)))
            setup.append((perm[:, :], a["k_perm"]))
            setup.append((rope[:, :, :], a["k_rope"]))
            setup.append((band[:, :, :], a["k_band"]))
            setup.append((tri[:, :, :], a["k_tri"]))
            setup.append((wrouter[:, :, :], a["w_router"].rearrange("(k p) n -> p k n", p=P)))
            setup.append((b_router[:, :], a["b_router"].partition_broadcast(P)))
            for l in range(DEPTH):
                setup.append((sink[:, l, :], a["attn_sink"][l].partition_broadcast(P)))
                setup.append((norm_g[:, l, :], a["mlstm_norm_g"][l].partition_broadcast(P)))
                for typ in range(2):
                    for d in range(2):
                        r = 64 * typ + 32 * d
                        setup.append((gate_bias[r:r + NH, l:l + 1],
                                      a["mlstm_gate_b"][l, d, typ].rearrange("(h o) -> h o", o=1)))
        row_pairs()
        SETUP = 16 * len(setup)

        @block.gpsimd
        def _(pool):
            for tile, (name, n) in enumerate((("x", S_LAT // P), ("ctx", S_CTX // P))):
                pool.dma_start(H[:, 2 * tile:2 * tile + 2, :],
                               a[name].rearrange("b (t p) d -> p (b t) d", p=P)).then_inc(x_loaded, 16)
            pool.dma_start(ln_g, a["ln_in_g"].partition_broadcast(P)).then_inc(ln_loaded, 16)
            pool.dma_start(ln_b, a["ln_in_b"].partition_broadcast(P)).then_inc(ln_loaded, 16)
            pool.wait_ge(consts_set, 1)
            for dst, src in setup:
                pool.dma_start(dst, src).then_inc(setup_loaded, 16)
            for l in range(DEPTH):
                if l:
                    wait_ready(pool, "ig", l - 1)
                else:
                    pool.wait_ge(wgate_cleared, 1)
                for typ in range(2):
                    for d in range(2):
                        c = C_MG + 8 * d + 4 * typ
                        r = 64 * typ + 32 * d
                        pool.dma_start(wgate[:, :, r:r + NH], win[l][:, :, c:c + NH]).then_inc(wgate_loaded, 16)
                for which, (g, b) in enumerate((("ln1_g", "ln1_b"), ("ln2_g", "ln2_b"))):
                    if which == 0:
                        wait_ready(pool, "bgc", l, KD - 1)
                    else:
                        bk, use = place[("moe", l, 1, ("u", FT - 1))]
                        pool.wait_ge(ready[bk], use + 1 + (NE // 2 - 1) * moe_round(l))
                    pool.dma_start(ln_g, a[g][l].partition_broadcast(P)).then_inc(ln_loaded, 16)
                    pool.dma_start(ln_b, a[b][l].partition_broadcast(P)).then_inc(ln_loaded, 16)
            pool.wait_ge(ln_loaded, 32 * (1 + 2 * DEPTH))
            pool.wait_ge(x_loaded, 32)
            pool.wait_ge(wgate_loaded, 64 * DEPTH)
            pool.wait_ge(setup_loaded, SETUP)

        h_base = [TT]
        for l in range(DEPTH):
            h_base += [h_base[-1] + token_tiles(l), h_base[-1] + 2 * token_tiles(l)]
        u_base = lambda l, which: 4 * (2 * l + which)
        n_att = [0, len(attention_units(0)), len(attention_units(0)) + len(attention_units(1))]

        @block.tensor
        def _(pe):
            def mm(dst, lhsT, rhs, start=True, stop=True):
                return nc.tensor.matmul(dst, lhsT, rhs, start=start, stop=stop)

            def done(ins, *key):
                ins.then_inc(ready_of(*key), 1)

            pe.wait_ge(setup_loaded, SETUP)
            prep = bank("prep")
            n_small = N_MOD + 12
            for l in range(DEPTH):
                nc.tensor.transpose(prep[:, l * n_small:(l + 1) * n_small], small_rows[:, l, :],
                                    ident[0:n_small, 0:n_small])
            nc.tensor.transpose(prep[:, 120:136], c_rows[:, :], ident[0:16, 0:16])
            for l in range(DEPTH):
                for j in range(CT):
                    o = 136 + (l * CT + j) * TAPS
                    last = nc.tensor.transpose(prep[:, o:o + TAPS], cw_rows[:, l, j * P:(j + 1) * P],
                                               ident[0:TAPS, 0:TAPS])
            done(last, "prep")

            for l in range(DEPTH):
                nt = token_tiles(l)
                n = nt * P

                pe.wait_ge(c_ready, 2)
                wait_bank(pe, "mod", l)
                b = bank("mod", l)
                def modulation(i, last_iteration):
                    for j in range(NS):
                        m = index[("mod", l, j)]
                        pe.wait_ge(loaded[m % NS], i * 32 + 32 * (m // NS + 1))
                        w = slot8(m % NS)
                        for half in range(2):
                            for k in range(KD):
                                last = mm(b[:, bass.ds(i * (4 * NS) + (4 * j + 2 * half), 2)],
                                          w[:, k, half * P:(half + 1) * P], cT[:, k, :], k == 0, k == KD - 1)
                        if last_iteration and j == NS - 1:
                            done(last, "mod", l)
                        else:
                            last.then_inc(mod_slot_used, 1)

                with pe.Fori(0, N_MOD // 2 // NS - 1) as i:
                    modulation(i, False)
                modulation(N_MOD // 2 // NS - 1, True)

                def transposes(which, tiles):
                    first = h_base[2 * l + which] - (TT if (l, which) == (0, 0) else token_tiles(l - 1 + which))
                    for k in range(KD):
                        wait_bank(pe, which and "tr2" or "tr1", l, k)
                        if k == 0:
                            pe.wait_ge(h_ready, h_base[2 * l + which])
                        b = bank(which and "tr2" or "tr1", l, k)
                        for t in range(tiles):
                            last = nc.tensor.transpose(b[:, t * P:(t + 1) * P], H[:, t, k * P:(k + 1) * P], ident[:, :])
                        done(last, which and "tr2" or "tr1", l, k)

                transposes(0, TT)
                for k in range(KD):
                    wait_drained(pe, "tr1", l, k)

                def by_channel(w, cols, width, *key):
                    wait_bank(pe, *key)
                    for k in range(KD):
                        last = mm(bank(*key)[:, 0:width], w[:, k, cols:cols + P], uT[:, k, 0:width], k == 0, k == KD - 1)
                    done(last, *key)

                for j in range(CT):
                    wait_slot(pe, "a", l, j)
                    w = slot8(slot_of("a", l, j))
                    by_channel(w, 0, n, "val", l, j)
                    by_channel(w, P, n, "gate", l, j)
                wait_slot(pe, "v", l)
                w = slot8(slot_of("v", l))
                wait_bank(pe, "v", l)
                for t in range(TT):
                    for k in range(KD):
                        last = mm(bank("v", l)[:, t * P:(t + 1) * P], uT[:, k, t * P:(t + 1) * P], w[:, k, 0:P],
                                  k == 0, k == KD - 1)
                done(last, "v", l)
                pe.wait_ge(wgate_loaded, 64 * (l + 1))
                by_channel(wgate, 0, T, "ig", l)
                wait_slot(pe, "kk", l)
                pe.wait_ge(k_copy_loaded, 32 * (l + 1))
                for g in range(NKV):
                    by_channel(slot8(slot_of("kk", l)), g * P, T, "qk", l, 4 + g)
                for c in range(2):
                    wait_slot(pe, "q", l, c)
                    for g in range(2):
                        by_channel(slot8(slot_of("q", l, c)), g * P, n, "qk", l, 2 * c + g)
                for t in range(6):
                    wait_drained(pe, "qk", l, t)
                    wait_bank(pe, "perm", l, t)
                    done(mm(bank("perm", l, t)[:, 0:S_LAT], perm[:, :], qkT[:, t, 0:S_LAT]), "perm", l, t)
                for c in range(4):
                    wait_slot(pe, "mqk", l, c)
                    for g in range(2):
                        by_channel(slot8(slot_of("mqk", l, c)), g * P, n if c < 2 else T, "mqk", l, 2 * c + g)
                for kind, tiles in (("mv", TT), ("mo", nt)):
                    for c in range(2):
                        wait_slot(pe, kind, l, c)
                        w = slot8(slot_of(kind, l, c))
                        for h in range(tiles // 2):
                            wait_bank(pe, kind, l, c, h)
                            for t in (2 * h, 2 * h + 1):
                                for k in range(KD):
                                    last = mm(bank(kind, l, c, h)[:, (t % 2) * 256:(t % 2 + 1) * 256],
                                              uT[:, k, t * P:(t + 1) * P], w[:, k, :], k == 0, k == KD - 1)
                            done(last, kind, l, c, h)

                pe.wait_ge(conv_ready, l + 1)
                wait_bank(pe, "mean", l)
                for j in range(CT):
                    last = mm(bank("mean", l)[:, 0:n], ones_mean[:, :], convT[:, j, 0:n], j == 0, j == CT - 1)
                done(last, "mean", l)
                pe.wait_ge(sq_ready, l + 1)
                wait_bank(pe, "var", l)
                for j in range(CT):
                    last = mm(bank("var", l)[:, 0:n], ones_mean[:, :], sq[:, j, 0:n], j == 0, j == CT - 1)
                done(last, "var", l)

                pe.wait_ge(gate_em, l + 1)
                wait_bank(pe, "cols", l)
                for i in range(8):
                    src = grow[0:64, 5 if i < 4 else 6, (i % 4) * P:(i % 4 + 1) * P]
                    last = nc.tensor.transpose(bank("cols", l)[:, i * 64:(i + 1) * 64], src, ident[0:64, 0:64])
                done(last, "cols", l)

                units = attention_units(l)
                pe.wait_ge(rope_ready, 6 * (l + 1))
                for i in range(len(units) + 3):
                    if i < len(units):
                        qt, h = units[i]
                        k0, k1 = key_range(qt)
                        r = slice(DH * (h % 2), DH * (h % 2) + DH)
                        wait_bank(pe, "S", l, i)
                        done(mm(bank("S", l, i)[:, k0:k1], qkT[r, h // 2, qt * P:(qt + 1) * P],
                                qkT[r, 4 + h // 4, k0:k1]), "S", l, i)
                    if 0 <= i - 2 < len(units):
                        m = i - 2
                        k0, k1 = key_range(units[m][0])
                        pe.wait_ge(p_ready, n_att[l] + m + 1)
                        wait_bank(pe, "PT", l, m)
                        for kt in range(k0 // P, k1 // P):
                            last = nc.tensor.transpose(bank("PT", l, m)[:, kt * P:(kt + 1) * P],
                                                       s_buf[:, m % 3, kt * P:(kt + 1) * P], ident[:, :])
                        done(last, "PT", l, m)
                    if 0 <= i - 3 < len(units):
                        m = i - 3
                        qt, h = units[m]
                        k0, k1 = key_range(qt)
                        if m == 0:
                            wait_drained(pe, "v", l)
                        wait_drained(pe, "PT", l, m)
                        wait_bank(pe, "PV", l, m)
                        g = h // 4
                        r = DH * (h % 2)
                        for kt in range(k0 // P, k1 // P):
                            last = mm(bank("PV", l, m)[r:r + DH, 0:P], v_tok[:, kt, g * DH:(g + 1) * DH],
                                      s_buf[:, 3 + m % 2, kt * P:(kt + 1) * P], kt == k0 // P, kt == k1 // P - 1)
                        done(last, "PV", l, m)

                for t in range(8):
                    wait_drained(pe, "mqk", l, t)
                for c in range(2):
                    for h in range(TT // 2):
                        wait_drained(pe, "mv", l, c, h)
                for i in range(len(UNITS) + 2):
                    if i < len(UNITS):
                        h, d = UNITS[i]
                        wait_bank(pe, "bm", l, i)
                        done(mm(bank("bm", l, i)[:, 0:n],
                                ident[0:64, 32 * d + h:32 * d + h + 1].broadcast_to([64, P]),
                                negM_tok[:, 0:n]), "bm", l, i)
                    if 0 <= i - 1 < len(UNITS):
                        h, d = UNITS[i - 1]
                        for s in range(TT):
                            wait_bank(pe, "st", l, i - 1, s)
                            done(mm(bank("st", l, i - 1, s)[:, 0:n], mqk[:, NH + h, s * P:(s + 1) * P],
                                    mqk[:, h, 0:n]), "st", l, i - 1, s)
                    if 0 <= i - 2 < len(UNITS):
                        m = i - 2
                        h, d = UNITS[m]
                        wait_drained(pe, "st", l, m, TT - 1)
                        for half in range(nt // 2):
                            wait_bank(pe, "hv", l, m, half)
                            for t in (2 * half, 2 * half + 1):
                                tiles = scan_tiles(t, d)
                                for s in tiles:
                                    o = (t % 2) * (MH + 1)
                                    last = mm(bank("hv", l, m, half)[:, o:o + MH + 1],
                                              w_buf[:, 4 * (m % 2) + s, t * P:(t + 1) * P],
                                              mv_tok[:, s, h, :], s == tiles[0], s == tiles[-1])
                            done(last, "hv", l, m, half)

                pe.wait_ge(hn_ready, l + 1)
                for h in range(NH):
                    wait_bank(pe, "yc", l, h)
                    for t in range(nt):
                        last = nc.tensor.transpose(bank("yc", l, h)[:, t * P:(t + 1) * P], hacc[:, t, h, :], ident[:, :])
                    done(last, "yc", l, h)

                pe.wait_ge(ya_ready, CT * (l + 1))
                wait_drained(pe, "PV", l, len(units) - 1)
                for j in range(KD):
                    cols = (j % 2) * P
                    for b in ("bga", "bgb", "bgc"):
                        if j % 2 == 0:
                            wait_slot(pe, b, l, j // 2)
                        by_channel(slot8(slot_of(b, l, j // 2)), cols, n, b, l, j)
                    if j % 2 == 0:
                        wait_slot(pe, "yab", l, j // 2)
                        wait_slot(pe, "yc", l, j // 2)
                    wab, wc = slot8(slot_of("yab", l, j // 2)), slot8(slot_of("yc", l, j // 2))
                    for key, w, k0, y, y0 in (("ya", wab, 0, yab, 0), ("yb", wab, 4, yab, 4), ("yc_", wc, 0, yc, 0)):
                        if key == "yc_" and j == 0:
                            for h in range(NH):
                                wait_drained(pe, "yc", l, h)
                        wait_bank(pe, key, l, j)
                        for k in range(4):
                            last = mm(bank(key, l, j)[:, 0:n], w[:, k0 + k, cols:cols + P], y[:, y0 + k, 0:n],
                                      k == 0, k == 3)
                        done(last, key, l, j)

                def gate_rows(which, first):
                    for c in range(4):
                        key = ("g1" if which == 0 else "g2", l, c)
                        wait_bank(pe, *key)
                        for j in range(4):
                            last = mm(bank(*key)[:, j * P:(j + 1) * P],
                                      modT[:, l, first + 4 * (c % 2) + j, c // 2:c // 2 + 1].broadcast_to([P, P]),
                                      ident[:, :])
                        done(last, *key)

                gate_rows(0, G1)
                pe.wait_ge(merged_ready, KD * (l + 1))
                for c in range(4):
                    wait_slot(pe, "out", l, c)
                    w = slot8(slot_of("out", l, c))
                    for h in range(nt // 2):
                        wait_bank(pe, "out", l, c, h)
                        for t in (2 * h, 2 * h + 1):
                            for k in range(KD):
                                last = mm(bank("out", l, c, h)[:, (t % 2) * 256:(t % 2 + 1) * 256],
                                          merged[:, k, t * P:(t + 1) * P], w[:, k, :], k == 0, k == KD - 1)
                        done(last, "out", l, c, h)

                transposes(1, nt)
                for k in range(KD):
                    wait_drained(pe, "tr2", l, k)
                wait_bank(pe, "router", l)
                for t in range(nt):
                    for k in range(KD):
                        last = mm(bank("router", l)[:, t * NE:(t + 1) * NE], uT[:, k, t * P:(t + 1) * P],
                                  wrouter[:, k, :], k == 0, k == KD - 1)
                done(last, "router", l)

                rounds = moe_round(l)
                with pe.Fori(0, NE // 2) as i:
                    for b in range(2):
                        for j in range(FT):
                            m = index[("moe", l, b, ("u", j))]
                            pe.wait_ge(loaded[m % NS], i * 64 + 32 * (m // NS + 1))
                            w = slot8(m % NS)
                            for g, part in enumerate("gu"):
                                bk, use = place[("moe", l, b, (part, j))]
                                pe.wait_ge(drained[bk], i * rounds + use)
                                for k in range(KD):
                                    last = mm(psum[bk][:, 0:n], w[:, k, g * P:(g + 1) * P], uT[:, k, 0:n],
                                              k == 0, k == KD - 1)
                                last.then_inc(ready[bk], 1)
                        for j in range(FT):
                            bk, use = place[("moe", l, b, ("u", j))]
                            pe.wait_ge(drained[bk], i * rounds + use + 1)
                        for c in range(2):
                            m = index[("moe", l, b, ("o", c, nt - 1))]
                            pe.wait_ge(loaded[m % NS], i * 64 + 32 * (m // NS + 1))
                            w = slot4(m % NS)
                            for t in range(nt):
                                bk, use = place[("moe", l, b, ("o", c, t))]
                                pe.wait_ge(drained[bk], i * rounds + use)
                                for k in range(FT):
                                    last = mm(psum[bk][:, :], yab[:, 4 * b + k, t * P:(t + 1) * P], w[:, k, :],
                                              k == 0, k == FT - 1)
                                last.then_inc(ready[bk], 1)
                gate_rows(1, G2)

        @block.scalar
        def _(act):
            chain = [0]

            def link(ins):
                chain[0] += 1
                ins.then_inc(act_chain, 1)
                act.wait_ge(act_chain, chain[0])

            f = nc.scalar.activation
            act.wait_ge(c_ready, 1)
            f(cT[:, :, :], cT[:, :, :], ACT.Silu).then_inc(c_ready, 1)

            def norm_std(first, tiles):
                act.wait_ge(ln_var, first)
                f(sd[:, 0:tiles], mv[:, 0:tiles, 1], ACT.Sqrt, bias=eps[:, :]).then_inc(ln_std, 1)

            act.wait_ge(consts_set, 1)
            norm_std(1, TT)
            for l in range(DEPTH):
                nt = token_tiles(l)
                n = nt * P
                wait_drained(act, "mod", l)

                def modulate(which, key, tiles):
                    sh, sc = (SH1, SC1) if which == 0 else (SH2, SC2)
                    for k in range(1, KD, 2):
                        wait_ready(act, key, l, k)
                        for c in range(max(1, tiles // 2)):
                            last = f(uT[:, k, c * 256:(c + 1) * 256], bank(key, l, k)[:, c * 256:(c + 1) * 256],
                                     ACT.Identity, bias=modT[:, l, sh + k, c:c + 1], scale=modT[:, l, sc + k, c:c + 1])
                            if c == max(1, tiles // 2) - 1:
                                last.then_inc(drained_of(key, l, k), 1)

                modulate(0, "tr1", TT)
                for j in range(CT):
                    if j >= 2:
                        wait_drained(act, "val", l, j - 2)
                    wait_ready(act, "gate", l, j)
                    f(arena[:, 4 + j % 2, 0:n], bank("gate", l, j)[:, 0:n], ACT.Sigmoid).then_inc(drained_of("gate", l, j), 1)
                wait_ready(act, "v", l)
                f(v_tok[:, :, :], bank("v", l)[:, :].rearrange("p (t d) -> p t d", t=TT), ACT.Copy)\
                    .then_inc(drained_of("v", l), 1)
                for t in (4, 5, 0, 1, 2, 3):
                    w = T if t >= 4 else n
                    wait_ready(act, "qk", l, t)
                    f(qkT[:, t, 0:w], bank("qk", l, t)[:, 0:w], ACT.Copy).then_inc(drained_of("qk", l, t), 1)
                for t in range(8):
                    w = n if t < 4 else T
                    wait_ready(act, "mqk", l, t)
                    f(mqk[:, t, 0:w], bank("mqk", l, t)[:, 0:w], ACT.Copy,
                      scale=1.0 if t < 4 else K_SCALE).then_inc(drained_of("mqk", l, t), 1)
                for c in range(2):
                    for h in range(TT // 2):
                        wait_ready(act, "mv", l, c, h)
                        key = ("mv", l, c, h)
                        f(mv_tok[:, 2 * h:2 * h + 2, 2 * c:2 * c + 2, 0:MH],
                          bank(*key)[:, :].rearrange("p (t g d) -> p t g d", t=2, g=2), ACT.Copy)\
                            .then_inc(drained_of(*key), 1)
                for c in range(2):
                    for h in range(nt // 2):
                        key = ("mo", l, c, h)
                        wait_ready(act, *key)
                        f(mo_tok[:, 2 * h:2 * h + 2, 2 * c:2 * c + 2, :],
                          bank(*key)[:, :].rearrange("p (t g d) -> p t g d", t=2, g=2), ACT.Sigmoid)\
                            .then_inc(drained_of(*key), 1)

                wait_drained(act, "mean", l)
                f(sq[:, :, 0:n], convT[:, :, 0:n], ACT.Square).then_inc(sq_ready, 1)
                wait_ready(act, "var", l)
                f(yab[:, 0, 0:n], bank("var", l)[:, 0:n], ACT.Sqrt, bias=eps[:, :]).then_inc(drained_of("var", l), 1)
                act.wait_ge(scaled_ready, l + 1)
                for j in range(CT):
                    f(yab[:, j, 0:n], convT[:, j, 0:n], ACT.Silu, bias=smallT[:, l, N_MOD + 8 + j:N_MOD + 9 + j],
                      scale=smallT[:, l, N_MOD + 4 + j:N_MOD + 5 + j]).then_inc(ya_ready, 1)

                act.wait_ge(gate_x, l + 1)
                link(f(grow[0:64, 2, :], grow[0:64, 1, :], ACT.Exp))
                f(grow[0:64, 3, :], grow[0:64, 2, :], ACT.Ln, bias=1.0).then_inc(gate_l, 1)
                act.wait_ge(gate_m, l + 1)
                f(grow[0:64, 6, :], grow[0:64, 4, :], ACT.Exp, scale=-1.0).then_inc(gate_em, 1)

                units = attention_units(l)
                for i in range(len(units) + 2):
                    if i < len(units):
                        qt, h = units[i]
                        k0, k1 = key_range(qt)
                        act.wait_ge(s_ready, n_att[l] + i + 1)
                        f(s_buf[:, i % 3, k0:k1], s_buf[:, i % 3, k0:k1], ACT.Exp, bias=a_max[:, i % 3, 1:2],
                          accum_out=a_sum[:, i % 3, 0:1])
                        f(a_sum[:, i % 3, 1:2], sink[:, l, h:h + 1], ACT.Exp, bias=a_max[:, i % 3, 1:2])\
                            .then_inc(p_exp, 1)
                    if 0 <= i - 2 < len(units):
                        m = i - 2
                        k0, k1 = key_range(units[m][0])
                        wait_ready(act, "PT", l, m)
                        if m >= 2:
                            wait_ready(act, "PV", l, m - 2)
                        f(s_buf[:, 3 + m % 2, k0:k1], bank("PT", l, m)[:, k0:k1], ACT.Copy)\
                            .then_inc(drained_of("PT", l, m), 1)

                for i in range(len(UNITS)):
                    h, d = UNITS[i]
                    r = 32 * d + h
                    act.wait_ge(tri_ready, len(UNITS) * l + i + 1)
                    if i >= 2:
                        wait_ready(act, "hv", l, i - 2, nt // 2 - 1)
                    for s in range(TT):
                        if s < nt:
                            last = f(w_buf[:, 4 * (i % 2) + s, s * P:(s + 1) * P], tri_buf[:, i % 2, s, :], ACT.Exp)
                        for t0, t1 in scan_ranges(s, d, n):
                            last = f(w_buf[:, 4 * (i % 2) + s, t0:t1], bank("bm", l, i)[:, t0:t1], ACT.Exp,
                                     bias=gate_cols[:, s, r:r + 1])
                    last.then_inc(drained_of("bm", l, i), 1)
                act.wait_ge(hc_ready, l + 1)
                f(hsq[:, 0:nt], hacc[:, 0:nt], ACT.Square).then_inc(hsq_ready, 1)
                act.wait_ge(hvar, l + 1)
                f(hstat[:, 2, 0:NH * nt], hstat[:, 1, 0:NH * nt], ACT.Sqrt, bias=eps[:, :], scale=1.0 / MH)\
                    .then_inc(hstd, 1)
                for h in range(NH):
                    wait_ready(act, "yc", l, h)
                    f(yc[:, h, 0:n], bank("yc", l, h)[:, 0:n], ACT.Copy).then_inc(drained_of("yc", l, h), 1)

                for j in range(KD):
                    if j >= 2:
                        wait_drained(act, "yc_", l, j - 2)
                    for b, key in enumerate(("bga", "bgb", "bgc")):
                        wait_ready(act, key, l, j)
                        f(sig[:, 3 * (j % 2) + b, 0:n], bank(key, l, j)[:, 0:n], ACT.Sigmoid)\
                            .then_inc(drained_of(key, l, j), 1)

                def gate_rows(which):
                    for c in range(4):
                        key = ("g1" if which == 0 else "g2", l, c)
                        wait_ready(act, *key)
                        f(g_rows[:, c // 2, (c % 2) * 512:(c % 2 + 1) * 512], bank(*key)[:, :], ACT.Copy)\
                            .then_inc(drained_of(*key), 1)

                gate_rows(0)
                norm_std(2 * l + 2, nt)
                modulate(1, "tr2", nt)
                wait_ready(act, "router", l)
                f(r_sc[:, 0:nt, :], bank("router", l)[:, 0:nt * NE].rearrange("p (t e) -> p t e", t=nt), ACT.Sigmoid)\
                    .then_inc(drained_of("router", l), 1)
                rounds = moe_round(l)
                with act.Fori(0, NE // 2) as i:
                    for b in range(2):
                        for j in range(FT):
                            bk, use = place[("moe", l, b, ("g", j))]
                            m = b * FT + j
                            if m >= 4:
                                bu, uu = place[("moe", l, 0, ("u", m - 4))]
                                act.wait_ge(drained[bu], i * rounds + uu + 1)
                            else:
                                bu, uu = place[("moe", l, 1, ("u", m))]
                                act.wait_ge(drained[bu], i * rounds + (uu + 1 - rounds))
                            act.wait_ge(ready[bk], i * rounds + use + 1)
                            f(mqk[:, m % 4, 0:n], psum[bk][:, 0:n], ACT.Silu).then_inc(drained[bk], 1)
                gate_rows(1)
                norm_std(2 * l + 3, nt)

        @block.vector
        def _(dve):
            v = nc.vector
            chain = [0]

            def link(ins):
                chain[0] += 1
                ins.then_inc(dve_chain, 1)
                dve.wait_ge(dve_chain, chain[0])

            v.memset(eps[:, :], EPS)
            v.memset(gate_bias[:, :], 0.0)
            v.memset(ones_mean[:, :], 1.0 / D_CONV).then_inc(consts_set, 1)
            v.memset(wgate[:, :, :], 0.0).then_inc(wgate_cleared, 1)
            v.memset(mv_tok[:, :, :, MH:MH + 1], 1.0)
            link(v.memset(ones_row[:, :], 1.0))
            wait_ready(dve, "prep")
            prep = bank("prep")
            v.tensor_copy(smallT[:, :, :], prep[:, 0:120].rearrange("p (l c) -> p l c", l=DEPTH))
            v.tensor_copy(cT[:, :, :], prep[:, 120:136].rearrange("p (c k) -> p k c", c=2)).then_inc(c_ready, 1)
            v.tensor_copy(cwT[:, :, :, :], prep[:, 136:136 + 8 * TAPS].rearrange("p (l j w) -> p l j w", l=DEPTH, j=CT))\
                .then_inc(drained_of("prep"), 1)
            dve.wait_ge(drained_of("prep"), 1)

            def layer_norm(which, tiles):
                for t in range(tiles):
                    v.bn_stats(st[:, t, 0:6], H[:, t, 0:512])
                    link(v.bn_stats(st[:, t, 6:12], H[:, t, 512:1024]))
                    last = v.bn_aggr(mv[:, t, :], st[:, t, :])
                last.then_inc(ln_var, 1)
                dve.wait_ge(ln_std, which + 1)
                link(v.reciprocal(rstd[:, 0:tiles], sd[:, 0:tiles]))
                dve.wait_ge(ln_loaded, 32 * (which + 1))
                for t in range(tiles):
                    link(v.tensor_scalar(H[:, t, :], H[:, t, :], mv[:, t, 0:1], rstd[:, t:t + 1], ALU.subtract, ALU.mult))
                    link(v.tensor_tensor(H[:, t, :], H[:, t, :], ln_g, ALU.mult))
                    v.tensor_tensor(H[:, t, :], H[:, t, :], ln_b, ALU.add).then_inc(h_ready, 1)

            dve.wait_ge(x_loaded, 32)
            layer_norm(0, TT)

            for l in range(DEPTH):
                nt = token_tiles(l)
                n = nt * P
                streams = nt // 2

                wait_ready(dve, "mod", l)
                link(v.tensor_tensor(modT[:, l, :, :], bank("mod", l)[:, 0:2 * N_MOD].rearrange("p (m c) -> p m c", c=2),
                                     smallT[:, l, 0:N_MOD].unsqueeze(2).broadcast_to([P, N_MOD, 2]), ALU.add))
                v.tensor_scalar(modT[:, l, SC1:SC1 + 8, :], modT[:, l, SC1:SC1 + 8, :], 1.0, None, ALU.add)
                v.tensor_scalar(modT[:, l, SC2:SC2 + 8, :], modT[:, l, SC2:SC2 + 8, :], 1.0, None, ALU.add)\
                    .then_inc(drained_of("mod", l), 1)
                wait_drained(dve, "mod", l)

                def modulate(which, key, tiles):
                    sh, sc = (SH1, SC1) if which == 0 else (SH2, SC2)
                    for k in range(0, KD, 2):
                        wait_ready(dve, key, l, k)
                        for c in range(max(1, tiles // 2)):
                            last = v.tensor_scalar(uT[:, k, c * 256:(c + 1) * 256], bank(key, l, k)[:, c * 256:(c + 1) * 256],
                                                   modT[:, l, sc + k, c:c + 1], modT[:, l, sh + k, c:c + 1],
                                                   ALU.mult, ALU.add)
                        last.then_inc(drained_of(key, l, k), 1)

                modulate(0, "tr1", TT)

                link(v.memset(upad[:, :, :, :], 0.0))
                for j in range(CT):
                    wait_ready(dve, "val", l, j)
                    wait_drained(dve, "gate", l, j)
                    v.tensor_tensor(upad[:, j, 0:streams, PAD:PAD + S_LAT],
                                    bank("val", l, j)[:, 0:n].rearrange("p (s t) -> p s t", s=streams),
                                    arena[:, 4 + j % 2, 0:n].rearrange("p (s t) -> p s t", s=streams), ALU.mult)\
                        .then_inc(drained_of("val", l, j), 1)
                    wait_drained(dve, "val", l, j)
                wait_ready(dve, "ig", l)
                v.tensor_scalar(grow[:, 7, :], bank("ig", l)[:, :], gate_bias[:, l:l + 1], None, ALU.add)\
                    .then_inc(drained_of("ig", l), 1)
                wait_drained(dve, "ig", l)
                cv = convT[:, :, :].rearrange("p j (s t) -> p j s t", s=2)
                for w in range(TAPS):
                    for j in range(CT):
                        src = upad[:, j, 0:streams, w:w + S_LAT]
                        if w == 0:
                            last = v.tensor_scalar(cv[:, j, 0:streams], src, cwT[:, l, j, 0:1],
                                                   smallT[:, l, N_MOD + j:N_MOD + j + 1], ALU.mult, ALU.add)
                        else:
                            last = v.scalar_tensor_tensor(cv[:, j, 0:streams], src, cwT[:, l, j, w:w + 1],
                                                          cv[:, j, 0:streams], ALU.mult, ALU.add)
                    if w < TAPS - 1:
                        link(last)
                last.then_inc(conv_ready, 1)

                for t in range(6):
                    wait_ready(dve, "perm", l, t)
                    v.tensor_tensor(arena[:, 6, 0:S_LAT], bank("perm", l, t)[:, 0:S_LAT], rope[:, 1, :], ALU.mult)\
                        .then_inc(drained_of("perm", l, t), 1)
                    link(v.tensor_tensor(qkT[:, t, 0:S_LAT], qkT[:, t, 0:S_LAT], rope[:, 0, :], ALU.mult))
                    v.tensor_tensor(qkT[:, t, 0:S_LAT], qkT[:, t, 0:S_LAT], arena[:, 6, 0:S_LAT], ALU.add)\
                        .then_inc(rope_ready, 1)
                    dve.wait_ge(rope_ready, 6 * l + t + 1)

                wait_ready(dve, "mean", l)
                v.tensor_tensor(convT[:, :, 0:n], convT[:, :, 0:n],
                                bank("mean", l)[:, 0:n].unsqueeze(1).broadcast_to([P, CT, n]), ALU.subtract)\
                    .then_inc(drained_of("mean", l), 1)
                wait_drained(dve, "var", l)
                link(v.reciprocal(yab[:, 0, 0:n], yab[:, 0, 0:n]))
                v.tensor_tensor(convT[:, :, 0:n], convT[:, :, 0:n],
                                yab[:, 0:1, 0:n].broadcast_to([P, CT, n]), ALU.mult).then_inc(scaled_ready, 1)

                link(v.tensor_copy(grow[0:64, 0, :], grow[64:128, 7, :]))
                link(v.tensor_scalar(grow[0:64, 1, :], grow[0:64, 0, :], -1.0, None, ALU.mult))
                v.tensor_tensor(grow[0:64, 1, :], grow[0:64, 0, :], grow[0:64, 1, :], ALU.min).then_inc(gate_x, 1)
                dve.wait_ge(gate_l, l + 1)
                link(v.scalar_tensor_tensor(grow[0:64, 0, :], grow[0:64, 0, :], 0.0, grow[0:64, 3, :],
                                            ALU.min, ALU.subtract))

                def reorder(dst, src, back):
                    lat, ctx_ = (slice(0, S_LAT), slice(S_LAT, T))
                    rev_lat, rev_ctx = slice(S_LAT - 1, None, -1), slice(T - 1, S_LAT - 1, -1)
                    if back:
                        v.tensor_copy(dst[0:32, lat], src[0:32, ctx_])
                        v.tensor_copy(dst[0:32, ctx_], src[0:32, lat])
                        v.tensor_copy(dst[32:64, lat], src[32:64, rev_ctx])
                        return v.tensor_copy(dst[32:64, ctx_], src[32:64, rev_lat])
                    v.tensor_copy(dst[0:32, lat], src[0:32, ctx_])
                    v.tensor_copy(dst[0:32, ctx_], src[0:32, lat])
                    v.tensor_copy(dst[32:64, lat], src[32:64, rev_ctx])
                    return v.tensor_copy(dst[32:64, ctx_], src[32:64, rev_lat])

                reorder(grow[0:64, 1, :], grow[0:64, 0, :], False)
                link(reorder(grow[0:64, 2, :], grow[0:64, 7, :], False))
                link(v.tensor_tensor_scan(grow[0:64, 3, :], ones_row[:, :], grow[0:64, 1, :], 0.0, ALU.mult, ALU.add))
                link(v.tensor_tensor(grow[0:64, 2, :], grow[0:64, 2, :], grow[0:64, 3, :], ALU.subtract))
                link(v.tensor_tensor_scan(grow[0:64, 0, :], grow[0:64, 2, :], grow[0:64, 2, :], 0.0, ALU.max, ALU.max))
                link(v.tensor_tensor(grow[0:64, 3, :], grow[0:64, 3, :], grow[0:64, 0, :], ALU.add))
                link(v.tensor_scalar(grow[0:64, 0, :], grow[0:64, 0, :], -1.0, None, ALU.mult))
                reorder(negM_tok[:, :], grow[0:64, 0, :], True)
                reorder(grow[0:64, 5, :], grow[0:64, 2, :], True)
                reorder(grow[0:64, 4, :], grow[0:64, 3, :], True).then_inc(gate_m, 1)
                wait_ready(dve, "cols", l)
                v.tensor_copy(gate_cols[:, :, :], bank("cols", l)[:, :].rearrange("p (i r) -> p i r", i=8))\
                    .then_inc(drained_of("cols", l), 1)
                wait_drained(dve, "cols", l)

                units = attention_units(l)
                for i in range(len(units) + 3):
                    if i < len(units):
                        qt, h = units[i]
                        k0, k1 = key_range(qt)
                        b = i % 3
                        wait_ready(dve, "S", l, i)
                        if i >= 3:
                            wait_ready(dve, "PT", l, i - 3)
                        if k0 == 0:
                            ins = v.scalar_tensor_tensor(s_buf[:, b, :], bank("S", l, i)[:, :], A_SCALE, band[:, qt, :],
                                                         ALU.mult, ALU.add)
                        else:
                            ins = v.tensor_scalar(s_buf[:, b, k0:k1], bank("S", l, i)[:, k0:k1], A_SCALE, None, ALU.mult)
                        ins.then_inc(drained_of("S", l, i), 1)
                        wait_drained(dve, "S", l, i)
                        link(v.tensor_reduce(a_max[:, b, 0:1], s_buf[:, b, k0:k1], AX_X, ALU.max))
                        v.tensor_scalar(a_max[:, b, 1:2], a_max[:, b, 0:1], sink[:, l, h:h + 1], -1.0,
                                        ALU.max, ALU.mult).then_inc(s_ready, 1)
                    if 0 <= i - 1 < len(units):
                        m = i - 1
                        b = m % 3
                        k0, k1 = key_range(units[m][0])
                        dve.wait_ge(p_exp, n_att[l] + m + 1)
                        link(v.tensor_tensor(a_sum[:, b, 2:3], a_sum[:, b, 0:1], a_sum[:, b, 1:2], ALU.add))
                        link(v.reciprocal(a_sum[:, b, 3:4], a_sum[:, b, 2:3]))
                        v.tensor_scalar(s_buf[:, b, k0:k1], s_buf[:, b, k0:k1], a_sum[:, b, 3:4], None, ALU.mult)\
                            .then_inc(p_ready, 1)
                    if 0 <= i - 3 < len(units):
                        m = i - 3
                        qt, h = units[m]
                        r = slice(DH * (h % 2), DH * (h % 2) + DH)
                        wait_ready(dve, "PV", l, m)
                        v.tensor_copy(yab[r, 4 + h // 2, qt * P:(qt + 1) * P], bank("PV", l, m)[r, 0:P])\
                            .then_inc(drained_of("PV", l, m), 1)

                def triangles(i):
                    h, d = UNITS[i]
                    r = 32 * d + h
                    wait_ready(dve, "bm", l, i)
                    if i >= 2:
                        wait_drained(dve, "bm", l, i - 2)
                    for s in range(nt):
                        last = v.scalar_tensor_tensor(tri_buf[:, i % 2, s, :], bank("bm", l, i)[:, s * P:(s + 1) * P],
                                                      gate_cols[:, s, r:r + 1], tri[:, d, :], ALU.add, ALU.add)
                    last.then_inc(tri_ready, 1)

                def weights(i):
                    h, d = UNITS[i]
                    wait_drained(dve, "bm", l, i)
                    for s in range(TT):
                        wait_ready(dve, "st", l, i, s)
                        own = [(s * P, (s + 1) * P)] if s < nt else []
                        for t0, t1 in joined(scan_ranges(s, d, n) + own):
                            w = w_buf[:, 4 * (i % 2) + s, t0:t1]
                            last = v.tensor_tensor(w, bank("st", l, i, s)[:, t0:t1], w, ALU.mult)
                        last.then_inc(drained_of("st", l, i, s), 1)

                def outputs(i):
                    h, d = UNITS[i]
                    r = 32 * d + h
                    for half in range(nt // 2):
                        b = bank("hv", l, i, half)
                        wait_ready(dve, "hv", l, i, half)
                        raw = b[:, MH:2 * MH + 2:MH + 1]
                        link(v.scalar_tensor_tensor(den[:, 0, :], raw, -1.0, gate_cols[:, 4 + 2 * half:6 + 2 * half, r],
                                                    ALU.mult, ALU.max))
                        link(v.tensor_tensor(den[:, 1, :], raw, den[:, 0, :], ALU.max))
                        link(v.reciprocal(den[:, 2, :], den[:, 1, :]))
                        for t in range(2):
                            dst = hacc[:, 2 * half + t, h, :]
                            src = b[:, t * (MH + 1):t * (MH + 1) + MH]
                            if d == 0:
                                last = v.tensor_scalar(dst, src, den[:, 2, t:t + 1], None, ALU.mult)
                            else:
                                last = v.scalar_tensor_tensor(dst, src, den[:, 2, t:t + 1], dst, ALU.mult, ALU.add)
                        last.then_inc(drained_of("hv", l, i, half), 1)
                        wait_drained(dve, "hv", l, i, half)

                for i in range(len(UNITS) + 2):
                    if i == 0:
                        dve.wait_ge(ya_ready, CT * (l + 1))
                    if i < len(UNITS):
                        triangles(i)
                    if 0 <= i - 1 < len(UNITS):
                        weights(i - 1)
                    if 0 <= i - 2 < len(UNITS):
                        outputs(i - 2)

                hs = hstat[:, :, 0:NH * nt].rearrange("p a (t h) -> p a t h", t=nt)
                hv = hacc[:, 0:nt]
                link(v.tensor_reduce(hs[:, 0], hv, AX_X, ALU.add))
                link(v.tensor_scalar(hs[:, 0], hs[:, 0], 1.0 / MH, None, ALU.mult))
                v.tensor_tensor(hv, hv, hs[:, 0].unsqueeze(3).broadcast_to([P, nt, NH, MH]), ALU.subtract)\
                    .then_inc(hc_ready, 1)
                dve.wait_ge(hsq_ready, l + 1)
                v.tensor_reduce(hs[:, 1], hsq[:, 0:nt], AX_X, ALU.add).then_inc(hvar, 1)
                dve.wait_ge(hstd, l + 1)
                link(v.reciprocal(hs[:, 3], hs[:, 2]))
                link(v.tensor_tensor(hv, hv, hs[:, 3].unsqueeze(3).broadcast_to([P, nt, NH, MH]), ALU.mult))
                gain = norm_g[:, l, :].rearrange("p (h d) -> p h d", h=NH)
                link(v.tensor_tensor(hv, hv, gain.unsqueeze(1).broadcast_to([P, nt, NH, MH]), ALU.mult))
                wait_drained(dve, "mo", l, 0, nt // 2 - 1)
                wait_drained(dve, "mo", l, 1, nt // 2 - 1)
                v.tensor_tensor(hv, hv, mo_tok[:, 0:nt], ALU.mult).then_inc(hn_ready, 1)

                for j in range(KD):
                    for b, (key, gkey) in enumerate((("ya", "bga"), ("yb", "bgb"), ("yc_", "bgc"))):
                        wait_ready(dve, key, l, j)
                        wait_drained(dve, gkey, l, j)
                        dst = merged[:, j, 0:n] if b == 0 else sig[:, 6, 0:n]
                        v.tensor_tensor(dst, bank(key, l, j)[:, 0:n], sig[:, 3 * (j % 2) + b, 0:n], ALU.mult)\
                            .then_inc(drained_of(key, l, j), 1)
                        wait_drained(dve, key, l, j)
                        if b == 1:
                            link(v.tensor_tensor(merged[:, j, 0:n], merged[:, j, 0:n], sig[:, 6, 0:n], ALU.add))
                        if b == 2:
                            v.tensor_tensor(merged[:, j, 0:n], merged[:, j, 0:n], sig[:, 6, 0:n], ALU.add)\
                                .then_inc(merged_ready, 1)
                            dve.wait_ge(merged_ready, l * KD + j + 1)

                for c in range(4):
                    for h in range(nt // 2):
                        if (c, h) == (0, 0):
                            for x in range(4):
                                wait_drained(dve, "g1", l, x)
                        key = ("out", l, c, h)
                        wait_ready(dve, *key)
                        tmp = sig[:, 6, :].rearrange("p (t d) -> p t d", t=2)
                        hh = H[:, 2 * h:2 * h + 2, c * 256:(c + 1) * 256]
                        g = g_rows[:, h:h + 1, c * 256:(c + 1) * 256].broadcast_to([P, 2, 256])
                        v.tensor_tensor(tmp, bank(*key)[:, :].rearrange("p (t d) -> p t d", t=2), g, ALU.mult)\
                            .then_inc(drained_of(*key), 1)
                        wait_drained(dve, *key)
                        link(v.scalar_tensor_tensor(hh, hh, ALPHA, tmp, ALU.mult, ALU.add))
                layer_norm(2 * l + 1, nt)
                modulate(1, "tr2", nt)

                wait_drained(dve, "router", l)
                rs = r_sel[:, 0:nt, :].rearrange("p t (g e) -> p t g e", g=NG)
                rk = r_rank[:, 0:nt, :].rearrange("p t (g e) -> p t g e", g=NG)
                rc = r_cmp[:, 0:nt, :].rearrange("p t (g e) -> p t g e", g=NG)
                link(v.tensor_tensor(r_sel[:, 0:nt, :], r_sc[:, 0:nt, :],
                                     b_router[:, :].unsqueeze(1).broadcast_to([P, nt, NE]), ALU.add))
                hi = r_hi[:, 0:nt]
                v.tensor_tensor(hi[:, :, :, 0:2], rs[:, :, :, 0:3:2], rs[:, :, :, 1:4:2], ALU.max)
                link(v.tensor_tensor(hi[:, :, :, 2:4], rs[:, :, :, 0:3:2], rs[:, :, :, 1:4:2], ALU.min))
                gs, gc, gr = r_gs[:, 0:nt], r_gcmp[:, 0:nt], r_grank[:, 0:nt]
                v.tensor_tensor(gs, hi[:, :, :, 0], hi[:, :, :, 1], ALU.max)
                v.tensor_tensor(gc, hi[:, :, :, 0], hi[:, :, :, 1], ALU.min)
                link(v.tensor_tensor(gr, hi[:, :, :, 2], hi[:, :, :, 3], ALU.max))
                link(v.tensor_tensor(gc, gc, gr, ALU.max))
                link(v.tensor_tensor(gs, gs, gc, ALU.add))
                for e in range(4):
                    v.memset(r_grank[:, :, e:e + 1], float(3 - e))
                    last = v.memset(r_rank[:, :, :].rearrange("p t (g e) -> p t g e", g=NG)[:, :, :, e:e + 1], float(3 - e))
                link(last)
                for sft in range(1, 4):
                    k = 4 - sft
                    link(v.tensor_tensor(gc[:, :, 0:k], gs[:, :, 0:k], gs[:, :, sft:4], ALU.is_ge))
                    link(v.tensor_tensor(gr[:, :, sft:4], gr[:, :, sft:4], gc[:, :, 0:k], ALU.add))
                    link(v.tensor_tensor(gr[:, :, 0:k], gr[:, :, 0:k], gc[:, :, 0:k], ALU.subtract))
                    link(v.tensor_tensor(rc[:, :, :, 0:k], rs[:, :, :, 0:k], rs[:, :, :, sft:4], ALU.is_ge))
                    link(v.tensor_tensor(rk[:, :, :, sft:4], rk[:, :, :, sft:4], rc[:, :, :, 0:k], ALU.add))
                    link(v.tensor_tensor(rk[:, :, :, 0:k], rk[:, :, :, 0:k], rc[:, :, :, 0:k], ALU.subtract))
                v.tensor_scalar(gr, gr, 0.5, None, ALU.is_lt)
                link(v.tensor_scalar(rk, rk, 1.5, None, ALU.is_lt))
                link(v.tensor_tensor(rk, rk, gr.unsqueeze(3).broadcast_to([P, nt, NG, EPG]), ALU.mult))
                link(v.tensor_tensor(r_sel[:, 0:nt, :], r_rank[:, 0:nt, :], r_sc[:, 0:nt, :], ALU.mult))
                link(v.tensor_reduce(r_sum[:, 0:nt], r_sel[:, 0:nt, :], AX_X, ALU.add))
                link(v.reciprocal(r_sum[:, 0:nt], r_sum[:, 0:nt]))
                link(v.tensor_tensor(gates[:, 0:nt, :], r_sel[:, 0:nt, :],
                                     r_sum[:, 0:nt].unsqueeze(2).broadcast_to([P, nt, NE]), ALU.mult))
                link(v.memset(acc[:, 0:nt, :], 0.0))

                rounds = moe_round(l)
                n_down = 2 * nt
                with dve.Fori(0, NE // 2) as i:
                    for b in range(2):
                        for j in range(FT):
                            bg_, ug = place[("moe", l, b, ("g", j))]
                            bk, use = place[("moe", l, b, ("u", j))]
                            m = b * FT + j
                            dve.wait_ge(drained[bg_], i * rounds + ug + 1)
                            dve.wait_ge(ready[bk], i * rounds + use + 1)
                            v.tensor_tensor(yab[:, 4 * b + j, 0:n], psum[bk][:, 0:n], mqk[:, m % 4, 0:n], ALU.mult)\
                                .then_inc(drained[bk], 1)
                        for c in range(2):
                            for t in range(nt):
                                bk, use = place[("moe", l, b, ("o", c, t))]
                                dve.wait_ge(ready[bk], i * rounds + use + 1)
                                dst = acc[:, t, c * 512:(c + 1) * 512]
                                v.scalar_tensor_tensor(dst, psum[bk][:, :], gates[:, t, bass.ds(i * 2 + b, 1)], dst,
                                                       ALU.mult, ALU.add).then_inc(drained[bk], 1)
                        dve.wait_ge(drained[bk], i * rounds + use + 1)
                for x in range(4):
                    wait_drained(dve, "g2", l, x)
                for t in range(nt):
                    link(v.tensor_tensor(acc[:, t, :], acc[:, t, :], g_rows[:, t // 2, :], ALU.mult))
                    link(v.scalar_tensor_tensor(H[:, t, :], H[:, t, :], ALPHA, acc[:, t, :], ALU.mult, ALU.add))
                layer_norm(2 * l + 2, nt)


INPUTS = ["x", "c", "ctx", "c_ctx", "ln_in_g", "ln_in_b", "w_router", "b_router", "w_mod", "b_mod", "w_in", "conv_w",
          "conv_b", "conv_ln_g", "conv_ln_b", "w_a_out", "attn_sink", "w_b_out", "mlstm_gate_b", "mlstm_norm_g",
          "w_c_out", "w_out", "ln1_g", "ln1_b", "moe_w_gu", "moe_w_dn", "ln2_g", "ln2_b"]


def kernel(**inputs):
    import concourse.bacc as bacc
    from concourse.bass_utils import run_bass_kernel_spmd

    nc = bacc.Bacc("TRN2", target_bir_lowering=False, num_devices=1)
    arrays, aps = {}, {}
    host = {name: np.ascontiguousarray(inputs[name]) for name in INPUTS}
    host.update(host_constants())
    for name, value in host.items():
        arrays[f"in_{name}"] = value
        aps[name] = nc.dram_tensor(f"in_{name}", value.shape, mybir.dt.from_np(value.dtype), kind="ExternalInput").ap()
    out = nc.dram_tensor("out", (1, S_LAT, D), F32, kind="ExternalOutput").ap()
    build(nc, aps, out)
    result = run_bass_kernel_spmd(nc, [arrays], core_ids=[0])
    return result.results[0]["out"]
```

```python
from contextlib import ExitStack

import numpy as np

import concourse.bass as bass
from concourse import mybir

F32 = mybir.dt.float32
ALU = mybir.AluOpType
ACT = mybir.ActivationFunctionType
AX_X = mybir.AxisListType.X

P = 128
D = 1024
KD = D // P
DEPTH = 2
S_LAT, S_CTX = 256, 256
T = S_LAT + S_CTX
TT = T // P
D_CONV, TAPS = 512, 31
PAD = TAPS // 2
CT = D_CONV // P
NQ, NKV, DH = 8, 2, 64
NH, MH = 4, 128
WINDOW, GRID_W, ROPE_BASE = 128, 64, 10000.0
NE, NG, EPG, DE, TOP_K = 16, 4, 4, 512, 2
FT = DE // P
EPS = 1e-5
ALPHA = (2.0 * DEPTH) ** 0.25
A_SCALE = DH ** -0.5
K_SCALE = MH ** -0.5
NEG = -1e30
NS = 6
SLOT = KD * 256
BANKS = 8
CAP = P

C_A, C_Q, C_K, C_V = 0, 1024, 1536, 1664
C_MQ, C_MK, C_MV, C_MO, C_MG, C_BG = 1792, 2304, 2816, 3328, 3840, 3856
SH1, SC1, G1, SH2, SC2, G2 = 0, 8, 16, 24, 32, 40
N_MOD = 6 * KD

UNITS = [(h, d) for h in range(NH) for d in range(2)]


def token_tiles(layer):
    return TT if layer < DEPTH - 1 else S_LAT // P


def attention_units(layer):
    return [(qt, h) for qt in range(token_tiles(layer)) for h in range(NQ)]


def key_range(qt):
    return (0, T) if qt < S_LAT // P else (S_LAT, T)


MOD_FIRST = 8


def later_modulation(layer):
    if layer:
        return []
    return [(0, n) for n in range(MOD_FIRST, N_MOD // 2)] + [(1, n) for n in range(N_MOD // 2)]


def first_modulation():
    return [(0, n) for n in range(MOD_FIRST)]


def modulation_step(slots, s):
    before = slots[s - 1:s] if s else []
    return [("modt",) + x for x in before] + [("mod",) + x for x in slots[s:s + 1]]


def scan_ranges(s, d, n):
    lat, ctx = (0, 2 * P), None
    if s == 0:
        full = [(P, 2 * P)] if d == 0 else []
    elif s == 1:
        full = [] if d == 0 else [(0, P)]
    elif s == 2:
        full = [lat, (3 * P, 4 * P)] if d == 0 else [lat]
    else:
        full = [lat] if d == 0 else [lat, (2 * P, 3 * P)]
    return [r for r in full if r[1] <= n]


def scan_tiles(t, d):
    return [s for s in range(TT) if s == t or any(a <= t * P < b for a, b in scan_ranges(s, d, T))]


def joined(ranges):
    out = []
    for a, b in sorted(ranges):
        if out and out[-1][1] == a:
            out[-1] = (out[-1][0], b)
        else:
            out.append((a, b))
    return out


def blocks(layer):
    tokens = token_tiles(layer) * P
    return (TOP_K * tokens - NE) // CAP + NE


def psum_order():
    order = [("prep",)]
    for s in range(MOD_FIRST + 1):
        order += modulation_step(first_modulation(), s)
    for l in range(DEPTH):
        nt = token_tiles(l)
        later = later_modulation(l)
        order += [("tr1", l, k) for k in range(KD)]
        for j in range(CT):
            order += [("val", l, j), ("gate", l, j)]
        order += [("v", l), ("ig", l)]
        order += [("qk", l, t) for t in (4, 5, 0, 1, 2, 3)]
        order += [("perm", l, t) for t in range(6)]
        order += [("mqk", l, t) for t in range(8)]
        order += [("mv", l, c, h) for c in range(2) for h in range(TT // 2)]
        order += [("mean", l)]
        order += [("mo", l, c, h) for c in range(2) for h in range(nt // 2)]
        order += [("var", l)]
        n = len(attention_units(l))
        for i in range(n + 3):
            order += [("S", l, i)] if i < n else []
            order += [("PT", l, i - 2)] if 0 <= i - 2 < n else []
            order += [("PV", l, i - 3)] if 0 <= i - 3 < n else []
            order += modulation_step(later, i) if i < n else []
        order += [("yb_rows", l, t) for t in range(nt)]
        order += [("cols", l)]
        n_first, n = n, len(UNITS)
        for i in range(n + 2):
            order += [("bm", l, i)] if i < n else []
            order += [("st", l, i - 1, s) for s in range(TT)] if 0 <= i - 1 < n else []
            order += [("hv", l, i - 2, t) for t in range(nt // 2)] if 0 <= i - 2 < n else []
            order += modulation_step(later, n_first + i)
        order += [("bga", l, 0), ("bgb", l, 0), ("bgc", l, 0)]
        order += [("yc", l, h) for h in range(NH)]
        for j in range(KD):
            order += [(b, l, j) for b in ("bga", "bgb", "bgc")] if j else []
            order += [(b, l, j) for b in ("ya", "yb", "yc_")]
        order += [("g1", l, c) for c in range(4)]
        order += [("out", l, c, h) for h in range(nt // 2) for c in range(4)]
        order += [("tr2", l, k) for k in range(KD)]
        order += [("router", l)]
        order += [("nat", l, t, h) for t in range(nt) for h in range(2)]
        order += [("g2", l, c) for c in range(4)]
        order += [("count", l)]
    return order, {key: (n % BANKS, n // BANKS) for n, key in enumerate(order)}


def host_constants():
    nf = DH // 4
    inv = ROPE_BASE ** (-np.arange(nf, dtype=np.float32) / np.float32(nf))
    pos = np.arange(S_LAT)
    row, col = pos // GRID_W, pos % GRID_W
    d = np.arange(P) % DH
    ang = np.where((d < DH // 2)[:, None], row[None, :], col[None, :]).astype(np.float32) * inv[d % nf][:, None]
    second = (d % (2 * nf)) >= nf
    cos, sin = np.cos(ang), np.where(second[:, None], np.sin(ang), -np.sin(ang))
    partner = np.arange(P) + np.where(second, -nf, nf)
    perm = np.zeros((P, P), np.float32)
    perm[partner, np.arange(P)] = 1.0
    q = np.arange(S_LAT).reshape(2, P, 1)
    k = np.arange(T).reshape(1, 1, T)
    band = np.where((np.abs(q - k) <= WINDOW) | (k >= S_LAT), 0.0, NEG).astype(np.float32).transpose(1, 0, 2)
    s, t = np.arange(P)[:, None], np.arange(P)[None, :]
    tri = np.stack([np.where(s <= t, 0.0, NEG), np.where(s >= t, 0.0, NEG)], 1).astype(np.float32)
    return {
        "k_ident": np.eye(P, dtype=np.float32),
        "k_perm": perm,
        "k_select": (np.arange(P)[:, None] % 32 == np.arange(2)[None, :]).astype(np.float32),
        "k_before": ((s < t) / np.float32(D_CONV)).astype(np.float32),
        "k_blocks": np.arange(32, dtype=np.float32).reshape(1, 32),
        "k_rope": np.stack([cos, sin], 1).astype(np.float32),
        "k_band": np.ascontiguousarray(band),
        "k_tri": np.ascontiguousarray(tri),
    }


def build(nc, a, out):
    order, place = psum_order()

    with ExitStack() as ctx:
        def sb(name, shape):
            return ctx.enter_context(nc.sbuf_tensor(name, shape, F32))

        H = sb("H", [P, TT, D])
        uT = sb("uT", [P, KD, T])
        ring = sb("ring", [P, NS, SLOT])
        arena = sb("arena", [P, KD, T])
        upad = sb("upad", [P, CT, 2, S_LAT + 2 * PAD])
        convT = sb("convT", [P, CT, T])
        qkT = sb("qkT", [P, 6, T])
        v_tok = sb("v_tok", [P, TT, NKV * DH])
        mqk = sb("mqk", [P, 8, T])
        mv_tok = sb("mv_tok", [P, TT, NH, MH + 1])
        mo_tok = sb("mo_tok", [P, TT, NH, MH])
        yab = sb("yab", [P, 8, T])
        wgate = sb("wgate", [P, KD, P])
        wrouter = sb("wrouter", [P, KD, NE])
        ident = sb("ident", [P, P])
        perm = sb("perm", [P, P])
        before = sb("before", [P, P])
        block_row = sb("block_row", [1, 32])
        rope = sb("rope", [P, 2, S_LAT])
        band = sb("band", [P, 2, T])
        tri = sb("tri", [P, 2, P])
        ones_mean = sb("ones_mean", [P, P])
        smallT = sb("smallT", [P, DEPTH, N_MOD + 12])
        cT = sb("cT", [P, KD, 32])
        select = sb("select", [P, 2])
        cwT = sb("cwT", [P, DEPTH, CT, TAPS])
        modT = sb("modT", [P, DEPTH, N_MOD, 2])
        gate_bias = sb("gate_bias", [P, DEPTH])
        sink = sb("sink", [P, DEPTH, NQ])
        norm_g = sb("norm_g", [P, DEPTH, NH * MH])
        b_router = sb("b_router", [P, NE])
        negM_tok = sb("negM_tok", [64, T])
        gate_cols = sb("gate_cols", [P, 8, 64])
        eps = sb("eps", [P, 1])
        ones_row = sb("ones_row", [64, T])
        ones_blk = sb("ones_blk", [P, NE])
        st = sb("st", [P, TT, 12])
        mv = sb("mv", [P, TT, 2])
        sd = sb("sd", [P, TT])
        rstd = sb("rstd", [P, TT])
        a_max = sb("a_max", [P, 3, 2])
        a_sum = sb("a_sum", [P, 3, 4])
        a_rden = sb("a_rden", [P, 4, 1])
        den = sb("den", [P, 3, 2])
        hstat = sb("hstat", [P, 4, TT * NH])
        r_sc = sb("r_sc", [P, TT, NE])
        r_sel = sb("r_sel", [P, TT, NE])
        r_rank = sb("r_rank", [P, TT, NE])
        r_cmp = sb("r_cmp", [P, TT, NE])
        r_hi = sb("r_hi", [P, TT, NG, 4])
        r_gs = sb("r_gs", [P, TT, NG])
        r_grank = sb("r_grank", [P, TT, NG])
        r_gcmp = sb("r_gcmp", [P, TT, NG])
        r_sum = sb("r_sum", [P, TT])
        gates = sb("gates", [P, TT, NE])
        r_pick = sb("r_pick", [P, 2, TT, NE])
        r_cnt = sb("r_cnt", [P, (TT + 1) * NE])
        r_blk = sb("r_blk", [P, 4, NE])
        r_slot = sb("r_slot", [P, 2, TT])
        r_w = sb("r_w", [P, 2, TT])
        r_cover = sb("r_cover", [1, 24, NE])
        r_expert = sb("r_expert", [1, 24])
        slot_id = ctx.enter_context(nc.sbuf_tensor("slot_id", [P, 2, TT], mybir.dt.uint32))
        expert_id = ctx.enter_context(nc.sbuf_tensor("expert_id", [1, 24], mybir.dt.int32))
        n_blocks = [blocks(l) for l in range(DEPTH)]
        xs = nc.dram_tensor("xs", [(n_blocks[0] + 2) * CAP, D], F32).ap()
        ys = nc.dram_tensor("ys", [n_blocks[0] * CAP, D], F32).ap()

        cw_rows = arena[0:TAPS, 0:DEPTH, :]
        small_rows = arena[0:N_MOD + 12, 2, 0:DEPTH * P].rearrange("r (l c) -> r l c", l=DEPTH)
        c_rows = arena[0:16, 3, 0:P]
        flat = arena[:, :, :].rearrange("p a b -> p (a b)")
        sq = flat[:, 0:CT * T].rearrange("p (a b) -> p a b", a=CT)
        grow = arena
        s_buf = arena
        w_buf = arena
        merged = arena
        u_nat = flat.rearrange("p (a b) -> p a b", a=TT)
        y_first = u_nat
        y_second = yab[:, :, :].rearrange("p a b -> p (a b)").rearrange("p (a b) -> p a b", a=TT)
        x_blk = convT[:, :, :].rearrange("p a b -> p (a b)").rearrange("p (u d) -> p u d", u=2)
        xT_blk = mo_tok[:, :, :, :].rearrange("p a b c -> p (a b c)").rearrange("p (u k t) -> p u k t", u=2, k=KD)
        y_blk = qkT[:, 0:4, :].rearrange("p a b -> p (a b)").rearrange("p (u d) -> p u d", u=2)
        silu_blk, hid_blk, hT_blk = mqk[:, 0:2, :], mqk[:, 2:4, :], mqk[:, 4:6, :]
        zeros = yab[:, 0:2, :].rearrange("p a b -> p (a b)")
        uflat = uT[:, :, :].rearrange("p a b -> p (a b)")
        ln_g, ln_b = uflat[:, 0:D], uflat[:, D:2 * D]
        g_rows = uflat[:, 2 * D:4 * D].rearrange("p (c d) -> p c d", c=2)
        tri_buf = upad[:, :, :, :].rearrange("p a b c -> p (a b c)")[:, 0:2 * TT * P]\
            .rearrange("p (u s t) -> p u s t", u=2, s=TT)
        mod_rows = upad[:, :, :, :].rearrange("p a b c -> p (a b c)")[:, 2 * TT * P:2 * TT * P + 512]\
            .rearrange("p (u n) -> p u n", u=2)
        hacc = convT[:, :, :].rearrange("p t (h d) -> p t h d", h=NH)
        hsq = arena[:, 0:TT, :].rearrange("p t (h d) -> p t h d", h=NH)
        yc = qkT
        sig = mqk
        psum = [ctx.enter_context(nc.psum_tensor(f"psum{b}", [P, 512], F32)) for b in range(BANKS)]

        def sem(name):
            return ctx.enter_context(nc.semaphore(name))

        ready = [sem(f"psum_ready{b}") for b in range(BANKS)]
        drained = [sem(f"psum_drained{b}") for b in range(BANKS)]
        loaded = [sem(f"slot_loaded{s}") for s in range(NS)]
        k_copy_loaded = sem("k_copy_loaded")
        setup_loaded = sem("setup_loaded")
        x_loaded = sem("x_loaded")
        ln_loaded = sem("ln_rows_loaded")
        wgate_loaded = sem("wgate_loaded")
        wgate_cleared = sem("wgate_cleared")
        consts_set = sem("consts_set")
        c_ready = sem("c_ready")
        h_ready = sem("h_ready")
        ln_var, ln_std = sem("ln_var"), sem("ln_std")
        conv_ready, sq_ready, scaled_ready, ya_ready = (sem("conv_ready"), sem("conv_squares"), sem("conv_scaled"),
                                                        sem("ya_ready"))
        rope_ready = sem("rope_ready")
        yb_done = sem("attention_done")
        gate_x, gate_l, gate_m, gate_em = sem("gate_negabs"), sem("gate_softplus"), sem("gate_m"), sem("gate_exp_m")
        s_ready, p_exp, p_ready = sem("scores_ready"), sem("probs_exp"), sem("probs_ready")
        tri_ready = sem("tri_ready")
        hc_ready, hsq_ready, hvar, hstd, hn_ready = (sem("head_centered"), sem("head_squares"), sem("head_var"),
                                                     sem("head_std"), sem("head_normed"))
        merged_ready = sem("merged_ready")
        ROLE = {"x0": 0, "x1": 1, "g": 2, "h": 3, "u": 4, "d0": 5, "d1": 6}
        blk_ready = {r: sem(f"block_{r}_ready") for r in ROLE}
        blk_drained = {r: sem(f"block_{r}_drained") for r in ROLE}
        x_blk_loaded = [sem(f"block_tokens_loaded{u}") for u in range(2)]
        y_stored = [sem(f"block_output_stored{u}") for u in range(2)]
        picked, counted = sem("choices_ready"), sem("slots_ready")
        scattered = sem("tokens_scattered")
        gathered = [sem(f"outputs_gathered{t}") for t in range(TT)]
        zeros_set = sem("zeros_set")
        dve_chain, act_chain, out_sent = sem("dve_chain"), sem("act_chain"), sem("out_sent")

        def bank(*key):
            return psum[place[key][0]]

        def wait_ready(eng, *key):
            eng.wait_ge(ready[place[key][0]], place[key][1] + 1)

        def wait_bank(pe, *key):
            if place[key][1] > 0:
                pe.wait_ge(drained[place[key][0]], place[key][1])

        def wait_drained(eng, *key):
            eng.wait_ge(drained[place[key][0]], place[key][1] + 1)

        def ready_of(*key):
            return ready[place[key][0]]

        def drained_of(*key):
            return drained[place[key][0]]

        blk_base = [sum(n_blocks[:l]) for l in range(DEPTH)]
        xblk_base = [sum(n_blocks[:l]) + l for l in range(DEPTH)]

        def loads_before(l, u):
            return sum((n + 3 - u) // 2 for n in n_blocks[:l])

        def stores_before(l, u):
            return 1 + sum((n + 1 - u) // 2 for n in n_blocks[:l])

        win = [a["w_in"][l].rearrange("(k p) n -> p k n", p=P) for l in range(DEPTH)]
        wmod = [a["w_mod"][l].rearrange("(k p) n -> p k n", p=P) for l in range(DEPTH)]
        wout = [a["w_out"][l].rearrange("(k p) n -> p k n", p=P) for l in range(DEPTH)]
        wbr = [[a[n][l].rearrange("(k p) n -> p k n", p=P) for n in ("w_a_out", "w_b_out", "w_c_out")]
               for l in range(DEPTH)]

        def slot8(s):
            return ring[:, s, :].rearrange("p (k n) -> p k n", k=KD)

        def slot4(s):
            return ring[:, s, :].rearrange("p (k n) -> p k n", k=FT)

        stream = []
        for l in range(DEPTH):
            nt = token_tiles(l)

            def used(key, last):
                stream.append((key, ready_of(*last), place[last][1] + 1))
            for n in range(MOD_FIRST if l == 0 else 0):
                used(("mod", l, n), ("mod", l, n))
            for j in range(CT):
                used(("a", l, j), ("gate", l, j))
            used(("v", l), ("v", l))
            used(("kk", l), ("qk", l, 5))
            for c in range(2):
                used(("q", l, c), ("qk", l, 2 * c + 1))
            for c in range(4):
                used(("mqk", l, c), ("mqk", l, 2 * c + 1))
            for c in range(2):
                used(("mv", l, c), ("mv", l, c, TT // 2 - 1))
            for c in range(2):
                used(("mo", l, c), ("mo", l, c, nt // 2 - 1))
            for x in later_modulation(l):
                used(("mod",) + x, ("mod",) + x)
            for j in range(KD // 2):
                last = 2 * j + 1
                used(("bga", l, j), ("bga", l, last))
                used(("bgb", l, j), ("bgb", l, last))
                used(("bgc", l, j), ("bgc", l, last))
                used(("yab", l, j), ("yb", l, last))
                used(("yc", l, j), ("yc_", l, last))
            for c in range(4):
                used(("out", l, c), ("out", l, c, nt // 2 - 1))
            nb = n_blocks[l]
            for b in range(nb + 1):
                if b < nb:
                    for x in ("g0", "g1", "u0", "u1"):
                        stream.append((("moe", l, b, x), blk_ready[x[0]], blk_base[l] + b + 1))
                if b > 0:
                    for x in ("d0", "d1"):
                        stream.append((("moe", l, b, x), blk_ready[x], blk_base[l] + b))
        index = {key: n for n, (key, _, _) in enumerate(stream)}

        def slot_of(*key):
            return index[key] % NS

        def wait_slot(eng, *key):
            eng.wait_ge(loaded[index[key] % NS], 32 * (index[key] // NS + 1))

        block = ctx.enter_context(nc.Block())

        @block.sync
        def _(sp):
            def load(key, offset=None):
                s = index[key] % NS
                w8, w4 = slot8(s), slot4(s)
                kind, l = key[0], key[1]
                if kind == "mod":
                    n = key[2]
                    src = wmod[l][:, :, bass.ds(n * 256, 256)]
                    pairs = [(w8[:, 0:4, :], src[:, 0:4, :]), (w8[:, 4:8, :], src[:, 4:8, :])]
                elif kind == "a":
                    j = key[2]
                    pairs = [(w8[:, :, g * P:(g + 1) * P],
                              win[l][:, :, C_A + g * D_CONV + j * P:C_A + g * D_CONV + (j + 1) * P]) for g in range(2)]
                elif kind == "v":
                    pairs = [(w8[:, 4 * g:4 * g + 4, 0:P], win[l][:, 4 * g:4 * g + 4, C_V:C_V + P]) for g in range(2)]
                elif kind == "kk":
                    copies = [(w8[:, :, (2 * g + r) * DH:(2 * g + r + 1) * DH],
                               win[l][:, :, C_K + g * DH:C_K + (g + 1) * DH]) for r in range(2) for g in range(NKV)]
                    pairs = copies[0:2]
                    for dst, src in copies[2:4]:
                        sp.dma_start(dst, src).then_inc(k_copy_loaded, 16)
                elif kind in ("q", "mqk", "mv", "mo"):
                    c0 = {"q": C_Q, "mqk": C_MQ, "mv": C_MV, "mo": C_MO}[kind] + 256 * key[2]
                    pairs = [(w8[:, 4 * g:4 * g + 4, :], win[l][:, 4 * g:4 * g + 4, c0:c0 + 256]) for g in range(2)]
                elif kind in ("bga", "bgb", "bgc"):
                    c0 = C_BG + "abc".index(kind[2]) * D + 256 * key[2]
                    pairs = [(w8[:, 4 * g:4 * g + 4, :], win[l][:, 4 * g:4 * g + 4, c0:c0 + 256]) for g in range(2)]
                elif kind == "yab":
                    c = slice(256 * key[2], 256 * key[2] + 256)
                    pairs = [(w8[:, 4 * g:4 * g + 4, :], wbr[l][g][:, :, c]) for g in range(2)]
                elif kind == "yc":
                    c = slice(256 * key[2], 256 * key[2] + 256)
                    pairs = [(w8[:, 2 * g:2 * g + 2, :], wbr[l][2][:, 2 * g:2 * g + 2, c]) for g in range(2)]
                elif kind == "out":
                    c = slice(256 * key[2], 256 * key[2] + 256)
                    pairs = [(w8[:, 4 * g:4 * g + 4, :], wout[l][:, 4 * g:4 * g + 4, c]) for g in range(2)]
                else:
                    e, x = offset, key[3]
                    half = int(x[1])
                    if x[0] == "d":
                        src = a["moe_w_dn"][l, e].rearrange("(k p) n -> p k n", p=P)[:, :, half * 512:half * 512 + 512]
                    else:
                        c = "gu".index(x[0]) * DE
                        src = a["moe_w_gu"][l, e].rearrange("(k p) n -> p k n", p=P)[:, 4 * half:4 * half + 4, c:c + DE]
                    pairs = [(w4[:, 2 * g:2 * g + 2, :], src[:, 2 * g:2 * g + 2, :]) for g in range(2)]
                for dst, src in pairs:
                    sp.dma_start(dst, src).then_inc(loaded[s], 16)

            def load_when_free(key, offset=None):
                n = index[key]
                if n >= NS:
                    sp.wait_ge(stream[n - NS][1], stream[n - NS][2])
                load(key, offset)

            def load_tokens(l, b, u):
                sp.dma_start(x_blk[:, u, :], xs[bass.ds(b * CAP, CAP), :]).then_inc(x_blk_loaded[u], 16)

            def expert(b):
                return sp.value_load(expert_id[0:1, bass.ds(b, 1)], min_val=0, max_val=NE - 1)

            keys = [key for key, _, _ in stream]
            at = 0
            while at < len(keys):
                key = keys[at]
                l = key[1]
                if key[0] == "moe":
                    nb = n_blocks[l]
                    base = index[("moe", l, 0, "g0")]
                    sp.wait_ge(counted, l + 1)
                    e = expert(0)
                    for x in ("g0", "g1", "u0", "u1"):
                        load_when_free(("moe", l, 0, x), e)
                    sp.wait_ge(scattered, 16 * sum(2 * token_tiles(x) for x in range(l + 1)))
                    load_tokens(l, 0, 0)
                    load_tokens(l, 1, 1)
                    sp.wait_ge(blk_ready["x1"], xblk_base[l] + 1)
                    load_tokens(l, 2, 0)

                    def weights_and_tokens(b, first, i):
                        e, e_before = expert(b), expert(b - 1)
                        for x in ("g0", "g1", "u0", "u1", "d0", "d1"):
                            k = ("moe", l, first, x)
                            _, free, value = stream[index[k] + (0 if i is None else 12) - NS]
                            sp.wait_ge(free, value if i is None else (i - 1) * 2 + value)
                            load(k, e_before if x[0] == "d" else e)
                        sp.wait_ge(blk_ready["x1"], b + (xblk_base[l] + 1))
                        load_tokens(l, b + 2, first % 2)

                    for first in (1, 2):
                        weights_and_tokens(first, first, None)
                    with sp.Fori(1, (nb - 1) // 2) as i:
                        for first in (1, 2):
                            weights_and_tokens(i * 2 + first, first, i)
                    e = expert(nb - 1)
                    for x in ("d0", "d1"):
                        load_when_free(("moe", l, nb, x), e)
                    at += 6 * nb
                else:
                    load_when_free(key)
                    at += 1
            sp.wait_ge(h_ready, TT + sum(2 * token_tiles(l) for l in range(DEPTH)))
            sp.dma_start(out.rearrange("b (t p) d -> p (b t) d", p=P), H[:, 0:2, :]).then_inc(out_sent, 16)
            sp.wait_ge(out_sent, 16)
            for u in range(2):
                sp.wait_ge(x_blk_loaded[u], 16 * loads_before(DEPTH, u))

        setup = []

        def row_pairs():
            setup.append((ident[:, :], a["k_ident"]))
            for l in range(DEPTH):
                setup.append((small_rows[0:N_MOD, l, :], a["b_mod"][l].rearrange("(r c) -> r c", c=P)))
                for i, n in enumerate(("conv_b", "conv_ln_g", "conv_ln_b")):
                    setup.append((small_rows[N_MOD + 4 * i:N_MOD + 4 * i + 4, l, :],
                                  a[n][l].rearrange("(r c) -> r c", c=P)))
                setup.append((cw_rows[:, l, :], a["conv_w"][l]))
            setup.append((select[:, :], a["k_select"]))
            setup.append((c_rows[0:8, :], a["c"][0].rearrange("(r c) -> r c", c=P)))
            setup.append((c_rows[8:16, :], a["c_ctx"].rearrange("(r c) -> r c", c=P)))
            setup.append((perm[:, :], a["k_perm"]))
            setup.append((rope[:, :, :], a["k_rope"]))
            setup.append((before[:, :], a["k_before"]))
            setup.append((block_row[:, :], a["k_blocks"]))
            setup.append((band[:, :, :], a["k_band"]))
            setup.append((tri[:, :, :], a["k_tri"]))
            setup.append((wrouter[:, :, :], a["w_router"].rearrange("(k p) n -> p k n", p=P)))
            setup.append((b_router[:, :], a["b_router"].partition_broadcast(P)))
            for l in range(DEPTH):
                setup.append((sink[:, l, :], a["attn_sink"][l].partition_broadcast(P)))
                setup.append((norm_g[:, l, :], a["mlstm_norm_g"][l].partition_broadcast(P)))
                for typ in range(2):
                    for d in range(2):
                        r = 64 * typ + 32 * d
                        setup.append((gate_bias[r:r + NH, l:l + 1],
                                      a["mlstm_gate_b"][l, d, typ].rearrange("(h o) -> h o", o=1)))
        row_pairs()
        SETUP = 16 * len(setup)

        @block.gpsimd
        def _(pool):
            def route_and_combine(l):
                nt, nb = token_tiles(l), n_blocks[l]
                pool.wait_ge(counted, l + 1)
                for t in range(nt):
                    for h in range(2):
                        wait_drained(pool, "nat", l, t, h)
                for u in range(2):
                    pool.wait_ge(y_stored[u], 16 * stores_before(l, u))
                    if l:
                        pool.wait_ge(x_blk_loaded[u], 16 * loads_before(l, u))
                for t in range(nt):
                    for c in range(2):
                        pool.indirect_dma_start(xs, bass.IndirectOffsetOnAxis(slot_id[:, c, t:t + 1], 0),
                                                u_nat[:, t, :], None).then_inc(scattered, 16)

                def store(b, u):
                    for r in ("d0", "d1"):
                        pool.wait_ge(blk_drained[r], b + (blk_base[l] + 1))
                    pool.dma_start(ys[bass.ds(b * CAP, CAP), :], y_blk[:, u, :]).then_inc(y_stored[u], 16)

                with pool.Fori(0, (nb - 1) // 2) as i:
                    for u in range(2):
                        store(i * 2 + u, u)
                store(nb - 1, (nb - 1) % 2)
                pool.wait_ge(scattered, 16 * sum(2 * token_tiles(x) for x in range(l + 1)))
                for u in range(2):
                    pool.wait_ge(y_stored[u], 16 * stores_before(l + 1, u))
                for t in range(nt):
                    for c, dst in enumerate((y_first, y_second)):
                        pool.indirect_dma_start(dst[:, t, :], None, ys,
                                                bass.IndirectOffsetOnAxis(slot_id[:, c, t:t + 1], 0))\
                            .then_inc(gathered[t], 16)
                for t in range(nt):
                    pool.wait_ge(gathered[t], 32 * (l + 1))

            for tile, (name, n) in enumerate((("x", S_LAT // P), ("ctx", S_CTX // P))):
                pool.dma_start(H[:, 2 * tile:2 * tile + 2, :],
                               a[name].rearrange("b (t p) d -> p (b t) d", p=P)).then_inc(x_loaded, 16)
            pool.dma_start(ln_g, a["ln_in_g"].partition_broadcast(P)).then_inc(ln_loaded, 16)
            pool.dma_start(ln_b, a["ln_in_b"].partition_broadcast(P)).then_inc(ln_loaded, 16)
            pool.wait_ge(consts_set, 1)
            for dst, src in setup:
                pool.dma_start(dst, src).then_inc(setup_loaded, 16)
            for l in range(DEPTH):
                if l:
                    wait_ready(pool, "ig", l - 1)
                else:
                    pool.wait_ge(wgate_cleared, 1)
                for typ in range(2):
                    for d in range(2):
                        c = C_MG + 8 * d + 4 * typ
                        r = 64 * typ + 32 * d
                        pool.dma_start(wgate[:, :, r:r + NH], win[l][:, :, c:c + NH]).then_inc(wgate_loaded, 16)
                if l == 0:
                    wait_ready(pool, "mod", 0, MOD_FIRST - 1)
                    pool.wait_ge(zeros_set, 1)
                    rows = xs.rearrange("(b p) d -> p b d", p=P)
                    nb = n_blocks[0] + 2
                    for u, (b0, b1) in enumerate(((0, nb // 2), (nb // 2, nb))):
                        pool.dma_start(rows[:, b0:b1, :], zeros.unsqueeze(1).broadcast_to([P, b1 - b0, D]))\
                            .then_inc(y_stored[u], 16)
                for which, (g, b) in enumerate((("ln1_g", "ln1_b"), ("ln2_g", "ln2_b"))):
                    if which == 0:
                        wait_ready(pool, "bgc", l, KD - 1)
                    else:
                        wait_ready(pool, "nat", l, token_tiles(l) - 1, 1)
                    pool.dma_start(ln_g, a[g][l].partition_broadcast(P)).then_inc(ln_loaded, 16)
                    pool.dma_start(ln_b, a[b][l].partition_broadcast(P)).then_inc(ln_loaded, 16)
                route_and_combine(l)
            pool.wait_ge(ln_loaded, 32 * (1 + 2 * DEPTH))
            pool.wait_ge(x_loaded, 32)
            pool.wait_ge(wgate_loaded, 64 * DEPTH)
            pool.wait_ge(setup_loaded, SETUP)

        h_base = [TT]
        for l in range(DEPTH):
            h_base += [h_base[-1] + token_tiles(l), h_base[-1] + 2 * token_tiles(l)]
        u_base = lambda l, which: 4 * (2 * l + which)
        n_att = [0, len(attention_units(0)), len(attention_units(0)) + len(attention_units(1))]

        @block.tensor
        def _(pe):
            def mm(dst, lhsT, rhs, start=True, stop=True):
                return nc.tensor.matmul(dst, lhsT, rhs, start=start, stop=stop)

            def done(ins, *key):
                ins.then_inc(ready_of(*key), 1)

            pe.wait_ge(setup_loaded, SETUP)
            prep = bank("prep")
            n_small = N_MOD + 12
            for l in range(DEPTH):
                nc.tensor.transpose(prep[:, l * n_small:(l + 1) * n_small], small_rows[:, l, :],
                                    ident[0:n_small, 0:n_small])
            nc.tensor.transpose(prep[:, 120:136], c_rows, ident[0:16, 0:16])
            for l in range(DEPTH):
                for j in range(CT):
                    o = 136 + (l * CT + j) * TAPS
                    last = nc.tensor.transpose(prep[:, o:o + TAPS], cw_rows[:, l, j * P:(j + 1) * P],
                                               ident[0:TAPS, 0:TAPS])
            done(last, "prep")

            for l in range(DEPTH):
                nt = token_tiles(l)
                n = nt * P

                def modulation(slots, s):
                    if 1 <= s <= len(slots):
                        x = slots[s - 1]
                        wait_drained(pe, "mod", *x)
                        wait_bank(pe, "modt", *x)
                        for half in range(2):
                            last = mm(bank("modt", *x)[:, 2 * half:2 * half + 2],
                                      mod_rows[:, x[1] % 2, half * P:(half + 1) * P], select[:, :])
                        done(last, "modt", *x)
                    if s < len(slots):
                        x = slots[s]
                        wait_slot(pe, "mod", *x)
                        wait_bank(pe, "mod", *x)
                        w = slot8(slot_of("mod", *x))
                        for k in range(KD):
                            q = 32 * (k % 4)
                            last = mm(bank("mod", *x)[q:q + 32, 0:256], cT[:, k, :], w[:, k, :], k < 4, k >= 4)
                        done(last, "mod", *x)

                if l == 0:
                    pe.wait_ge(c_ready, 2)
                    for s in range(MOD_FIRST + 1):
                        modulation(first_modulation(), s)
                later = later_modulation(l)

                def transposes(which, tiles):
                    first = h_base[2 * l + which] - (TT if (l, which) == (0, 0) else token_tiles(l - 1 + which))
                    for k in range(KD):
                        wait_bank(pe, which and "tr2" or "tr1", l, k)
                        if k == 0:
                            pe.wait_ge(h_ready, h_base[2 * l + which])
                        b = bank(which and "tr2" or "tr1", l, k)
                        for t in range(tiles):
                            last = nc.tensor.transpose(b[:, t * P:(t + 1) * P], H[:, t, k * P:(k + 1) * P], ident[:, :])
                        done(last, which and "tr2" or "tr1", l, k)

                transposes(0, TT)
                for k in range(KD):
                    wait_drained(pe, "tr1", l, k)

                def by_channel(w, cols, width, *key):
                    wait_bank(pe, *key)
                    for k in range(KD):
                        last = mm(bank(*key)[:, 0:width], w[:, k, cols:cols + P], uT[:, k, 0:width], k == 0, k == KD - 1)
                    done(last, *key)

                for j in range(CT):
                    wait_slot(pe, "a", l, j)
                    w = slot8(slot_of("a", l, j))
                    by_channel(w, 0, n, "val", l, j)
                    by_channel(w, P, n, "gate", l, j)
                wait_slot(pe, "v", l)
                w = slot8(slot_of("v", l))
                wait_bank(pe, "v", l)
                for t in range(TT):
                    for k in range(KD):
                        last = mm(bank("v", l)[:, t * P:(t + 1) * P], uT[:, k, t * P:(t + 1) * P], w[:, k, 0:P],
                                  k == 0, k == KD - 1)
                done(last, "v", l)
                pe.wait_ge(wgate_loaded, 64 * (l + 1))
                by_channel(wgate, 0, T, "ig", l)
                wait_slot(pe, "kk", l)
                pe.wait_ge(k_copy_loaded, 32 * (l + 1))
                for g in range(NKV):
                    by_channel(slot8(slot_of("kk", l)), g * P, T, "qk", l, 4 + g)
                for c in range(2):
                    wait_slot(pe, "q", l, c)
                    for g in range(2):
                        by_channel(slot8(slot_of("q", l, c)), g * P, n, "qk", l, 2 * c + g)
                for t in range(6):
                    wait_drained(pe, "qk", l, t)
                    wait_bank(pe, "perm", l, t)
                    done(mm(bank("perm", l, t)[:, 0:S_LAT], perm[:, :], qkT[:, t, 0:S_LAT]), "perm", l, t)
                for c in range(4):
                    wait_slot(pe, "mqk", l, c)
                    for g in range(2):
                        by_channel(slot8(slot_of("mqk", l, c)), g * P, n if c < 2 else T, "mqk", l, 2 * c + g)
                for kind, tiles, norm, src, src_ready in (("mv", TT, "mean", convT, conv_ready),
                                                          ("mo", nt, "var", sq, sq_ready)):
                    for c in range(2):
                        wait_slot(pe, kind, l, c)
                        w = slot8(slot_of(kind, l, c))
                        for h in range(tiles // 2):
                            wait_bank(pe, kind, l, c, h)
                            for t in (2 * h, 2 * h + 1):
                                for k in range(KD):
                                    last = mm(bank(kind, l, c, h)[:, (t % 2) * 256:(t % 2 + 1) * 256],
                                              uT[:, k, t * P:(t + 1) * P], w[:, k, :], k == 0, k == KD - 1)
                            done(last, kind, l, c, h)
                    pe.wait_ge(src_ready, l + 1)
                    wait_bank(pe, norm, l)
                    for j in range(CT):
                        last = mm(bank(norm, l)[:, 0:n], ones_mean[:, :], src[:, j, 0:n], j == 0, j == CT - 1)
                    done(last, norm, l)

                units = attention_units(l)
                pe.wait_ge(rope_ready, 6 * (l + 1))
                for i in range(len(units) + 3):
                    if i < len(units):
                        qt, h = units[i]
                        k0, k1 = key_range(qt)
                        r = slice(DH * (h % 2), DH * (h % 2) + DH)
                        wait_bank(pe, "S", l, i)
                        done(mm(bank("S", l, i)[:, k0:k1], qkT[r, h // 2, qt * P:(qt + 1) * P],
                                qkT[r, 4 + h // 4, k0:k1]), "S", l, i)
                    if 0 <= i - 2 < len(units):
                        m = i - 2
                        k0, k1 = key_range(units[m][0])
                        pe.wait_ge(p_ready, n_att[l] + m + 1)
                        wait_bank(pe, "PT", l, m)
                        for kt in range(k0 // P, k1 // P):
                            last = nc.tensor.transpose(bank("PT", l, m)[:, kt * P:(kt + 1) * P],
                                                       s_buf[:, m % 3, kt * P:(kt + 1) * P], ident[:, :])
                        done(last, "PT", l, m)
                    if 0 <= i - 3 < len(units):
                        m = i - 3
                        qt, h = units[m]
                        k0, k1 = key_range(qt)
                        if m == 0:
                            wait_drained(pe, "v", l)
                        wait_drained(pe, "PT", l, m)
                        wait_bank(pe, "PV", l, m)
                        g = h // 4
                        for kt in range(k0 // P, k1 // P):
                            last = mm(bank("PV", l, m)[:, 0:DH], s_buf[:, 3 + m % 2, kt * P:(kt + 1) * P],
                                      v_tok[:, kt, g * DH:(g + 1) * DH], kt == k0 // P, kt == k1 // P - 1)
                        done(last, "PV", l, m)
                    if i < len(units):
                        modulation(later, i)
                for t in range(nt):
                    wait_bank(pe, "yb_rows", l, t)
                    wait_drained(pe, "PV", l, NQ * (t + 1) - 1)
                    for c in range(4):
                        last = nc.tensor.transpose(bank("yb_rows", l, t)[:, c * P:(c + 1) * P],
                                                   convT[:, t, c * P:(c + 1) * P], ident[:, :])
                    done(last, "yb_rows", l, t)

                pe.wait_ge(gate_em, l + 1)
                wait_bank(pe, "cols", l)
                for i in range(8):
                    src = grow[0:64, 5 if i < 4 else 6, (i % 4) * P:(i % 4 + 1) * P]
                    last = nc.tensor.transpose(bank("cols", l)[:, i * 64:(i + 1) * 64], src, ident[0:64, 0:64])
                done(last, "cols", l)

                for t in range(8):
                    wait_drained(pe, "mqk", l, t)
                for c in range(2):
                    for h in range(TT // 2):
                        wait_drained(pe, "mv", l, c, h)
                for i in range(len(UNITS) + 2):
                    if i < len(UNITS):
                        h, d = UNITS[i]
                        wait_bank(pe, "bm", l, i)
                        done(mm(bank("bm", l, i)[:, 0:n],
                                ident[0:64, 32 * d + h:32 * d + h + 1].broadcast_to([64, P]),
                                negM_tok[:, 0:n]), "bm", l, i)
                    if 0 <= i - 1 < len(UNITS):
                        h, d = UNITS[i - 1]
                        for s in range(TT):
                            wait_bank(pe, "st", l, i - 1, s)
                            done(mm(bank("st", l, i - 1, s)[:, 0:n], mqk[:, NH + h, s * P:(s + 1) * P],
                                    mqk[:, h, 0:n]), "st", l, i - 1, s)
                    if 0 <= i - 2 < len(UNITS):
                        m = i - 2
                        h, d = UNITS[m]
                        wait_drained(pe, "st", l, m, TT - 1)
                        for half in range(nt // 2):
                            wait_bank(pe, "hv", l, m, half)
                            for t in (2 * half, 2 * half + 1):
                                tiles = scan_tiles(t, d)
                                for s in tiles:
                                    o = (t % 2) * (MH + 1)
                                    last = mm(bank("hv", l, m, half)[:, o:o + MH + 1],
                                              w_buf[:, 4 * (m % 2) + s, t * P:(t + 1) * P],
                                              mv_tok[:, s, h, :], s == tiles[0], s == tiles[-1])
                            done(last, "hv", l, m, half)
                    modulation(later, len(units) + i)

                def branch_gates(j):
                    for b in ("bga", "bgb", "bgc"):
                        if j % 2 == 0:
                            wait_slot(pe, b, l, j // 2)
                        by_channel(slot8(slot_of(b, l, j // 2)), (j % 2) * P, n, b, l, j)

                branch_gates(0)
                pe.wait_ge(hn_ready, l + 1)
                for h in range(NH):
                    wait_bank(pe, "yc", l, h)
                    for t in range(nt):
                        last = nc.tensor.transpose(bank("yc", l, h)[:, t * P:(t + 1) * P], hacc[:, t, h, :], ident[:, :])
                    done(last, "yc", l, h)

                pe.wait_ge(ya_ready, CT * (l + 1))
                for t in range(nt):
                    wait_drained(pe, "yb_rows", l, t)
                for j in range(KD):
                    cols = (j % 2) * P
                    if j:
                        branch_gates(j)
                    if j % 2 == 0:
                        wait_slot(pe, "yab", l, j // 2)
                        wait_slot(pe, "yc", l, j // 2)
                    wab, wc = slot8(slot_of("yab", l, j // 2)), slot8(slot_of("yc", l, j // 2))
                    for key, w, k0, y, y0 in (("ya", wab, 0, yab, 0), ("yb", wab, 4, yab, 4), ("yc_", wc, 0, yc, 0)):
                        if key == "yc_" and j == 0:
                            for h in range(NH):
                                wait_drained(pe, "yc", l, h)
                        wait_bank(pe, key, l, j)
                        for k in range(4):
                            last = mm(bank(key, l, j)[:, 0:n], w[:, k0 + k, cols:cols + P], y[:, y0 + k, 0:n],
                                      k == 0, k == 3)
                        done(last, key, l, j)

                def gate_rows(which, first):
                    for x in range(first // 2, first // 2 + 4):
                        wait_drained(pe, "modt", l, x)
                    for c in range(4):
                        key = ("g1" if which == 0 else "g2", l, c)
                        wait_bank(pe, *key)
                        for j in range(4):
                            last = mm(bank(*key)[:, j * P:(j + 1) * P],
                                      modT[:, l, first + 4 * (c % 2) + j, c // 2:c // 2 + 1].broadcast_to([P, P]),
                                      ident[:, :])
                        done(last, *key)

                gate_rows(0, G1)
                pe.wait_ge(merged_ready, KD * (l + 1))
                for h in range(nt // 2):
                    for c in range(4):
                        if h == 0:
                            wait_slot(pe, "out", l, c)
                        w = slot8(slot_of("out", l, c))
                        wait_bank(pe, "out", l, c, h)
                        for t in (2 * h, 2 * h + 1):
                            for k in range(KD):
                                last = mm(bank("out", l, c, h)[:, (t % 2) * 256:(t % 2 + 1) * 256],
                                          merged[:, k, t * P:(t + 1) * P], w[:, k, :], k == 0, k == KD - 1)
                        done(last, "out", l, c, h)

                transposes(1, nt)
                for k in range(KD):
                    wait_drained(pe, "tr2", l, k)
                wait_bank(pe, "router", l)
                for t in range(nt):
                    for k in range(KD):
                        last = mm(bank("router", l)[:, t * NE:(t + 1) * NE], uT[:, k, t * P:(t + 1) * P],
                                  wrouter[:, k, :], k == 0, k == KD - 1)
                done(last, "router", l)

                for t in range(nt):
                    for h in range(2):
                        wait_bank(pe, "nat", l, t, h)
                        for k in range(4):
                            last = nc.tensor.transpose(bank("nat", l, t, h)[:, k * P:(k + 1) * P],
                                                       uT[:, 4 * h + k, t * P:(t + 1) * P], ident[:, :])
                        done(last, "nat", l, t, h)
                gate_rows(1, G2)
                pe.wait_ge(picked, l + 1)
                wait_bank(pe, "count", l)
                b = bank("count", l)
                for t in range(nt + 1):
                    for x in range(min(t + 1, nt)):
                        last = mm(b[:, t * NE:(t + 1) * NE], before[:, :] if x == t else ones_mean[:, :],
                                  r_rank[:, x, :], x == 0, x == min(t, nt - 1))
                done(last, "count", l)

                uses = {}
                for key in order[:order.index(("count", l)) + 1]:
                    uses[place[key][0]] = place[key][1] + 1
                for bk, use in uses.items():
                    pe.wait_ge(drained[bk], use)

                def role_wait(role, count):
                    if not (isinstance(count, int) and count == 0):
                        pe.wait_ge(blk_drained[role], count)

                def x_transposes(b, u, nth):
                    pe.wait_ge(x_blk_loaded[u], nth * 16 + 16 * (loads_before(l, u) + 1))
                    for r, k0 in (("x0", 0), ("x1", 4)):
                        role_wait(r, b + xblk_base[l])
                        for k in range(4):
                            last = nc.tensor.transpose(psum[ROLE[r]][:, k * P:(k + 1) * P],
                                                       x_blk[:, u, (k0 + k) * P:(k0 + k + 1) * P], ident[:, :])
                        last.then_inc(blk_ready[r], 1)

                def up(b, u, role, first, i):
                    for half in range(2):
                        m = index[("moe", l, first, f"{role}{half}")]
                        pe.wait_ge(loaded[m % NS], i * 64 + 32 * (m // NS + 1))
                        if half == 0:
                            role_wait(role, b + blk_base[l])
                        for k in range(4):
                            last = mm(psum[ROLE[role]][:, :], xT_blk[:, u, 4 * half + k, :], slot4(m % NS)[:, k, :],
                                      half == 0 and k == 0, half == 1 and k == 3)
                    last.then_inc(blk_ready[role], 1)

                def hidden(b, u):
                    pe.wait_ge(blk_drained["u"], b + (blk_base[l] + 1))
                    role_wait("h", b + blk_base[l])
                    for k in range(FT):
                        last = nc.tensor.transpose(psum[ROLE["h"]][:, k * P:(k + 1) * P],
                                                   hid_blk[:, u, k * P:(k + 1) * P], ident[:, :])
                    last.then_inc(blk_ready["h"], 1)

                def down(b, u, first, i):
                    pe.wait_ge(blk_drained["h"], b + (blk_base[l] + 1))
                    for half in range(2):
                        m = index[("moe", l, first, f"d{half}")]
                        pe.wait_ge(loaded[m % NS], i * 64 + 32 * (m // NS + 1))
                        role = f"d{half}"
                        role_wait(role, b + blk_base[l])
                        for k in range(FT):
                            last = mm(psum[ROLE[role]][:, :], hT_blk[:, u, k * P:(k + 1) * P], slot4(m % NS)[:, k, :],
                                      k == 0, k == FT - 1)
                        last.then_inc(blk_ready[role], 1)

                def block_products(b, first, i):
                    u = first % 2
                    x_transposes(b + 1, 1 - u, i + (first + 1) // 2)
                    for r in ("x0", "x1"):
                        pe.wait_ge(blk_drained[r], b + (xblk_base[l] + 1))
                    up(b, u, "g", first, i)
                    if first > 0:
                        hidden(b - 1, 1 - u)
                    up(b, u, "u", first, i)
                    if first > 0:
                        down(b - 1, 1 - u, first, i)

                nb = n_blocks[l]
                x_transposes(0, 0, 0)
                block_products(0, 0, 0)
                with pe.Fori(0, (nb - 1) // 2) as i:
                    for first in (1, 2):
                        block_products(i * 2 + first, first, i)
                hidden(nb - 1, (nb - 1) % 2)
                down(nb - 1, (nb - 1) % 2, nb, 0)
                for r in ROLE:
                    pe.wait_ge(blk_drained[r], xblk_base[l] + nb + 1 if r[0] == "x" else blk_base[l] + nb)

        @block.scalar
        def _(act):
            chain = [0]

            def link(ins):
                chain[0] += 1
                ins.then_inc(act_chain, 1)
                act.wait_ge(act_chain, chain[0])

            f = nc.scalar.activation
            act.wait_ge(c_ready, 1)
            f(cT[:, :, 0:2], cT[:, :, 0:2], ACT.Silu).then_inc(c_ready, 1)

            def norm_std(first, tiles):
                act.wait_ge(ln_var, first)
                f(sd[:, 0:tiles], mv[:, 0:tiles, 1], ACT.Sqrt, bias=eps[:, :]).then_inc(ln_std, 1)

            act.wait_ge(consts_set, 1)
            norm_std(1, TT)
            for l in range(DEPTH):
                nt = token_tiles(l)
                n = nt * P
                later = later_modulation(l)

                def modulation(slots, s):
                    if s < len(slots):
                        x = slots[s]
                        wait_ready(act, "mod", *x)
                        if s >= 2:
                            wait_ready(act, "modt", *slots[s - 2])
                        f(mod_rows[:, x[1] % 2, :], bank("mod", *x)[:, 0:256], ACT.Copy)\
                            .then_inc(drained_of("mod", *x), 1)

                if l == 0:
                    for s in range(MOD_FIRST):
                        modulation(first_modulation(), s)
                for x in range(MOD_FIRST):
                    wait_drained(act, "modt", l, x)

                def modulate(which, key, tiles):
                    sh, sc = (SH1, SC1) if which == 0 else (SH2, SC2)
                    for k in range(1, KD, 2):
                        wait_ready(act, key, l, k)
                        for c in range(max(1, tiles // 2)):
                            last = f(uT[:, k, c * 256:(c + 1) * 256], bank(key, l, k)[:, c * 256:(c + 1) * 256],
                                     ACT.Identity, bias=modT[:, l, sh + k, c:c + 1], scale=modT[:, l, sc + k, c:c + 1])
                            if c == max(1, tiles // 2) - 1:
                                last.then_inc(drained_of(key, l, k), 1)

                modulate(0, "tr1", TT)
                for j in range(CT):
                    if j >= 2:
                        wait_drained(act, "val", l, j - 2)
                    wait_ready(act, "gate", l, j)
                    f(arena[:, 4 + j % 2, 0:n], bank("gate", l, j)[:, 0:n], ACT.Sigmoid).then_inc(drained_of("gate", l, j), 1)
                wait_ready(act, "v", l)
                f(v_tok[:, :, :], bank("v", l)[:, :].rearrange("p (t d) -> p t d", t=TT), ACT.Copy)\
                    .then_inc(drained_of("v", l), 1)
                for t in (4, 5, 0, 1, 2, 3):
                    w = T if t >= 4 else n
                    wait_ready(act, "qk", l, t)
                    f(qkT[:, t, 0:w], bank("qk", l, t)[:, 0:w], ACT.Copy).then_inc(drained_of("qk", l, t), 1)
                for t in range(6):
                    wait_ready(act, "perm", l, t)
                    f(arena[:, t // 2, (t % 2) * S_LAT:(t % 2 + 1) * S_LAT], bank("perm", l, t)[:, 0:S_LAT], ACT.Copy)\
                        .then_inc(drained_of("perm", l, t), 1)
                for t in range(8):
                    w = n if t < 4 else T
                    wait_ready(act, "mqk", l, t)
                    f(mqk[:, t, 0:w], bank("mqk", l, t)[:, 0:w], ACT.Copy,
                      scale=1.0 if t < 4 else K_SCALE).then_inc(drained_of("mqk", l, t), 1)
                for c in range(2):
                    for h in range(TT // 2):
                        wait_ready(act, "mv", l, c, h)
                        key = ("mv", l, c, h)
                        f(mv_tok[:, 2 * h:2 * h + 2, 2 * c:2 * c + 2, 0:MH],
                          bank(*key)[:, :].rearrange("p (t g d) -> p t g d", t=2, g=2), ACT.Copy)\
                            .then_inc(drained_of(*key), 1)
                wait_drained(act, "mean", l)
                f(sq[:, :, 0:n], convT[:, :, 0:n], ACT.Square).then_inc(sq_ready, 1)
                for c in range(2):
                    for h in range(nt // 2):
                        key = ("mo", l, c, h)
                        wait_ready(act, *key)
                        f(mo_tok[:, 2 * h:2 * h + 2, 2 * c:2 * c + 2, :],
                          bank(*key)[:, :].rearrange("p (t g d) -> p t g d", t=2, g=2), ACT.Sigmoid)\
                            .then_inc(drained_of(*key), 1)

                for u in range(2):
                    act.wait_ge(y_stored[u], 16)
                wait_ready(act, "var", l)
                f(yab[:, 0, 0:n], bank("var", l)[:, 0:n], ACT.Sqrt, bias=eps[:, :]).then_inc(drained_of("var", l), 1)
                act.wait_ge(scaled_ready, l + 1)
                for j in range(CT):
                    f(yab[:, j, 0:n], convT[:, j, 0:n], ACT.Silu, bias=smallT[:, l, N_MOD + 8 + j:N_MOD + 9 + j],
                      scale=smallT[:, l, N_MOD + 4 + j:N_MOD + 5 + j]).then_inc(ya_ready, 1)

                act.wait_ge(gate_x, l + 1)
                link(f(grow[0:64, 2, :], grow[0:64, 1, :], ACT.Exp))
                f(grow[0:64, 3, :], grow[0:64, 2, :], ACT.Ln, bias=1.0).then_inc(gate_l, 1)
                act.wait_ge(gate_m, l + 1)
                f(grow[0:64, 6, :], grow[0:64, 4, :], ACT.Exp, scale=-1.0).then_inc(gate_em, 1)

                units = attention_units(l)
                for i in range(len(units) + 2):
                    if i < len(units):
                        qt, h = units[i]
                        k0, k1 = key_range(qt)
                        act.wait_ge(s_ready, n_att[l] + i + 1)
                        f(s_buf[:, i % 3, k0:k1], s_buf[:, i % 3, k0:k1], ACT.Exp, bias=a_max[:, i % 3, 1:2],
                          accum_out=a_sum[:, i % 3, 0:1])
                        f(a_sum[:, i % 3, 1:2], sink[:, l, h:h + 1], ACT.Exp, bias=a_max[:, i % 3, 1:2])\
                            .then_inc(p_exp, 1)
                    if 0 <= i - 2 < len(units):
                        m = i - 2
                        k0, k1 = key_range(units[m][0])
                        wait_ready(act, "PT", l, m)
                        if m >= 2:
                            wait_ready(act, "PV", l, m - 2)
                        f(s_buf[:, 3 + m % 2, k0:k1], bank("PT", l, m)[:, k0:k1], ACT.Copy)\
                            .then_inc(drained_of("PT", l, m), 1)
                    if i < len(units):
                        modulation(later, i)

                for t in range(nt):
                    wait_ready(act, "yb_rows", l, t)
                    f(yab[:, 4:8, t * P:(t + 1) * P], bank("yb_rows", l, t)[:, :].rearrange("p (c q) -> p c q", c=4),
                      ACT.Copy).then_inc(drained_of("yb_rows", l, t), 1)

                for i in range(len(UNITS)):
                    h, d = UNITS[i]
                    r = 32 * d + h
                    act.wait_ge(tri_ready, len(UNITS) * l + i + 1)
                    if i >= 2:
                        wait_ready(act, "hv", l, i - 2, nt // 2 - 1)
                    for s in range(TT):
                        if s < nt:
                            last = f(w_buf[:, 4 * (i % 2) + s, s * P:(s + 1) * P], tri_buf[:, i % 2, s, :], ACT.Exp)
                        for t0, t1 in scan_ranges(s, d, n):
                            last = f(w_buf[:, 4 * (i % 2) + s, t0:t1], bank("bm", l, i)[:, t0:t1], ACT.Exp,
                                     bias=gate_cols[:, s, r:r + 1])
                    last.then_inc(drained_of("bm", l, i), 1)
                    modulation(later, len(units) + i)
                act.wait_ge(hc_ready, l + 1)
                f(hsq[:, 0:nt], hacc[:, 0:nt], ACT.Square).then_inc(hsq_ready, 1)
                act.wait_ge(hvar, l + 1)
                f(hstat[:, 2, 0:NH * nt], hstat[:, 1, 0:NH * nt], ACT.Sqrt, bias=eps[:, :], scale=1.0 / MH)\
                    .then_inc(hstd, 1)
                for h in range(NH):
                    wait_ready(act, "yc", l, h)
                    f(yc[:, h, 0:n], bank("yc", l, h)[:, 0:n], ACT.Copy).then_inc(drained_of("yc", l, h), 1)

                for j in range(KD):
                    if j >= 2:
                        wait_drained(act, "yc_", l, j - 2)
                    for b, key in enumerate(("bga", "bgb", "bgc")):
                        wait_ready(act, key, l, j)
                        f(sig[:, 3 * (j % 2) + b, 0:n], bank(key, l, j)[:, 0:n], ACT.Sigmoid)\
                            .then_inc(drained_of(key, l, j), 1)

                def gate_rows(which):
                    for c in range(4):
                        key = ("g1" if which == 0 else "g2", l, c)
                        wait_ready(act, *key)
                        f(g_rows[:, c // 2, (c % 2) * 512:(c % 2 + 1) * 512], bank(*key)[:, :], ACT.Copy)\
                            .then_inc(drained_of(*key), 1)

                gate_rows(0)
                norm_std(2 * l + 2, nt)
                modulate(1, "tr2", nt)
                wait_ready(act, "router", l)
                f(r_sc[:, 0:nt, :], bank("router", l)[:, 0:nt * NE].rearrange("p (t e) -> p t e", t=nt), ACT.Sigmoid)\
                    .then_inc(drained_of("router", l), 1)
                for t in range(nt):
                    for h in range(2):
                        wait_ready(act, "nat", l, t, h)
                        f(u_nat[:, t, h * 512:(h + 1) * 512], bank("nat", l, t, h)[:, :], ACT.Copy)\
                            .then_inc(drained_of("nat", l, t, h), 1)
                gate_rows(1)

                def x_copy(b, u):
                    act.wait_ge(blk_ready["x0"], b + (xblk_base[l] + 1))
                    f(xT_blk[:, u, 0:4, :], psum[ROLE["x0"]][:, :].rearrange("p (k t) -> p k t", k=4), ACT.Copy)\
                        .then_inc(blk_drained["x0"], 1)

                def silu(b, u):
                    act.wait_ge(blk_ready["g"], b + (blk_base[l] + 1))
                    f(silu_blk[:, u, :], psum[ROLE["g"]][:, :], ACT.Silu).then_inc(blk_drained["g"], 1)

                def output(b, u, nth):
                    act.wait_ge(blk_ready["d0"], b + (blk_base[l] + 1))
                    act.wait_ge(y_stored[u], nth * 16 + 16 * stores_before(l, u))
                    f(y_blk[:, u, 0:512], psum[ROLE["d0"]][:, :], ACT.Copy).then_inc(blk_drained["d0"], 1)

                nb = n_blocks[l]
                x_copy(0, 0)
                x_copy(1, 1)
                silu(0, 0)
                with act.Fori(0, (nb - 1) // 2) as i:
                    for first in (1, 2):
                        x_copy(i * 2 + first + 1, (first + 1) % 2)
                        silu(i * 2 + first, first % 2)
                        output(i * 2 + first - 1, (first - 1) % 2, i)
                output(nb - 1, (nb - 1) % 2, (nb - 1) // 2)
                norm_std(2 * l + 3, nt)

        @block.vector
        def _(dve):
            v = nc.vector
            chain = [0]

            def link(ins):
                chain[0] += 1
                ins.then_inc(dve_chain, 1)
                dve.wait_ge(dve_chain, chain[0])

            v.memset(eps[:, :], EPS)
            v.memset(gate_bias[:, :], 0.0)
            v.memset(ones_mean[:, :], 1.0 / D_CONV).then_inc(consts_set, 1)
            v.memset(wgate[:, :, :], 0.0).then_inc(wgate_cleared, 1)
            v.memset(mv_tok[:, :, :, MH:MH + 1], 1.0)
            v.memset(zeros, 0.0).then_inc(zeros_set, 1)
            v.memset(ones_blk[:, :], 1.0)
            link(v.memset(ones_row[:, :], 1.0))
            wait_ready(dve, "prep")
            prep = bank("prep")
            v.tensor_copy(smallT[:, :, :], prep[:, 0:120].rearrange("p (l c) -> p l c", l=DEPTH))
            link(v.memset(cT[:, :, :], 0.0))
            v.tensor_copy(cT[:, :, 0:2], prep[:, 120:136].rearrange("p (c k) -> p k c", c=2)).then_inc(c_ready, 1)
            v.tensor_copy(cwT[:, :, :, :], prep[:, 136:136 + 8 * TAPS].rearrange("p (l j w) -> p l j w", l=DEPTH, j=CT))\
                .then_inc(drained_of("prep"), 1)
            dve.wait_ge(drained_of("prep"), 1)
            for sc in (SC1, SC2):
                last = v.tensor_scalar(smallT[:, :, sc:sc + KD], smallT[:, :, sc:sc + KD], 1.0, None, ALU.add)
            link(last)

            def layer_norm(which, tiles):
                for t in range(tiles):
                    v.bn_stats(st[:, t, 0:6], H[:, t, 0:512])
                    link(v.bn_stats(st[:, t, 6:12], H[:, t, 512:1024]))
                    last = v.bn_aggr(mv[:, t, :], st[:, t, :])
                last.then_inc(ln_var, 1)
                dve.wait_ge(ln_std, which + 1)
                link(v.reciprocal(rstd[:, 0:tiles], sd[:, 0:tiles]))
                dve.wait_ge(ln_loaded, 32 * (which + 1))
                for t in range(tiles):
                    link(v.tensor_scalar(H[:, t, :], H[:, t, :], mv[:, t, 0:1], rstd[:, t:t + 1], ALU.subtract, ALU.mult))
                    link(v.tensor_tensor(H[:, t, :], H[:, t, :], ln_g, ALU.mult))
                    v.tensor_tensor(H[:, t, :], H[:, t, :], ln_b, ALU.add).then_inc(h_ready, 1)

            dve.wait_ge(x_loaded, 32)
            layer_norm(0, TT)

            for l in range(DEPTH):
                nt = token_tiles(l)
                n = nt * P
                streams = nt // 2

                def modulation(slots, s):
                    if 1 <= s <= len(slots):
                        m, x = slots[s - 1]
                        wait_ready(dve, "modt", m, x)
                        v.tensor_tensor(modT[:, m, 2 * x:2 * x + 2, :],
                                        bank("modt", m, x)[:, 0:4].rearrange("p (m c) -> p m c", c=2),
                                        smallT[:, m, 2 * x:2 * x + 2].unsqueeze(2).broadcast_to([P, 2, 2]), ALU.add)\
                            .then_inc(drained_of("modt", m, x), 1)

                if l == 0:
                    for s in range(1, MOD_FIRST + 1):
                        modulation(first_modulation(), s)
                later = later_modulation(l)
                for x in range(MOD_FIRST):
                    wait_drained(dve, "modt", l, x)

                def modulate(which, key, tiles):
                    sh, sc = (SH1, SC1) if which == 0 else (SH2, SC2)
                    for k in range(0, KD, 2):
                        wait_ready(dve, key, l, k)
                        for c in range(max(1, tiles // 2)):
                            last = v.tensor_scalar(uT[:, k, c * 256:(c + 1) * 256], bank(key, l, k)[:, c * 256:(c + 1) * 256],
                                                   modT[:, l, sc + k, c:c + 1], modT[:, l, sh + k, c:c + 1],
                                                   ALU.mult, ALU.add)
                        last.then_inc(drained_of(key, l, k), 1)

                modulate(0, "tr1", TT)

                link(v.memset(upad[:, :, :, :], 0.0))
                for j in range(CT):
                    wait_ready(dve, "val", l, j)
                    wait_drained(dve, "gate", l, j)
                    v.tensor_tensor(upad[:, j, 0:streams, PAD:PAD + S_LAT],
                                    bank("val", l, j)[:, 0:n].rearrange("p (s t) -> p s t", s=streams),
                                    arena[:, 4 + j % 2, 0:n].rearrange("p (s t) -> p s t", s=streams), ALU.mult)\
                        .then_inc(drained_of("val", l, j), 1)
                    wait_drained(dve, "val", l, j)
                wait_ready(dve, "ig", l)
                v.tensor_scalar(grow[:, 7, :], bank("ig", l)[:, :], gate_bias[:, l:l + 1], None, ALU.add)\
                    .then_inc(drained_of("ig", l), 1)
                wait_drained(dve, "ig", l)
                cv = convT[:, :, :].rearrange("p j (s t) -> p j s t", s=2)
                for w in range(TAPS):
                    for j in range(CT):
                        src = upad[:, j, 0:streams, w:w + S_LAT]
                        if w == 0:
                            last = v.tensor_scalar(cv[:, j, 0:streams], src, cwT[:, l, j, 0:1],
                                                   smallT[:, l, N_MOD + j:N_MOD + j + 1], ALU.mult, ALU.add)
                        else:
                            last = v.scalar_tensor_tensor(cv[:, j, 0:streams], src, cwT[:, l, j, w:w + 1],
                                                          cv[:, j, 0:streams], ALU.mult, ALU.add)
                    if w < TAPS - 1:
                        link(last)
                last.then_inc(conv_ready, 1)

                for t in range(6):
                    wait_drained(dve, "perm", l, t)
                    partner = arena[:, t // 2, (t % 2) * S_LAT:(t % 2 + 1) * S_LAT]
                    v.tensor_tensor(partner, partner, rope[:, 1, :], ALU.mult)
                    link(v.tensor_tensor(qkT[:, t, 0:S_LAT], qkT[:, t, 0:S_LAT], rope[:, 0, :], ALU.mult))
                    v.tensor_tensor(qkT[:, t, 0:S_LAT], qkT[:, t, 0:S_LAT], partner, ALU.add).then_inc(rope_ready, 1)
                dve.wait_ge(rope_ready, 6 * (l + 1))
                wait_ready(dve, "mean", l)
                v.tensor_tensor(convT[:, :, 0:n], convT[:, :, 0:n],
                                bank("mean", l)[:, 0:n].unsqueeze(1).broadcast_to([P, CT, n]), ALU.subtract)\
                    .then_inc(drained_of("mean", l), 1)
                wait_drained(dve, "var", l)
                link(v.reciprocal(yab[:, 0, 0:n], yab[:, 0, 0:n]))
                v.tensor_tensor(convT[:, :, 0:n], convT[:, :, 0:n],
                                yab[:, 0:1, 0:n].broadcast_to([P, CT, n]), ALU.mult).then_inc(scaled_ready, 1)

                link(v.tensor_copy(grow[0:64, 0, :], grow[64:128, 7, :]))
                link(v.tensor_scalar(grow[0:64, 1, :], grow[0:64, 0, :], -1.0, None, ALU.mult))
                v.tensor_tensor(grow[0:64, 1, :], grow[0:64, 0, :], grow[0:64, 1, :], ALU.min).then_inc(gate_x, 1)
                dve.wait_ge(gate_l, l + 1)
                link(v.scalar_tensor_tensor(grow[0:64, 0, :], grow[0:64, 0, :], 0.0, grow[0:64, 3, :],
                                            ALU.min, ALU.subtract))

                def reorder(dst, src, back):
                    lat, ctx_ = (slice(0, S_LAT), slice(S_LAT, T))
                    rev_lat, rev_ctx = slice(S_LAT - 1, None, -1), slice(T - 1, S_LAT - 1, -1)
                    if back:
                        v.tensor_copy(dst[0:32, lat], src[0:32, ctx_])
                        v.tensor_copy(dst[0:32, ctx_], src[0:32, lat])
                        v.tensor_copy(dst[32:64, lat], src[32:64, rev_ctx])
                        return v.tensor_copy(dst[32:64, ctx_], src[32:64, rev_lat])
                    v.tensor_copy(dst[0:32, lat], src[0:32, ctx_])
                    v.tensor_copy(dst[0:32, ctx_], src[0:32, lat])
                    v.tensor_copy(dst[32:64, lat], src[32:64, rev_ctx])
                    return v.tensor_copy(dst[32:64, ctx_], src[32:64, rev_lat])

                reorder(grow[0:64, 1, :], grow[0:64, 0, :], False)
                link(reorder(grow[0:64, 2, :], grow[0:64, 7, :], False))
                link(v.tensor_tensor_scan(grow[0:64, 3, :], ones_row[:, :], grow[0:64, 1, :], 0.0, ALU.mult, ALU.add))
                link(v.tensor_tensor(grow[0:64, 2, :], grow[0:64, 2, :], grow[0:64, 3, :], ALU.subtract))
                link(v.tensor_tensor_scan(grow[0:64, 0, :], grow[0:64, 2, :], grow[0:64, 2, :], 0.0, ALU.max, ALU.max))
                link(v.tensor_tensor(grow[0:64, 3, :], grow[0:64, 3, :], grow[0:64, 0, :], ALU.add))
                link(v.tensor_scalar(grow[0:64, 0, :], grow[0:64, 0, :], -1.0, None, ALU.mult))
                reorder(negM_tok[:, :], grow[0:64, 0, :], True)
                reorder(grow[0:64, 5, :], grow[0:64, 2, :], True)
                reorder(grow[0:64, 4, :], grow[0:64, 3, :], True).then_inc(gate_m, 1)
                dve.wait_ge(gate_m, l + 1)
                units = attention_units(l)
                for i in range(len(units) + 3):
                    if i < len(units):
                        qt, h = units[i]
                        k0, k1 = key_range(qt)
                        b = i % 3
                        wait_ready(dve, "S", l, i)
                        if i >= 3:
                            wait_ready(dve, "PT", l, i - 3)
                        if k0 == 0:
                            ins = v.scalar_tensor_tensor(s_buf[:, b, :], bank("S", l, i)[:, :], A_SCALE, band[:, qt, :],
                                                         ALU.mult, ALU.add)
                        else:
                            ins = v.tensor_scalar(s_buf[:, b, k0:k1], bank("S", l, i)[:, k0:k1], A_SCALE, None, ALU.mult)
                        ins.then_inc(drained_of("S", l, i), 1)
                        wait_drained(dve, "S", l, i)
                        link(v.tensor_reduce(a_max[:, b, 0:1], s_buf[:, b, k0:k1], AX_X, ALU.max))
                        v.tensor_scalar(a_max[:, b, 1:2], a_max[:, b, 0:1], sink[:, l, h:h + 1], -1.0,
                                        ALU.max, ALU.mult).then_inc(s_ready, 1)
                    if 0 <= i - 1 < len(units):
                        m = i - 1
                        b = m % 3
                        k0, k1 = key_range(units[m][0])
                        dve.wait_ge(p_exp, n_att[l] + m + 1)
                        link(v.tensor_tensor(a_sum[:, b, 2:3], a_sum[:, b, 0:1], a_sum[:, b, 1:2], ALU.add))
                        v.reciprocal(a_rden[:, m % 4, :], a_sum[:, b, 2:3]).then_inc(p_ready, 1)
                    if 0 <= i - 3 < len(units):
                        m = i - 3
                        qt, h = units[m]
                        wait_ready(dve, "PV", l, m)
                        dve.wait_ge(p_ready, n_att[l] + m + 1)
                        if m == 0:
                            dve.wait_ge(ya_ready, CT * (l + 1))
                        v.tensor_scalar(convT[:, qt, h * DH:(h + 1) * DH], bank("PV", l, m)[:, 0:DH],
                                        a_rden[:, m % 4, :], None, ALU.mult).then_inc(drained_of("PV", l, m), 1)
                    if i < len(units):
                        modulation(later, i)
                wait_ready(dve, "cols", l)
                v.tensor_copy(gate_cols[:, :, :], bank("cols", l)[:, :].rearrange("p (i r) -> p i r", i=8))\
                    .then_inc(drained_of("cols", l), 1)
                wait_drained(dve, "cols", l)


                def triangles(i):
                    h, d = UNITS[i]
                    r = 32 * d + h
                    wait_ready(dve, "bm", l, i)
                    if i >= 2:
                        wait_drained(dve, "bm", l, i - 2)
                    for s in range(nt):
                        last = v.scalar_tensor_tensor(tri_buf[:, i % 2, s, :], bank("bm", l, i)[:, s * P:(s + 1) * P],
                                                      gate_cols[:, s, r:r + 1], tri[:, d, :], ALU.add, ALU.add)
                    last.then_inc(tri_ready, 1)

                def weights(i):
                    h, d = UNITS[i]
                    wait_drained(dve, "bm", l, i)
                    for s in range(TT):
                        wait_ready(dve, "st", l, i, s)
                        own = [(s * P, (s + 1) * P)] if s < nt else []
                        for t0, t1 in joined(scan_ranges(s, d, n) + own):
                            w = w_buf[:, 4 * (i % 2) + s, t0:t1]
                            last = v.tensor_tensor(w, bank("st", l, i, s)[:, t0:t1], w, ALU.mult)
                        last.then_inc(drained_of("st", l, i, s), 1)

                def outputs(i):
                    h, d = UNITS[i]
                    r = 32 * d + h
                    for half in range(nt // 2):
                        b = bank("hv", l, i, half)
                        wait_ready(dve, "hv", l, i, half)
                        raw = b[:, MH:2 * MH + 2:MH + 1]
                        link(v.scalar_tensor_tensor(den[:, 0, :], raw, -1.0, gate_cols[:, 4 + 2 * half:6 + 2 * half, r],
                                                    ALU.mult, ALU.max))
                        link(v.tensor_tensor(den[:, 1, :], raw, den[:, 0, :], ALU.max))
                        link(v.reciprocal(den[:, 2, :], den[:, 1, :]))
                        for t in range(2):
                            dst = hacc[:, 2 * half + t, h, :]
                            src = b[:, t * (MH + 1):t * (MH + 1) + MH]
                            if d == 0:
                                last = v.tensor_scalar(dst, src, den[:, 2, t:t + 1], None, ALU.mult)
                            else:
                                last = v.scalar_tensor_tensor(dst, src, den[:, 2, t:t + 1], dst, ALU.mult, ALU.add)
                        last.then_inc(drained_of("hv", l, i, half), 1)
                        wait_drained(dve, "hv", l, i, half)

                for i in range(len(UNITS) + 2):
                    if i < len(UNITS):
                        triangles(i)
                    if 0 <= i - 1 < len(UNITS):
                        weights(i - 1)
                    if 0 <= i - 2 < len(UNITS):
                        outputs(i - 2)
                    modulation(later, len(units) + i)

                hs = hstat[:, :, 0:NH * nt].rearrange("p a (t h) -> p a t h", t=nt)
                hv = hacc[:, 0:nt]
                link(v.tensor_reduce(hs[:, 0], hv, AX_X, ALU.add))
                link(v.tensor_scalar(hs[:, 0], hs[:, 0], 1.0 / MH, None, ALU.mult))
                v.tensor_tensor(hv, hv, hs[:, 0].unsqueeze(3).broadcast_to([P, nt, NH, MH]), ALU.subtract)\
                    .then_inc(hc_ready, 1)
                dve.wait_ge(hsq_ready, l + 1)
                v.tensor_reduce(hs[:, 1], hsq[:, 0:nt], AX_X, ALU.add).then_inc(hvar, 1)
                dve.wait_ge(hstd, l + 1)
                link(v.reciprocal(hs[:, 3], hs[:, 2]))
                link(v.tensor_tensor(hv, hv, hs[:, 3].unsqueeze(3).broadcast_to([P, nt, NH, MH]), ALU.mult))
                gain = norm_g[:, l, :].rearrange("p (h d) -> p h d", h=NH)
                link(v.tensor_tensor(hv, hv, gain.unsqueeze(1).broadcast_to([P, nt, NH, MH]), ALU.mult))
                wait_drained(dve, "mo", l, 0, nt // 2 - 1)
                wait_drained(dve, "mo", l, 1, nt // 2 - 1)
                v.tensor_tensor(hv, hv, mo_tok[:, 0:nt], ALU.mult).then_inc(hn_ready, 1)

                for j in range(KD):
                    for b, (key, gkey) in enumerate((("ya", "bga"), ("yb", "bgb"), ("yc_", "bgc"))):
                        wait_ready(dve, key, l, j)
                        wait_drained(dve, gkey, l, j)
                        dst = merged[:, j, 0:n] if b == 0 else sig[:, 6, 0:n]
                        v.tensor_tensor(dst, bank(key, l, j)[:, 0:n], sig[:, 3 * (j % 2) + b, 0:n], ALU.mult)\
                            .then_inc(drained_of(key, l, j), 1)
                        wait_drained(dve, key, l, j)
                        if b == 1:
                            link(v.tensor_tensor(merged[:, j, 0:n], merged[:, j, 0:n], sig[:, 6, 0:n], ALU.add))
                        if b == 2:
                            v.tensor_tensor(merged[:, j, 0:n], merged[:, j, 0:n], sig[:, 6, 0:n], ALU.add)\
                                .then_inc(merged_ready, 1)
                            dve.wait_ge(merged_ready, l * KD + j + 1)

                for h in range(nt // 2):
                    for c in range(4):
                        if (c, h) == (0, 0):
                            for x in range(4):
                                wait_drained(dve, "g1", l, x)
                        key = ("out", l, c, h)
                        wait_ready(dve, *key)
                        tmp = sig[:, 6, :].rearrange("p (t d) -> p t d", t=2)
                        hh = H[:, 2 * h:2 * h + 2, c * 256:(c + 1) * 256]
                        g = g_rows[:, h:h + 1, c * 256:(c + 1) * 256].broadcast_to([P, 2, 256])
                        v.tensor_tensor(tmp, bank(*key)[:, :].rearrange("p (t d) -> p t d", t=2), g, ALU.mult)\
                            .then_inc(drained_of(*key), 1)
                        wait_drained(dve, *key)
                        link(v.scalar_tensor_tensor(hh, hh, ALPHA, tmp, ALU.mult, ALU.add))
                layer_norm(2 * l + 1, nt)
                modulate(1, "tr2", nt)

                wait_drained(dve, "router", l)
                rs = r_sel[:, 0:nt, :].rearrange("p t (g e) -> p t g e", g=NG)
                rk = r_rank[:, 0:nt, :].rearrange("p t (g e) -> p t g e", g=NG)
                rc = r_cmp[:, 0:nt, :].rearrange("p t (g e) -> p t g e", g=NG)
                link(v.tensor_tensor(r_sel[:, 0:nt, :], r_sc[:, 0:nt, :],
                                     b_router[:, :].unsqueeze(1).broadcast_to([P, nt, NE]), ALU.add))
                hi = r_hi[:, 0:nt]
                v.tensor_tensor(hi[:, :, :, 0:2], rs[:, :, :, 0:3:2], rs[:, :, :, 1:4:2], ALU.max)
                link(v.tensor_tensor(hi[:, :, :, 2:4], rs[:, :, :, 0:3:2], rs[:, :, :, 1:4:2], ALU.min))
                gs, gc, gr = r_gs[:, 0:nt], r_gcmp[:, 0:nt], r_grank[:, 0:nt]
                v.tensor_tensor(gs, hi[:, :, :, 0], hi[:, :, :, 1], ALU.max)
                v.tensor_tensor(gc, hi[:, :, :, 0], hi[:, :, :, 1], ALU.min)
                link(v.tensor_tensor(gr, hi[:, :, :, 2], hi[:, :, :, 3], ALU.max))
                link(v.tensor_tensor(gc, gc, gr, ALU.max))
                link(v.tensor_tensor(gs, gs, gc, ALU.add))
                for e in range(4):
                    v.memset(r_grank[:, :, e:e + 1], float(3 - e))
                    last = v.memset(r_rank[:, :, :].rearrange("p t (g e) -> p t g e", g=NG)[:, :, :, e:e + 1], float(3 - e))
                link(last)
                for sft in range(1, 4):
                    k = 4 - sft
                    link(v.tensor_tensor(gc[:, :, 0:k], gs[:, :, 0:k], gs[:, :, sft:4], ALU.is_ge))
                    link(v.tensor_tensor(gr[:, :, sft:4], gr[:, :, sft:4], gc[:, :, 0:k], ALU.add))
                    link(v.tensor_tensor(gr[:, :, 0:k], gr[:, :, 0:k], gc[:, :, 0:k], ALU.subtract))
                    link(v.tensor_tensor(rc[:, :, :, 0:k], rs[:, :, :, 0:k], rs[:, :, :, sft:4], ALU.is_ge))
                    link(v.tensor_tensor(rk[:, :, :, sft:4], rk[:, :, :, sft:4], rc[:, :, :, 0:k], ALU.add))
                    link(v.tensor_tensor(rk[:, :, :, 0:k], rk[:, :, :, 0:k], rc[:, :, :, 0:k], ALU.subtract))
                first, second = r_pick[:, 0, 0:nt], r_pick[:, 1, 0:nt]
                fg = first.rearrange("p t (g e) -> p t g e", g=NG)
                link(v.tensor_scalar(gr, gr, 0.5, None, ALU.is_lt))
                in_group = gr.unsqueeze(3).broadcast_to([P, nt, NG, EPG])
                v.tensor_scalar(fg, rk, 0.5, None, ALU.is_lt)
                link(v.tensor_scalar(rk, rk, 1.5, None, ALU.is_lt))
                v.tensor_tensor(fg, fg, in_group, ALU.mult)
                v.tensor_tensor(rk, rk, in_group, ALU.mult).then_inc(picked, 1)
                dve.wait_ge(picked, l + 1)
                v.tensor_tensor(second, r_rank[:, 0:nt, :], first, ALU.subtract)
                link(v.tensor_tensor(r_sel[:, 0:nt, :], r_rank[:, 0:nt, :], r_sc[:, 0:nt, :], ALU.mult))
                link(v.tensor_reduce(r_sum[:, 0:nt], r_sel[:, 0:nt, :], AX_X, ALU.add))
                link(v.reciprocal(r_sum[:, 0:nt], r_sum[:, 0:nt]))
                link(v.tensor_tensor(gates[:, 0:nt, :], r_sel[:, 0:nt, :],
                                     r_sum[:, 0:nt].unsqueeze(2).broadcast_to([P, nt, NE]), ALU.mult))

                wait_ready(dve, "count", l)
                v.tensor_scalar(r_cnt[:, 0:(nt + 1) * NE], bank("count", l)[:, 0:(nt + 1) * NE], float(D_CONV), None,
                                ALU.mult).then_inc(drained_of("count", l), 1)
                wait_drained(dve, "count", l)
                total = r_cnt[:, nt * NE:(nt + 1) * NE]
                link(v.tensor_scalar(r_blk[:, 0, :], total, 0.0, None, ALU.is_gt))
                for j in range(1, nt * P // CAP):
                    link(v.scalar_tensor_tensor(r_blk[:, 0, :], total, float(j * CAP), r_blk[:, 0, :], ALU.is_gt, ALU.add))
                link(v.tensor_tensor_scan(r_blk[:, 1, :], ones_blk[:, :], r_blk[:, 0, :], 0.0, ALU.mult, ALU.add))
                link(v.tensor_tensor(r_blk[:, 2, :], r_blk[:, 1, :], r_blk[:, 0, :], ALU.subtract))
                link(v.tensor_scalar(r_blk[:, 2, :], r_blk[:, 2, :], float(CAP), None, ALU.mult))
                cnt = r_cnt[:, 0:nt * NE].rearrange("p (t e) -> p t e", t=nt)
                link(v.tensor_tensor(cnt, cnt, r_blk[:, 2:3, :].broadcast_to([P, nt, NE]), ALU.add))
                for c in range(2):
                    pick = r_pick[:, c, 0:nt]
                    v.tensor_tensor(r_cmp[:, 0:nt], pick, cnt, ALU.mult)
                    link(v.tensor_tensor(r_sel[:, 0:nt], pick, gates[:, 0:nt], ALU.mult))
                    v.tensor_reduce(r_slot[:, c, 0:nt], r_cmp[:, 0:nt], AX_X, ALU.add)
                    link(v.tensor_reduce(r_w[:, c, 0:nt], r_sel[:, 0:nt], AX_X, ALU.add))
                if l:
                    for t in range(TT):
                        dve.wait_ge(gathered[t], 32 * l)
                v.tensor_copy(slot_id[:, :, 0:nt], r_slot[:, :, 0:nt])
                link(v.tensor_tensor(r_cover[:, :, :], block_row[0:1, 0:24].unsqueeze(2).broadcast_to([1, 24, NE]),
                                     r_blk[0:1, 1:2, :].broadcast_to([1, 24, NE]), ALU.is_ge))
                link(v.tensor_reduce(r_expert[:, :], r_cover[:, :, :], AX_X, ALU.add))
                link(v.tensor_scalar(r_expert[:, :], r_expert[:, :], float(NE - 1), None, ALU.min))
                v.tensor_copy(expert_id[:, :], r_expert[:, :]).then_inc(counted, 1)

                def x_copy(b, u):
                    dve.wait_ge(blk_ready["x1"], b + (xblk_base[l] + 1))
                    v.tensor_copy(xT_blk[:, u, 4:8, :], psum[ROLE["x1"]][:, :].rearrange("p (k t) -> p k t", k=4))\
                        .then_inc(blk_drained["x1"], 1)

                def hidden(b, u):
                    dve.wait_ge(blk_drained["g"], b + (blk_base[l] + 1))
                    dve.wait_ge(blk_ready["u"], b + (blk_base[l] + 1))
                    v.tensor_tensor(hid_blk[:, u, :], psum[ROLE["u"]][:, :], silu_blk[:, u, :], ALU.mult)\
                        .then_inc(blk_drained["u"], 1)

                def hidden_copy(b, u):
                    dve.wait_ge(blk_ready["h"], b + (blk_base[l] + 1))
                    v.tensor_copy(hT_blk[:, u, :], psum[ROLE["h"]][:, :]).then_inc(blk_drained["h"], 1)

                def output(b, u, nth):
                    dve.wait_ge(blk_ready["d1"], b + (blk_base[l] + 1))
                    dve.wait_ge(y_stored[u], nth * 16 + 16 * stores_before(l, u))
                    v.tensor_copy(y_blk[:, u, 512:1024], psum[ROLE["d1"]][:, :]).then_inc(blk_drained["d1"], 1)

                nb = n_blocks[l]
                x_copy(0, 0)
                x_copy(1, 1)
                hidden(0, 0)
                with dve.Fori(0, (nb - 1) // 2) as i:
                    for first in (1, 2):
                        u = first % 2
                        x_copy(i * 2 + first + 1, 1 - u)
                        hidden_copy(i * 2 + first - 1, 1 - u)
                        hidden(i * 2 + first, u)
                        output(i * 2 + first - 1, 1 - u, i)
                hidden_copy(nb - 1, (nb - 1) % 2)
                output(nb - 1, (nb - 1) % 2, (nb - 1) // 2)

                for x in range(4):
                    wait_drained(dve, "g2", l, x)
                for t in range(nt):
                    dve.wait_ge(gathered[t], 32 * (l + 1))
                    link(v.tensor_scalar(y_first[:, t, :], y_first[:, t, :], r_w[:, 0, t:t + 1], None, ALU.mult))
                    link(v.scalar_tensor_tensor(y_first[:, t, :], y_second[:, t, :], r_w[:, 1, t:t + 1],
                                                y_first[:, t, :], ALU.mult, ALU.add))
                    link(v.tensor_tensor(y_first[:, t, :], y_first[:, t, :], g_rows[:, t // 2, :], ALU.mult))
                    link(v.scalar_tensor_tensor(H[:, t, :], H[:, t, :], ALPHA, y_first[:, t, :], ALU.mult, ALU.add))
                layer_norm(2 * l + 2, nt)


INPUTS = ["x", "c", "ctx", "c_ctx", "ln_in_g", "ln_in_b", "w_router", "b_router", "w_mod", "b_mod", "w_in", "conv_w",
          "conv_b", "conv_ln_g", "conv_ln_b", "w_a_out", "attn_sink", "w_b_out", "mlstm_gate_b", "mlstm_norm_g",
          "w_c_out", "w_out", "ln1_g", "ln1_b", "moe_w_gu", "moe_w_dn", "ln2_g", "ln2_b"]


def kernel(**inputs):
    import concourse.bacc as bacc
    from concourse.bass_utils import run_bass_kernel_spmd

    nc = bacc.Bacc("TRN2", target_bir_lowering=False, num_devices=1)
    arrays, aps = {}, {}
    host = {name: np.ascontiguousarray(inputs[name]) for name in INPUTS}
    host.update(host_constants())
    for name, value in host.items():
        arrays[f"in_{name}"] = value
        aps[name] = nc.dram_tensor(f"in_{name}", value.shape, mybir.dt.from_np(value.dtype), kind="ExternalInput").ap()
    out = nc.dram_tensor("out", (1, S_LAT, D), F32, kind="ExternalOutput").ap()
    build(nc, aps, out)
    result = run_bass_kernel_spmd(nc, [arrays], core_ids=[0])
    return result.results[0]["out"]
```

```python
from contextlib import ExitStack

import numpy as np

import concourse.bass as bass
from concourse import mybir

F32 = mybir.dt.float32
ALU = mybir.AluOpType
ACT = mybir.ActivationFunctionType
AX_X = mybir.AxisListType.X

P = 128
D = 1024
KD = D // P
DEPTH = 2
S_LAT, S_CTX = 256, 256
T = S_LAT + S_CTX
TT = T // P
D_CONV, TAPS = 512, 31
PAD = TAPS // 2
CT = D_CONV // P
NQ, NKV, DH = 8, 2, 64
NH, MH = 4, 128
WINDOW, GRID_W, ROPE_BASE = 128, 64, 10000.0
NE, NG, EPG, DE, TOP_K = 16, 4, 4, 512, 2
FT = DE // P
EPS = 1e-5
ALPHA = (2.0 * DEPTH) ** 0.25
A_SCALE = DH ** -0.5
K_SCALE = MH ** -0.5
NEG = -1e30
NS = 6
SLOT = KD * 256
BANKS = 8
CAP = P

C_A, C_Q, C_K, C_V = 0, 1024, 1536, 1664
C_MQ, C_MK, C_MV, C_MO, C_MG, C_BG = 1792, 2304, 2816, 3328, 3840, 3856
SH1, SC1, G1, SH2, SC2, G2 = 0, 8, 16, 24, 32, 40
N_MOD = 6 * KD

UNITS = [(h, d) for h in range(NH) for d in range(2)]


def token_tiles(layer):
    return TT if layer < DEPTH - 1 else S_LAT // P


def attention_units(layer):
    return [(qt, h) for qt in range(token_tiles(layer)) for h in range(NQ)]


def key_range(qt):
    return (0, T) if qt < S_LAT // P else (S_LAT, T)


MOD_FIRST = 8


PREP_STEP = 4
TOKENS_STEP = 7


def later_modulation(layer):
    if layer:
        return []
    rest = [(0, n) for n in range(MOD_FIRST, N_MOD // 2)] + [(1, n) for n in range(N_MOD // 2)]
    return [x for x in rest if x not in last_modulation(0)]


def last_modulation(layer):
    return [(1, n) for n in (8, 9, 10, 11, 20, 21)] if layer == 0 else []


def first_modulation():
    return [(0, n) for n in range(MOD_FIRST)]


def modulation_step(slots, s):
    before = slots[s - 1:s] if s else []
    return [("mod",) + x for x in slots[s:s + 1]] + [("modt",) + x for x in before]


def scan_ranges(s, d, n):
    lat, ctx = (0, 2 * P), None
    if s == 0:
        full = [(P, 2 * P)] if d == 0 else []
    elif s == 1:
        full = [] if d == 0 else [(0, P)]
    elif s == 2:
        full = [lat, (3 * P, 4 * P)] if d == 0 else [lat]
    else:
        full = [lat] if d == 0 else [lat, (2 * P, 3 * P)]
    return [r for r in full if r[1] <= n]


def scan_tiles(t, d):
    return [s for s in range(TT) if s == t or any(a <= t * P < b for a, b in scan_ranges(s, d, T))]


def joined(ranges):
    out = []
    for a, b in sorted(ranges):
        if out and out[-1][1] == a:
            out[-1] = (out[-1][0], b)
        else:
            out.append((a, b))
    return out


def blocks(layer):
    tokens = token_tiles(layer) * P
    return (TOP_K * tokens - NE) // CAP + NE


NORM_TILES = [TT] + [token_tiles(l) for l in range(DEPTH) for which in range(2)]


def norm_halves(w):
    return sum(NORM_TILES[:w]) // 2


def on_scalar(which, h, k, tiles):
    if tiles == 2:
        return k % 2 == 1
    return h == 0 or (which == 0 and k == KD // 2 - 1)


def psum_order():
    order = [("c",)]
    for s in range(MOD_FIRST + 1):
        order += [("prep",)] if s == PREP_STEP else []
        order += [("tr1", 0, 0, k) for k in range(KD // 2)] if s == TOKENS_STEP else []
        order += modulation_step(first_modulation(), s)
    for l in range(DEPTH):
        nt = token_tiles(l)
        later = later_modulation(l)
        order += [("tr1", l, h, k) for h in range(1 if l == 0 else 0, TT // 2) for k in range(KD // 2)]
        for j in range(CT):
            order += [("val", l, j), ("gate", l, j)]
        order += [("v", l), ("ig", l)]
        order += [("qk", l, t) for t in (4, 5, 0, 1, 2, 3)]
        order += [("perm", l, t) for t in range(6)]
        order += [("mqk", l, t) for t in range(8)]
        order += [("mv", l, c, h) for c in range(2) for h in range(TT // 2)]
        order += [("mean", l)]
        order += [("mo", l, 0, h) for h in range(nt // 2)]
        order += [("var", l)]
        order += [("S", l, 0), ("S", l, 1)]
        order += [("mo", l, 1, h) for h in range(nt // 2)]
        n = len(attention_units(l))
        for i in range(n + 3):
            order += [("S", l, i)] if 2 <= i < n else []
            order += [("PT", l, i - 2)] if 0 <= i - 2 < n else []
            order += [("PV", l, i - 3)] if 0 <= i - 3 < n else []
            order += modulation_step(later, i) if i < n else []
        order += [("yb_rows", l, t) for t in range(nt)]
        order += [("cols", l)]
        n_first, n = n, len(UNITS)
        for i in range(n + 2):
            order += [("bm", l, i)] if i < n else []
            order += [("hv", l, i - 2, t) for t in range(nt // 2)] if 0 <= i - 2 < n else []
            order += [("st", l, i - 1, s) for s in range(TT)] if 0 <= i - 1 < n else []
            order += modulation_step(later, n_first + i)
        order += [("bga", l, 0), ("bgb", l, 0), ("bgc", l, 0)]
        order += [("yc", l, h) for h in range(NH)]
        for j in range(KD):
            order += [(b, l, j) for b in ("bga", "bgb", "bgc")] if j else []
            order += [(b, l, j) for b in ("ya", "yb", "yc_")]
        order += [("g1", l, c) for c in range(nt)]
        order += [("out", l, c, h) for h in range(nt // 2) for c in range(4)]
        for h in range(nt // 2):
            order += [("tr2", l, h, k) for k in range(KD // 2)]
            order += [("router", l, h)]
            order += [("scores", l)] if h == nt // 2 - 1 else []
            order += [("nat", l, t, c) for t in (2 * h, 2 * h + 1) for c in range(2)]
        order += [("g2", l, c) for c in range(nt)]
        order += [("count", l)]
        last = last_modulation(l)
        for i in range(len(last) + 1 if last else 0):
            order += modulation_step(last, i)
    return order, {key: (n % BANKS, n // BANKS) for n, key in enumerate(order)}


def host_constants():
    nf = DH // 4
    inv = ROPE_BASE ** (-np.arange(nf, dtype=np.float32) / np.float32(nf))
    pos = np.arange(S_LAT)
    row, col = pos // GRID_W, pos % GRID_W
    d = np.arange(P) % DH
    ang = np.where((d < DH // 2)[:, None], row[None, :], col[None, :]).astype(np.float32) * inv[d % nf][:, None]
    second = (d % (2 * nf)) >= nf
    cos, sin = np.cos(ang), np.where(second[:, None], np.sin(ang), -np.sin(ang))
    partner = np.arange(P) + np.where(second, -nf, nf)
    perm = np.zeros((P, P), np.float32)
    perm[partner, np.arange(P)] = 1.0
    q = np.arange(S_LAT).reshape(2, P, 1)
    k = np.arange(T).reshape(1, 1, T)
    band = np.where((np.abs(q - k) <= WINDOW) | (k >= S_LAT), 0.0, NEG).astype(np.float32).transpose(1, 0, 2)
    s, t = np.arange(P)[:, None], np.arange(P)[None, :]
    tri = np.stack([np.where(s <= t, 0.0, NEG), np.where(s >= t, 0.0, NEG)], 1).astype(np.float32)
    return {
        "k_ident": np.eye(P, dtype=np.float32),
        "k_perm": perm,
        "k_select": (np.arange(P)[:, None] % 32 == np.arange(NE)[None, :]).astype(np.float32),
        "k_before": ((s < t) / np.float32(D_CONV)).astype(np.float32),
        "k_blocks": np.arange(32, dtype=np.float32).reshape(1, 32),
        "k_rope": np.stack([cos, sin], 1).astype(np.float32),
        "k_band": np.ascontiguousarray(band),
        "k_tri": np.ascontiguousarray(tri),
    }


def build(nc, a, out):
    order, place = psum_order()

    with ExitStack() as ctx:
        def sb(name, shape):
            return ctx.enter_context(nc.sbuf_tensor(name, shape, F32))

        H = sb("H", [P, TT, D])
        uT = sb("uT", [P, KD, T])
        ring = sb("ring", [P, NS, SLOT])
        arena = sb("arena", [P, KD, T])
        upad = sb("upad", [P, CT, 2, S_LAT + 2 * PAD])
        convT = sb("convT", [P, CT, T])
        qkT = sb("qkT", [P, 6, T])
        v_tok = sb("v_tok", [P, TT, NKV * DH])
        mqk = sb("mqk", [P, 8, T])
        mv_tok = sb("mv_tok", [P, TT, NH, MH + 1])
        mo_tok = sb("mo_tok", [P, TT, NH, MH])
        yab = sb("yab", [P, 8, T])
        wgate = sb("wgate", [P, KD, P])
        wrouter = sb("wrouter", [P, KD, 32])
        ident = sb("ident", [P, P])
        perm = sb("perm", [P, P])
        before = sb("before", [P, P])
        block_row = sb("block_row", [1, 32])
        rope = sb("rope", [P, 2, S_LAT])
        band = sb("band", [P, 2, T])
        tri = sb("tri", [P, 2, P])
        ones_mean = sb("ones_mean", [P, P])
        smallT = sb("smallT", [P, DEPTH, N_MOD + 12])
        cT = sb("cT", [P, KD, 32])
        select = sb("select", [P, NE])
        lnT = sb("lnT", [P, 2 * DEPTH, 2, KD])
        fold = sb("fold", [P, 2 * DEPTH, 2, KD, 2])
        cwT = sb("cwT", [P, DEPTH, CT, TAPS])
        modT = sb("modT", [P, DEPTH, N_MOD, 2])
        gate_bias = sb("gate_bias", [P, DEPTH])
        sink = sb("sink", [P, DEPTH, NQ])
        norm_g = sb("norm_g", [P, DEPTH, NH * MH])
        b_router = sb("b_router", [P, NE])
        negM_tok = sb("negM_tok", [64, T])
        gate_cols = sb("gate_cols", [P, 8, 64])
        eps = sb("eps", [P, 1])
        ones_row = sb("ones_row", [64, T])
        ones_blk = sb("ones_blk", [P, NE])
        st = sb("st", [P, TT, 12])
        mv = sb("mv", [P, TT, 2])
        sd = sb("sd", [P, TT])
        rstd = sb("rstd", [P, TT])
        a_max = sb("a_max", [P, 3, 2])
        a_sum = sb("a_sum", [P, 3, 4])
        a_rden = sb("a_rden", [P, 4, 1])
        den = sb("den", [P, 3, 2])
        hstat = sb("hstat", [P, 4, TT * NH])
        r_sc = sb("r_sc", [P, TT, NE])
        r_sel = sb("r_sel", [P, TT, NE])
        r_rank = sb("r_rank", [P, TT, NE])
        r_cmp = sb("r_cmp", [P, TT, NE])
        r_hi = sb("r_hi", [P, TT, NG, 4])
        r_gs = sb("r_gs", [P, TT, NG])
        r_grank = sb("r_grank", [P, TT, NG])
        r_gcmp = sb("r_gcmp", [P, TT, NG])
        r_sum = sb("r_sum", [P, TT])
        gates = sb("gates", [P, TT, NE])
        r_pick = sb("r_pick", [P, 2, TT, NE])
        r_cnt = sb("r_cnt", [P, (TT + 1) * NE])
        r_blk = sb("r_blk", [P, 4, NE])
        r_slot = sb("r_slot", [P, 2, TT])
        r_w = sb("r_w", [P, 2, TT])
        r_expert = sb("r_expert", [1, 24])
        slot_id = ctx.enter_context(nc.sbuf_tensor("slot_id", [P, 2, TT], mybir.dt.uint32))
        expert_id = ctx.enter_context(nc.sbuf_tensor("expert_id", [1, 24], mybir.dt.int32))
        n_blocks = [blocks(l) for l in range(DEPTH)]
        xs = nc.dram_tensor("xs", [(n_blocks[0] + 2) * CAP, D], F32).ap()
        ys = nc.dram_tensor("ys", [n_blocks[0] * CAP, D], F32).ap()

        cw_rows = arena[0:TAPS, 0:DEPTH, :]
        small_rows = arena[0:N_MOD + 12, 2, 0:DEPTH * P].rearrange("r (l c) -> r l c", l=DEPTH)
        c_rows = arena[0:16, 3, 0:P]
        norm_rows = arena[0:32 * DEPTH, 4, 0:P]
        flat = arena[:, :, :].rearrange("p a b -> p (a b)")
        sq = flat[:, 0:CT * T].rearrange("p (a b) -> p a b", a=CT)
        grow = arena
        s_buf = arena
        w_buf = arena
        merged = arena
        u_nat = flat.rearrange("p (a b) -> p a b", a=TT)
        y_first = u_nat
        y_second = yab[:, :, :].rearrange("p a b -> p (a b)").rearrange("p (a b) -> p a b", a=TT)
        x_blk = convT[:, :, :].rearrange("p a b -> p (a b)").rearrange("p (u d) -> p u d", u=2)
        xT_blk = mo_tok[:, :, :, :].rearrange("p a b c -> p (a b c)").rearrange("p (u k t) -> p u k t", u=2, k=KD)
        y_blk = qkT[:, 0:4, :].rearrange("p a b -> p (a b)").rearrange("p (u d) -> p u d", u=2)
        silu_blk, hid_blk, hT_blk = mqk[:, 0:2, :], mqk[:, 2:4, :], mqk[:, 4:6, :]
        zeros = yab[:, 0:2, :].rearrange("p a b -> p (a b)")
        ln_rows = mo_tok[:, :, :, :].rearrange("p a b c -> p (a b c)")
        ln_g, ln_b = ln_rows[:, 0:D], ln_rows[:, D:2 * D]
        g_rows = [qkT[:, 4:6, :].rearrange("p a b -> p (a b)"),
                  upad[:, :, :, :].rearrange("p a b c -> p (a b c)")[:, 0:D]]
        tri_buf = upad[:, :, :, :].rearrange("p a b c -> p (a b c)")[:, 0:2 * TT * P]\
            .rearrange("p (u s t) -> p u s t", u=2, s=TT)
        r_cover = negM_tok[0:1, 0:24 * NE].rearrange("p (b e) -> p b e", b=24)
        mod_rows = upad[:, :, :, :].rearrange("p a b c -> p (a b c)")[:, 2 * TT * P:2 * TT * P + 512]\
            .rearrange("p (u n) -> p u n", u=2)
        router_rows = upad[:, :, :, :].rearrange("p a b c -> p (a b c)")[:, 2 * TT * P:2 * TT * P + T]
        hacc = convT[:, :, :].rearrange("p t (h d) -> p t h d", h=NH)
        hsq = arena[:, 0:TT, :].rearrange("p t (h d) -> p t h d", h=NH)
        yc = qkT
        sig = mqk
        psum = [ctx.enter_context(nc.psum_tensor(f"psum{b}", [P, 512], F32)) for b in range(BANKS)]

        def sem(name):
            return ctx.enter_context(nc.semaphore(name))

        ready = [sem(f"psum_ready{b}") for b in range(BANKS)]
        drained = [sem(f"psum_drained{b}") for b in range(BANKS)]
        loaded = [sem(f"slot_loaded{s}") for s in range(NS)]
        k_copy_loaded = sem("k_copy_loaded")
        c_rows_loaded, rows_loaded = sem("c_rows_loaded"), sem("small_rows_loaded")
        setup_loaded = sem("setup_loaded")
        folded = sem("norm_and_modulation_folded")
        rows_used = sem("ln_rows_used")
        first_scaled = sem("first_choice_scaled")
        x_loaded = [sem(f"x_loaded{h}") for h in range(2)]
        ln_loaded = sem("ln_rows_loaded")
        wgate_loaded = sem("wgate_loaded")
        wgate_cleared = sem("wgate_cleared")
        consts_set = sem("consts_set")
        c_ready = sem("c_ready")
        h_ready = sem("h_ready")
        ln_var, ln_std = sem("ln_var"), sem("ln_std")
        conv_ready, sq_ready, scaled_ready, ya_ready = (sem("conv_ready"), sem("conv_squares"), sem("conv_scaled"),
                                                        sem("ya_ready"))
        rope_ready = sem("rope_ready")
        yb_done = sem("attention_done")
        gate_x, gate_l, gate_m, gate_em = sem("gate_negabs"), sem("gate_softplus"), sem("gate_m"), sem("gate_exp_m")
        s_ready, p_exp, p_ready = sem("scores_ready"), sem("probs_exp"), sem("probs_ready")
        tri_ready = sem("tri_ready")
        hc_ready, hsq_ready, hvar, hstd, hn_ready = (sem("head_centered"), sem("head_squares"), sem("head_var"),
                                                     sem("head_std"), sem("head_normed"))
        merged_ready = sem("merged_ready")
        out_gates_ready = sem("output_gates_ready")
        ROLE = {"x0": 0, "x1": 1, "g": 2, "h": 3, "u": 4, "d0": 5, "d1": 6}
        blk_ready = {r: sem(f"block_{r}_ready") for r in ROLE}
        blk_drained = {r: sem(f"block_{r}_drained") for r in ROLE}
        x_blk_loaded = [sem(f"block_tokens_loaded{u}") for u in range(2)]
        y_stored = [sem(f"block_output_stored{u}") for u in range(2)]
        picked, counted = sem("choices_ready"), sem("slots_ready")
        scattered = sem("tokens_scattered")
        gathered = [sem(f"outputs_gathered{t}") for t in range(TT)]
        zeros_set = sem("zeros_set")
        dve_chain, act_chain, out_sent = sem("dve_chain"), sem("act_chain"), sem("out_sent")

        def bank(*key):
            return psum[place[key][0]]

        def wait_ready(eng, *key):
            eng.wait_ge(ready[place[key][0]], place[key][1] + 1)

        def wait_bank(pe, *key):
            if place[key][1] > 0:
                pe.wait_ge(drained[place[key][0]], place[key][1])

        def wait_drained(eng, *key):
            eng.wait_ge(drained[place[key][0]], place[key][1] + 1)

        def ready_of(*key):
            return ready[place[key][0]]

        def drained_of(*key):
            return drained[place[key][0]]

        blk_base = [sum(n_blocks[:l]) for l in range(DEPTH)]
        xblk_base = [sum(n_blocks[:l]) + l for l in range(DEPTH)]

        def loads_before(l, u):
            return sum((n + 3 - u) // 2 for n in n_blocks[:l])

        def stores_before(l, u):
            return 1 + sum((n + 1 - u) // 2 for n in n_blocks[:l])

        win = [a["w_in"][l].rearrange("(k p) n -> p k n", p=P) for l in range(DEPTH)]
        wmod = [a["w_mod"][l].rearrange("(k p) n -> p k n", p=P) for l in range(DEPTH)]
        wout = [a["w_out"][l].rearrange("(k p) n -> p k n", p=P) for l in range(DEPTH)]
        wbr = [[a[n][l].rearrange("(k p) n -> p k n", p=P) for n in ("w_a_out", "w_b_out", "w_c_out")]
               for l in range(DEPTH)]

        def slot8(s):
            return ring[:, s, :].rearrange("p (k n) -> p k n", k=KD)

        def slot4(s):
            return ring[:, s, :].rearrange("p (k n) -> p k n", k=FT)

        stream = []
        for l in range(DEPTH):
            nt = token_tiles(l)

            def used(key, last):
                stream.append((key, ready_of(*last), place[last][1] + 1))
            for n in range(MOD_FIRST if l == 0 else 0):
                used(("mod", l, n), ("mod", l, n))
            for j in range(CT):
                used(("a", l, j), ("gate", l, j))
            used(("v", l), ("v", l))
            used(("kk", l), ("qk", l, 5))
            for c in range(2):
                used(("q", l, c), ("qk", l, 2 * c + 1))
            for c in range(4):
                used(("mqk", l, c), ("mqk", l, 2 * c + 1))
            for c in range(2):
                used(("mv", l, c), ("mv", l, c, TT // 2 - 1))
            for c in range(2):
                used(("mo", l, c), ("mo", l, c, nt // 2 - 1))
            for x in later_modulation(l):
                used(("mod",) + x, ("mod",) + x)
            for j in range(KD // 2):
                last = 2 * j + 1
                used(("bga", l, j), ("bga", l, last))
                used(("bgb", l, j), ("bgb", l, last))
                used(("bgc", l, j), ("bgc", l, last))
                used(("yab", l, j), ("yb", l, last))
                used(("yc", l, j), ("yc_", l, last))
            for c in range(4):
                used(("out", l, c), ("out", l, c, nt // 2 - 1))
            for x in last_modulation(l):
                used(("mod",) + x, ("mod",) + x)
            nb = n_blocks[l]
            for b in range(nb + 1):
                if b < nb:
                    for x in ("g0", "g1", "u0", "u1"):
                        stream.append((("moe", l, b, x), blk_ready[x[0]], blk_base[l] + b + 1))
                if b > 0:
                    for x in ("d0", "d1"):
                        stream.append((("moe", l, b, x), blk_ready[x], blk_base[l] + b))
        index = {key: n for n, (key, _, _) in enumerate(stream)}

        def slot_of(*key):
            return index[key] % NS

        def wait_slot(eng, *key):
            eng.wait_ge(loaded[index[key] % NS], 32 * (index[key] // NS + 1))

        block = ctx.enter_context(nc.Block())

        setup, small, first_small = [], [], []

        def row_pairs():
            first_small.append((ident[:, :], a["k_ident"]))
            first_small.append((c_rows[0:8, :], a["c"][0].rearrange("(r c) -> r c", c=P)))
            first_small.append((c_rows[8:16, :], a["c_ctx"].rearrange("(r c) -> r c", c=P)))
            first_small.append((select[:, :], a["k_select"]))
            small.append((small_rows[0:N_MOD, :, :], a["b_mod"].rearrange("l (r c) -> r l c", c=P)))
            for i, n in enumerate(("conv_b", "conv_ln_g", "conv_ln_b")):
                small.append((small_rows[N_MOD + 4 * i:N_MOD + 4 * i + 4, :, :],
                              a[n].rearrange("l (r c) -> r l c", c=P)))
            small.append((cw_rows[:, :, :], a["conv_w"].rearrange("l w c -> w l c")))
            for w in range(2 * DEPTH):
                g, b = ("ln_in_g", "ln_in_b") if w == 0 else (("ln2_g", "ln1_g")[w % 2], ("ln2_b", "ln1_b")[w % 2])
                for i, x in enumerate((g, b)):
                    src = a[x] if w == 0 else a[x][(w - 1) // 2]
                    small.append((norm_rows[16 * w + 8 * i:16 * w + 8 * i + 8, :], src.rearrange("(r c) -> r c", c=P)))
            setup.append((perm[:, :], a["k_perm"]))
            setup.append((rope[:, :, :], a["k_rope"]))
            setup.append((before[:, :], a["k_before"]))
            setup.append((block_row[:, :], a["k_blocks"]))
            setup.append((band[:, :, :], a["k_band"]))
            setup.append((tri[:, :, :], a["k_tri"]))
            setup.append((wrouter[:, :, 0:NE], a["w_router"].rearrange("(k p) n -> p k n", p=P)))
            setup.append((b_router[:, :], a["b_router"].partition_broadcast(P)))
            for l in range(DEPTH):
                setup.append((sink[:, l, :], a["attn_sink"][l].partition_broadcast(P)))
                setup.append((norm_g[:, l, :], a["mlstm_norm_g"][l].partition_broadcast(P)))
                for typ in range(2):
                    for d in range(2):
                        r = 64 * typ + 32 * d
                        setup.append((gate_bias[r:r + NH, l:l + 1],
                                      a["mlstm_gate_b"][l, d, typ].rearrange("(h o) -> h o", o=1)))
        row_pairs()
        SETUP, SMALL, FIRST_SMALL = 16 * len(setup), 16 * len(small), 16 * len(first_small)

        @block.sync
        def _(sp):
            def load(key, offset=None):
                s = index[key] % NS
                w8, w4 = slot8(s), slot4(s)
                kind, l = key[0], key[1]
                if kind == "mod":
                    n = key[2]
                    src = wmod[l][:, :, bass.ds(n * 256, 256)]
                    pairs = [(w8[:, 0:4, :], src[:, 0:4, :]), (w8[:, 4:8, :], src[:, 4:8, :])]
                elif kind == "a":
                    j = key[2]
                    pairs = [(w8[:, :, g * P:(g + 1) * P],
                              win[l][:, :, C_A + g * D_CONV + j * P:C_A + g * D_CONV + (j + 1) * P]) for g in range(2)]
                elif kind == "v":
                    pairs = [(w8[:, 4 * g:4 * g + 4, 0:P], win[l][:, 4 * g:4 * g + 4, C_V:C_V + P]) for g in range(2)]
                elif kind == "kk":
                    copies = [(w8[:, :, (2 * g + r) * DH:(2 * g + r + 1) * DH],
                               win[l][:, :, C_K + g * DH:C_K + (g + 1) * DH]) for r in range(2) for g in range(NKV)]
                    pairs = copies[0:2]
                    for dst, src in copies[2:4]:
                        sp.dma_start(dst, src).then_inc(k_copy_loaded, 16)
                elif kind in ("q", "mqk", "mv", "mo"):
                    c0 = {"q": C_Q, "mqk": C_MQ, "mv": C_MV, "mo": C_MO}[kind] + 256 * key[2]
                    pairs = [(w8[:, 4 * g:4 * g + 4, :], win[l][:, 4 * g:4 * g + 4, c0:c0 + 256]) for g in range(2)]
                elif kind in ("bga", "bgb", "bgc"):
                    c0 = C_BG + "abc".index(kind[2]) * D + 256 * key[2]
                    pairs = [(w8[:, 4 * g:4 * g + 4, :], win[l][:, 4 * g:4 * g + 4, c0:c0 + 256]) for g in range(2)]
                elif kind == "yab":
                    c = slice(256 * key[2], 256 * key[2] + 256)
                    pairs = [(w8[:, 4 * g:4 * g + 4, :], wbr[l][g][:, :, c]) for g in range(2)]
                elif kind == "yc":
                    c = slice(256 * key[2], 256 * key[2] + 256)
                    pairs = [(w8[:, 2 * g:2 * g + 2, :], wbr[l][2][:, 2 * g:2 * g + 2, c]) for g in range(2)]
                elif kind == "out":
                    c = slice(256 * key[2], 256 * key[2] + 256)
                    pairs = [(w8[:, 4 * g:4 * g + 4, :], wout[l][:, 4 * g:4 * g + 4, c]) for g in range(2)]
                else:
                    e, x = offset, key[3]
                    half = int(x[1])
                    if x[0] == "d":
                        src = a["moe_w_dn"][l, e].rearrange("(k p) n -> p k n", p=P)[:, :, half * 512:half * 512 + 512]
                    else:
                        c = "gu".index(x[0]) * DE
                        src = a["moe_w_gu"][l, e].rearrange("(k p) n -> p k n", p=P)[:, 4 * half:4 * half + 4, c:c + DE]
                    pairs = [(w4[:, 2 * g:2 * g + 2, :], src[:, 2 * g:2 * g + 2, :]) for g in range(2)]
                for dst, src in pairs:
                    sp.dma_start(dst, src).then_inc(loaded[s], 16)

            def load_when_free(key, offset=None):
                n = index[key]
                if n >= NS:
                    sp.wait_ge(stream[n - NS][1], stream[n - NS][2])
                load(key, offset)

            def load_tokens(l, b, u):
                sp.dma_start(x_blk[:, u, :], xs[bass.ds(b * CAP, CAP), :]).then_inc(x_blk_loaded[u], 16)

            def expert(b):
                return sp.value_load(expert_id[0:1, bass.ds(b, 1)], min_val=0, max_val=NE - 1)

            for dst, src in first_small:
                sp.dma_start(dst, src).then_inc(c_rows_loaded, 16)
            keys = [key for key, _, _ in stream]
            at = 0
            while at < len(keys):
                key = keys[at]
                l = key[1]
                if key[0] == "moe":
                    nb = n_blocks[l]
                    base = index[("moe", l, 0, "g0")]
                    sp.wait_ge(counted, l + 1)
                    e = expert(0)
                    for x in ("g0", "g1"):
                        load_when_free(("moe", l, 0, x), e)
                    sp.wait_ge(scattered, 16 * sum(2 * token_tiles(x) for x in range(l + 1)))
                    load_tokens(l, 0, 0)
                    for x in ("u0", "u1"):
                        load_when_free(("moe", l, 0, x), e)
                    load_tokens(l, 1, 1)
                    sp.wait_ge(blk_ready["x1"], xblk_base[l] + 1)
                    load_tokens(l, 2, 0)

                    def weights_and_tokens(b, first, i):
                        e, e_before = expert(b), expert(b - 1)
                        for x in ("g0", "g1", "u0", "u1", "d0", "d1"):
                            k = ("moe", l, first, x)
                            _, free, value = stream[index[k] + (0 if i is None else 12) - NS]
                            sp.wait_ge(free, value if i is None else (i - 1) * 2 + value)
                            load(k, e_before if x[0] == "d" else e)
                        sp.wait_ge(blk_ready["x1"], b + (xblk_base[l] + 1))
                        load_tokens(l, b + 2, first % 2)

                    for first in (1, 2):
                        weights_and_tokens(first, first, None)
                    with sp.Fori(1, (nb - 1) // 2) as i:
                        for first in (1, 2):
                            weights_and_tokens(i * 2 + first, first, i)
                    e = expert(nb - 1)
                    for x in ("d0", "d1"):
                        load_when_free(("moe", l, nb, x), e)
                    at += 6 * nb
                else:
                    load_when_free(key)
                    at += 1
            sp.wait_ge(h_ready, sum(NORM_TILES))
            sp.dma_start(out.rearrange("b (t p) d -> p (b t) d", p=P), H[:, 0:2, :]).then_inc(out_sent, 16)
            sp.wait_ge(out_sent, 16)
            for u in range(2):
                sp.wait_ge(x_blk_loaded[u], 16 * loads_before(DEPTH, u))

        @block.gpsimd
        def _(pool):
            def load_norm_rows(w):
                pool.wait_ge(rows_used, w)
                for x, dst in (("g", ln_g), ("b", ln_b)):
                    pool.dma_start(dst, a[f"ln{2 - w % 2}_{x}"][(w - 1) // 2].partition_broadcast(P))\
                        .then_inc(ln_loaded, 16)

            def route_and_combine(l):
                nt, nb = token_tiles(l), n_blocks[l]
                pool.wait_ge(counted, l + 1)
                for t in range(nt):
                    for h in range(2):
                        wait_drained(pool, "nat", l, t, h)
                for u in range(2):
                    pool.wait_ge(y_stored[u], 16 * stores_before(l, u))
                    if l:
                        pool.wait_ge(x_blk_loaded[u], 16 * loads_before(l, u))
                for t in range(nt):
                    for c in range(2):
                        pool.indirect_dma_start(xs, bass.IndirectOffsetOnAxis(slot_id[:, c, t:t + 1], 0),
                                                u_nat[:, t, :], None).then_inc(scattered, 16)

                def store(b, u):
                    for r in ("d0", "d1"):
                        pool.wait_ge(blk_drained[r], b + (blk_base[l] + 1))
                    pool.dma_start(ys[bass.ds(b * CAP, CAP), :], y_blk[:, u, :]).then_inc(y_stored[u], 16)

                with pool.Fori(0, (nb - 1) // 2) as i:
                    for u in range(2):
                        store(i * 2 + u, u)
                store(nb - 1, (nb - 1) % 2)
                pool.wait_ge(scattered, 16 * sum(2 * token_tiles(x) for x in range(l + 1)))
                for u in range(2):
                    pool.wait_ge(y_stored[u], 16 * stores_before(l + 1, u))
                for t in range(nt):
                    for c, dst in enumerate((y_first, y_second)):
                        pool.indirect_dma_start(dst[:, t, :], None, ys,
                                                bass.IndirectOffsetOnAxis(slot_id[:, c, t:t + 1], 0))\
                            .then_inc(gathered[t], 16)
                for r, count in (("x0", xblk_base[l] + nb + 1), ("x1", xblk_base[l] + nb + 1)):
                    pool.wait_ge(blk_drained[r], count)
                pool.wait_ge(blk_ready["u"], blk_base[l] + nb)
                load_norm_rows(2 * l + 2)
                for t in range(nt):
                    pool.wait_ge(gathered[t], 32 * (l + 1))

            for tile, (name, n) in enumerate((("x", S_LAT // P), ("ctx", S_CTX // P))):
                pool.dma_start(H[:, 2 * tile:2 * tile + 2, :],
                               a[name].rearrange("b (t p) d -> p (b t) d", p=P)).then_inc(x_loaded[tile], 16)
            wait_ready(pool, "gate", 0, 0)
            pool.dma_start(ln_g, a["ln_in_g"].partition_broadcast(P)).then_inc(ln_loaded, 16)
            pool.dma_start(ln_b, a["ln_in_b"].partition_broadcast(P)).then_inc(ln_loaded, 16)
            pool.wait_ge(consts_set, 1)
            for dst, src in setup:
                pool.dma_start(dst, src).then_inc(setup_loaded, 16)
            for l in range(DEPTH):
                if l:
                    wait_ready(pool, "ig", l - 1)
                else:
                    pool.wait_ge(wgate_cleared, 1)
                for typ in range(2):
                    for d in range(2):
                        c = C_MG + 8 * d + 4 * typ
                        r = 64 * typ + 32 * d
                        pool.dma_start(wgate[:, :, r:r + NH], win[l][:, :, c:c + NH]).then_inc(wgate_loaded, 16)
                if l == 0:
                    wait_ready(pool, "v", 0)
                    pool.wait_ge(zeros_set, 1)
                    rows = xs.rearrange("(b p) d -> p b d", p=P)
                    nb = n_blocks[0] + 2
                    for u, (b0, b1) in enumerate(((0, nb // 2), (nb // 2, nb))):
                        pool.dma_start(rows[:, b0:b1, :], zeros.unsqueeze(1).broadcast_to([P, b1 - b0, D]))\
                            .then_inc(y_stored[u], 16)
                pool.wait_ge(hn_ready, l + 1)
                load_norm_rows(2 * l + 1)
                route_and_combine(l)
            pool.wait_ge(ln_loaded, 32 * (1 + 2 * DEPTH))
            for h in range(2):
                pool.wait_ge(x_loaded[h], 16)
            pool.wait_ge(wgate_loaded, 64 * DEPTH)
            pool.wait_ge(setup_loaded, SETUP)

        u_base = lambda l, which: 4 * (2 * l + which)
        n_att = [0, len(attention_units(0)), len(attention_units(0)) + len(attention_units(1))]

        @block.tensor
        def _(pe):
            def mm(dst, lhsT, rhs, start=True, stop=True):
                return nc.tensor.matmul(dst, lhsT, rhs, start=start, stop=stop)

            def done(ins, *key):
                ins.then_inc(ready_of(*key), 1)

            pe.wait_ge(c_rows_loaded, FIRST_SMALL)
            done(nc.tensor.transpose(bank("c")[:, 0:16], c_rows, ident[0:16, 0:16]), "c")

            def small_rows_to_columns():
                pe.wait_ge(rows_loaded, SMALL)
                wait_bank(pe, "prep")
                prep = bank("prep")
                n_small = N_MOD + 12
                for l in range(DEPTH):
                    nc.tensor.transpose(prep[:, l * n_small:(l + 1) * n_small], small_rows[:, l, :],
                                        ident[0:n_small, 0:n_small])
                for l in range(DEPTH):
                    for j in range(CT):
                        o = 136 + (l * CT + j) * TAPS
                        nc.tensor.transpose(prep[:, o:o + TAPS], cw_rows[:, l, j * P:(j + 1) * P], ident[0:TAPS, 0:TAPS])
                done(nc.tensor.transpose(prep[:, 384:384 + 32 * DEPTH], norm_rows, ident[0:32 * DEPTH, 0:32 * DEPTH]),
                     "prep")

            for l in range(DEPTH):
                nt = token_tiles(l)
                n = nt * P

                def modulation(slots, s):
                    if s < len(slots):
                        x = slots[s]
                        wait_slot(pe, "mod", *x)
                        wait_bank(pe, "mod", *x)
                        w = slot8(slot_of("mod", *x))
                        for k in range(KD):
                            q = 32 * (k % 4)
                            last = mm(bank("mod", *x)[q:q + 32, 0:256], cT[:, k, :], w[:, k, :], k < 4, k >= 4)
                        done(last, "mod", *x)
                    if 1 <= s <= len(slots):
                        x = slots[s - 1]
                        wait_drained(pe, "mod", *x)
                        wait_bank(pe, "modt", *x)
                        for half in range(2):
                            last = mm(bank("modt", *x)[:, 2 * half:2 * half + 2],
                                      mod_rows[:, x[1] % 2, half * P:(half + 1) * P], select[:, 0:2])
                        done(last, "modt", *x)

                later = later_modulation(l)

                def transposes(which, h):
                    pe.wait_ge(h_ready, 2 * (norm_halves(2 * l + which) + h + 1))
                    for k in range(KD // 2):
                        key = ("tr2" if which else "tr1", l, h, k)
                        wait_bank(pe, *key)
                        for i in range(4):
                            t, c = 2 * h + i % 2, 2 * k + i // 2
                            last = nc.tensor.transpose(bank(*key)[:, i * P:(i + 1) * P], H[:, t, c * P:(c + 1) * P],
                                                       ident[:, :])
                        done(last, *key)

                if l == 0:
                    pe.wait_ge(c_ready, 1)
                    for s in range(MOD_FIRST + 1):
                        if s == PREP_STEP:
                            small_rows_to_columns()
                        if s == TOKENS_STEP:
                            transposes(0, 0)
                        modulation(first_modulation(), s)
                for h in range(1 if l == 0 else 0, TT // 2):
                    transposes(0, h)
                for h in range(TT // 2):
                    for k in range(KD // 2):
                        wait_drained(pe, "tr1", l, h, k)

                def by_channel(w, cols, width, *key):
                    wait_bank(pe, *key)
                    for k in range(KD):
                        last = mm(bank(*key)[:, 0:width], w[:, k, cols:cols + P], uT[:, k, 0:width], k == 0, k == KD - 1)
                    done(last, *key)

                for j in range(CT):
                    wait_slot(pe, "a", l, j)
                    w = slot8(slot_of("a", l, j))
                    by_channel(w, 0, n, "val", l, j)
                    by_channel(w, P, n, "gate", l, j)
                wait_slot(pe, "v", l)
                w = slot8(slot_of("v", l))
                wait_bank(pe, "v", l)
                for t in range(TT):
                    for k in range(KD):
                        last = mm(bank("v", l)[:, t * P:(t + 1) * P], uT[:, k, t * P:(t + 1) * P], w[:, k, 0:P],
                                  k == 0, k == KD - 1)
                done(last, "v", l)
                pe.wait_ge(setup_loaded, SETUP)
                pe.wait_ge(wgate_loaded, 64 * (l + 1))
                by_channel(wgate, 0, T, "ig", l)
                wait_slot(pe, "kk", l)
                pe.wait_ge(k_copy_loaded, 32 * (l + 1))
                for g in range(NKV):
                    by_channel(slot8(slot_of("kk", l)), g * P, T, "qk", l, 4 + g)
                for c in range(2):
                    wait_slot(pe, "q", l, c)
                    for g in range(2):
                        by_channel(slot8(slot_of("q", l, c)), g * P, n, "qk", l, 2 * c + g)
                for t in range(6):
                    wait_drained(pe, "qk", l, t)
                    wait_bank(pe, "perm", l, t)
                    done(mm(bank("perm", l, t)[:, 0:S_LAT], perm[:, :], qkT[:, t, 0:S_LAT]), "perm", l, t)
                for c in range(4):
                    wait_slot(pe, "mqk", l, c)
                    for g in range(2):
                        by_channel(slot8(slot_of("mqk", l, c)), g * P, n if c < 2 else T, "mqk", l, 2 * c + g)
                def by_token(kind, c, tiles):
                    wait_slot(pe, kind, l, c)
                    w = slot8(slot_of(kind, l, c))
                    for h in range(tiles // 2):
                        wait_bank(pe, kind, l, c, h)
                        for t in (2 * h, 2 * h + 1):
                            for k in range(KD):
                                last = mm(bank(kind, l, c, h)[:, (t % 2) * 256:(t % 2 + 1) * 256],
                                          uT[:, k, t * P:(t + 1) * P], w[:, k, :], k == 0, k == KD - 1)
                        done(last, kind, l, c, h)

                def conv_norm(key, src):
                    wait_bank(pe, key, l)
                    for j in range(CT):
                        last = mm(bank(key, l)[:, 0:n], ones_mean[:, :], src[:, j, 0:n], j == 0, j == CT - 1)
                    done(last, key, l)

                by_token("mv", 0, TT)
                by_token("mv", 1, TT)
                pe.wait_ge(conv_ready, l + 1)
                conv_norm("mean", convT)
                by_token("mo", 0, nt)
                pe.wait_ge(sq_ready, l + 1)
                conv_norm("var", sq)

                units = attention_units(l)
                pe.wait_ge(rope_ready, 6 * (l + 1))

                def scores(i):
                    qt, h = units[i]
                    k0, k1 = key_range(qt)
                    r = slice(DH * (h % 2), DH * (h % 2) + DH)
                    wait_bank(pe, "S", l, i)
                    done(mm(bank("S", l, i)[:, k0:k1], qkT[r, h // 2, qt * P:(qt + 1) * P],
                            qkT[r, 4 + h // 4, k0:k1]), "S", l, i)

                scores(0)
                scores(1)
                by_token("mo", 1, nt)
                for i in range(len(units) + 3):
                    if 2 <= i < len(units):
                        scores(i)
                    if 0 <= i - 2 < len(units):
                        m = i - 2
                        k0, k1 = key_range(units[m][0])
                        pe.wait_ge(p_ready, n_att[l] + m + 1)
                        wait_bank(pe, "PT", l, m)
                        for kt in range(k0 // P, k1 // P):
                            last = nc.tensor.transpose(bank("PT", l, m)[:, kt * P:(kt + 1) * P],
                                                       s_buf[:, m % 3, kt * P:(kt + 1) * P], ident[:, :])
                        done(last, "PT", l, m)
                    if 0 <= i - 3 < len(units):
                        m = i - 3
                        qt, h = units[m]
                        k0, k1 = key_range(qt)
                        if m == 0:
                            wait_drained(pe, "v", l)
                        wait_drained(pe, "PT", l, m)
                        wait_bank(pe, "PV", l, m)
                        g = h // 4
                        for kt in range(k0 // P, k1 // P):
                            last = mm(bank("PV", l, m)[:, 0:DH], s_buf[:, 3 + m % 2, kt * P:(kt + 1) * P],
                                      v_tok[:, kt, g * DH:(g + 1) * DH], kt == k0 // P, kt == k1 // P - 1)
                        done(last, "PV", l, m)
                    if i < len(units):
                        modulation(later, i)
                for t in range(nt):
                    wait_bank(pe, "yb_rows", l, t)
                    wait_drained(pe, "PV", l, NQ * (t + 1) - 1)
                    for c in range(4):
                        last = nc.tensor.transpose(bank("yb_rows", l, t)[:, c * P:(c + 1) * P],
                                                   convT[:, t, c * P:(c + 1) * P], ident[:, :])
                    done(last, "yb_rows", l, t)

                pe.wait_ge(gate_em, l + 1)
                wait_bank(pe, "cols", l)
                for i in range(8):
                    src = grow[0:64, 5 if i < 4 else 6, (i % 4) * P:(i % 4 + 1) * P]
                    last = nc.tensor.transpose(bank("cols", l)[:, i * 64:(i + 1) * 64], src, ident[0:64, 0:64])
                done(last, "cols", l)

                for t in range(8):
                    wait_drained(pe, "mqk", l, t)
                for c in range(2):
                    for h in range(TT // 2):
                        wait_drained(pe, "mv", l, c, h)
                for i in range(len(UNITS) + 2):
                    if i < len(UNITS):
                        h, d = UNITS[i]
                        wait_bank(pe, "bm", l, i)
                        done(mm(bank("bm", l, i)[:, 0:n],
                                ident[0:64, 32 * d + h:32 * d + h + 1].broadcast_to([64, P]),
                                negM_tok[:, 0:n]), "bm", l, i)
                    if 0 <= i - 2 < len(UNITS):
                        m = i - 2
                        h, d = UNITS[m]
                        wait_drained(pe, "st", l, m, TT - 1)
                        for half in range(nt // 2):
                            wait_bank(pe, "hv", l, m, half)
                            for t in (2 * half, 2 * half + 1):
                                tiles = scan_tiles(t, d)
                                for s in tiles:
                                    o = (t % 2) * (MH + 1)
                                    last = mm(bank("hv", l, m, half)[:, o:o + MH + 1],
                                              w_buf[:, 4 * (m % 2) + s, t * P:(t + 1) * P],
                                              mv_tok[:, s, h, :], s == tiles[0], s == tiles[-1])
                            done(last, "hv", l, m, half)
                    if 0 <= i - 1 < len(UNITS):
                        h, d = UNITS[i - 1]
                        for s in range(TT):
                            wait_bank(pe, "st", l, i - 1, s)
                            done(mm(bank("st", l, i - 1, s)[:, 0:n], mqk[:, NH + h, s * P:(s + 1) * P],
                                    mqk[:, h, 0:n]), "st", l, i - 1, s)
                    modulation(later, len(units) + i)

                def branch_gates(j):
                    for b in ("bga", "bgb", "bgc"):
                        if j % 2 == 0:
                            wait_slot(pe, b, l, j // 2)
                        by_channel(slot8(slot_of(b, l, j // 2)), (j % 2) * P, n, b, l, j)

                branch_gates(0)
                pe.wait_ge(hn_ready, l + 1)
                for h in range(NH):
                    wait_bank(pe, "yc", l, h)
                    for t in range(nt):
                        last = nc.tensor.transpose(bank("yc", l, h)[:, t * P:(t + 1) * P], hacc[:, t, h, :], ident[:, :])
                    done(last, "yc", l, h)

                pe.wait_ge(ya_ready, CT * (l + 1))
                for t in range(nt):
                    wait_drained(pe, "yb_rows", l, t)
                for j in range(KD):
                    cols = (j % 2) * P
                    if j:
                        branch_gates(j)
                    if j % 2 == 0:
                        wait_slot(pe, "yab", l, j // 2)
                        wait_slot(pe, "yc", l, j // 2)
                    wab, wc = slot8(slot_of("yab", l, j // 2)), slot8(slot_of("yc", l, j // 2))
                    for key, w, k0, y, y0 in (("ya", wab, 0, yab, 0), ("yb", wab, 4, yab, 4), ("yc_", wc, 0, yc, 0)):
                        if key == "yc_" and j == 0:
                            for h in range(NH):
                                wait_drained(pe, "yc", l, h)
                        wait_bank(pe, key, l, j)
                        for k in range(4):
                            last = mm(bank(key, l, j)[:, 0:n], w[:, k0 + k, cols:cols + P], y[:, y0 + k, 0:n],
                                      k == 0, k == 3)
                        done(last, key, l, j)

                def gate_rows(which, first):
                    for x in range(first // 2, first // 2 + 4):
                        wait_drained(pe, "modt", l, x)
                    for c in range(nt):
                        key = ("g1" if which == 0 else "g2", l, c)
                        wait_bank(pe, *key)
                        for j in range(4):
                            last = mm(bank(*key)[:, j * P:(j + 1) * P],
                                      modT[:, l, first + 4 * (c % 2) + j, c // 2:c // 2 + 1].broadcast_to([P, P]),
                                      ident[:, :])
                        done(last, *key)

                gate_rows(0, G1)
                pe.wait_ge(merged_ready, KD * (l + 1))
                for h in range(nt // 2):
                    for c in range(4):
                        if h == 0:
                            wait_slot(pe, "out", l, c)
                        w = slot8(slot_of("out", l, c))
                        wait_bank(pe, "out", l, c, h)
                        for t in (2 * h, 2 * h + 1):
                            for k in range(KD):
                                last = mm(bank("out", l, c, h)[:, (t % 2) * 256:(t % 2 + 1) * 256],
                                          merged[:, k, t * P:(t + 1) * P], w[:, k, :], k == 0, k == KD - 1)
                        done(last, "out", l, c, h)

                for h in range(nt // 2):
                    transposes(1, h)
                    for k in range(KD // 2):
                        wait_drained(pe, "tr2", l, h, k)
                    key = ("router", l, h)
                    wait_bank(pe, *key)
                    for k in range(KD):
                        q = 32 * (k % 4)
                        last = mm(bank(*key)[q:q + 32, 0:256], wrouter[:, k, :], uT[:, k, h * 256:(h + 1) * 256],
                                  k < 4, k >= 4)
                    done(last, *key)
                    if h == nt // 2 - 1:
                        for x in range(nt // 2):
                            wait_drained(pe, "router", l, x)
                        wait_bank(pe, "scores", l)
                        for t in range(nt):
                            last = mm(bank("scores", l)[:, t * NE:(t + 1) * NE], router_rows[:, t * P:(t + 1) * P],
                                      select[:, :])
                        done(last, "scores", l)
                    for t in (2 * h, 2 * h + 1):
                        for c in range(2):
                            wait_bank(pe, "nat", l, t, c)
                            for k in range(4):
                                last = nc.tensor.transpose(bank("nat", l, t, c)[:, k * P:(k + 1) * P],
                                                           uT[:, 4 * c + k, t * P:(t + 1) * P], ident[:, :])
                            done(last, "nat", l, t, c)
                gate_rows(1, G2)
                pe.wait_ge(picked, l + 1)
                wait_bank(pe, "count", l)
                b = bank("count", l)
                for t in range(nt + 1):
                    for x in range(min(t + 1, nt)):
                        last = mm(b[:, t * NE:(t + 1) * NE], before[:, :] if x == t else ones_mean[:, :],
                                  r_rank[:, x, :], x == 0, x == min(t, nt - 1))
                done(last, "count", l)

                last_slots = last_modulation(l)
                for s in range(len(last_slots) + 1):
                    modulation(last_slots, s)
                uses = {}
                final = ("modt",) + last_slots[-1] if last_slots else ("count", l)
                for key in order[:order.index(final) + 1]:
                    uses[place[key][0]] = place[key][1] + 1
                for bk, use in uses.items():
                    pe.wait_ge(drained[bk], use)

                def role_wait(role, count):
                    if not (isinstance(count, int) and count == 0):
                        pe.wait_ge(blk_drained[role], count)

                def x_transposes(b, u, nth):
                    pe.wait_ge(x_blk_loaded[u], nth * 16 + 16 * (loads_before(l, u) + 1))
                    for r, k0 in (("x0", 0), ("x1", 4)):
                        role_wait(r, b + xblk_base[l])
                        for k in range(4):
                            last = nc.tensor.transpose(psum[ROLE[r]][:, k * P:(k + 1) * P],
                                                       x_blk[:, u, (k0 + k) * P:(k0 + k + 1) * P], ident[:, :])
                        last.then_inc(blk_ready[r], 1)

                def up(b, u, role, first, i):
                    for half in range(2):
                        m = index[("moe", l, first, f"{role}{half}")]
                        pe.wait_ge(loaded[m % NS], i * 64 + 32 * (m // NS + 1))
                        if half == 0:
                            role_wait(role, b + blk_base[l])
                        for k in range(4):
                            last = mm(psum[ROLE[role]][:, :], xT_blk[:, u, 4 * half + k, :], slot4(m % NS)[:, k, :],
                                      half == 0 and k == 0, half == 1 and k == 3)
                    last.then_inc(blk_ready[role], 1)

                def hidden(b, u):
                    pe.wait_ge(blk_drained["u"], b + (blk_base[l] + 1))
                    role_wait("h", b + blk_base[l])
                    for k in range(FT):
                        last = nc.tensor.transpose(psum[ROLE["h"]][:, k * P:(k + 1) * P],
                                                   hid_blk[:, u, k * P:(k + 1) * P], ident[:, :])
                    last.then_inc(blk_ready["h"], 1)

                def down(b, u, first, i):
                    pe.wait_ge(blk_drained["h"], b + (blk_base[l] + 1))
                    for half in range(2):
                        m = index[("moe", l, first, f"d{half}")]
                        pe.wait_ge(loaded[m % NS], i * 64 + 32 * (m // NS + 1))
                        role = f"d{half}"
                        role_wait(role, b + blk_base[l])
                        for k in range(FT):
                            last = mm(psum[ROLE[role]][:, :], hT_blk[:, u, k * P:(k + 1) * P], slot4(m % NS)[:, k, :],
                                      k == 0, k == FT - 1)
                        last.then_inc(blk_ready[role], 1)

                def block_products(b, first, i):
                    u = first % 2
                    if first > 0:
                        x_transposes(b + 1, 1 - u, i + (first + 1) // 2)
                    for r in ("x0", "x1"):
                        pe.wait_ge(blk_drained[r], b + (xblk_base[l] + 1))
                    up(b, u, "g", first, i)
                    if first == 0:
                        x_transposes(1, 1, 0)
                    if first > 0:
                        hidden(b - 1, 1 - u)
                    up(b, u, "u", first, i)
                    if first > 0:
                        down(b - 1, 1 - u, first, i)

                nb = n_blocks[l]
                x_transposes(0, 0, 0)
                block_products(0, 0, 0)
                with pe.Fori(0, (nb - 1) // 2) as i:
                    for first in (1, 2):
                        block_products(i * 2 + first, first, i)
                hidden(nb - 1, (nb - 1) % 2)
                down(nb - 1, (nb - 1) % 2, nb, 0)
                for r in ROLE:
                    pe.wait_ge(blk_drained[r], xblk_base[l] + nb + 1 if r[0] == "x" else blk_base[l] + nb)

        @block.scalar
        def _(act):
            chain = [0]

            def link(ins):
                chain[0] += 1
                ins.then_inc(act_chain, 1)
                act.wait_ge(act_chain, chain[0])

            f = nc.scalar.activation
            for dst, src in small:
                act.dma_start(dst, src).then_inc(rows_loaded, 16)
            wait_drained(act, "c")
            f(cT[:, :, 0:2], cT[:, :, 0:2], ACT.Silu).then_inc(c_ready, 1)

            def norm_std(w, h):
                act.wait_ge(ln_var, norm_halves(w) + h + 1)
                f(sd[:, 2 * h:2 * h + 2], mv[:, 2 * h:2 * h + 2, 1], ACT.Sqrt, bias=eps[:, :]).then_inc(ln_std, 1)

            act.wait_ge(consts_set, 1)
            norm_std(0, 0)
            for l in range(DEPTH):
                nt = token_tiles(l)
                n = nt * P
                later = later_modulation(l)

                def modulation(slots, s):
                    if s < len(slots):
                        x = slots[s]
                        wait_ready(act, "mod", *x)
                        if s >= 2:
                            wait_ready(act, "modt", *slots[s - 2])
                        f(mod_rows[:, x[1] % 2, :], bank("mod", *x)[:, 0:256], ACT.Copy)\
                            .then_inc(drained_of("mod", *x), 1)

                if l == 0:
                    modulation(first_modulation(), 0)
                    norm_std(0, 1)
                    for s in range(1, MOD_FIRST):
                        modulation(first_modulation(), s)

                def modulate(which, h, k):
                    key = ("tr2" if which else "tr1", l, h, k)
                    if not on_scalar(which, h, k, nt if which else TT):
                        return
                    wait_ready(act, *key)
                    for c in range(2):
                        x = 2 * k + c
                        last = f(uT[:, x, h * 256:(h + 1) * 256], bank(*key)[:, c * 256:(c + 1) * 256], ACT.Identity,
                                 bias=fold[:, 2 * l + which, 1, x, h:h + 1], scale=fold[:, 2 * l + which, 0, x, h:h + 1])
                    last.then_inc(drained_of(*key), 1)

                def norm_and_modulate(which, after_first):
                    w = 2 * l + which
                    if w:
                        norm_std(w, 0)
                    act.wait_ge(folded, w + 1)
                    for h in range((nt if which else TT) // 2):
                        for k in range(KD // 2):
                            if (h, k) == ((0, 2) if which else (1, 0)) and w and NORM_TILES[w] > 2:
                                norm_std(w, 1)
                            modulate(which, h, k)
                        if which:
                            after_first(h)

                norm_and_modulate(0, None)
                for j in range(CT):
                    if j >= 2:
                        wait_drained(act, "val", l, j - 2)
                    wait_ready(act, "gate", l, j)
                    f(arena[:, 4 + j % 2, 0:n], bank("gate", l, j)[:, 0:n], ACT.Sigmoid).then_inc(drained_of("gate", l, j), 1)
                wait_ready(act, "v", l)
                f(v_tok[:, :, :], bank("v", l)[:, :].rearrange("p (t d) -> p t d", t=TT), ACT.Copy)\
                    .then_inc(drained_of("v", l), 1)
                for t in (4, 5, 0, 1, 2, 3):
                    w = T if t >= 4 else n
                    wait_ready(act, "qk", l, t)
                    f(qkT[:, t, 0:w], bank("qk", l, t)[:, 0:w], ACT.Copy).then_inc(drained_of("qk", l, t), 1)
                for t in range(6):
                    wait_ready(act, "perm", l, t)
                    f(arena[:, t // 2, (t % 2) * S_LAT:(t % 2 + 1) * S_LAT], bank("perm", l, t)[:, 0:S_LAT], ACT.Copy)\
                        .then_inc(drained_of("perm", l, t), 1)
                for t in range(8):
                    w = n if t < 4 else T
                    wait_ready(act, "mqk", l, t)
                    f(mqk[:, t, 0:w], bank("mqk", l, t)[:, 0:w], ACT.Copy,
                      scale=1.0 if t < 4 else K_SCALE).then_inc(drained_of("mqk", l, t), 1)
                def values(c):
                    for h in range(TT // 2):
                        wait_ready(act, "mv", l, c, h)
                        key = ("mv", l, c, h)
                        f(mv_tok[:, 2 * h:2 * h + 2, 2 * c:2 * c + 2, 0:MH],
                          bank(*key)[:, :].rearrange("p (t g d) -> p t g d", t=2, g=2), ACT.Copy)\
                            .then_inc(drained_of(*key), 1)

                def output_gates(c):
                    for h in range(nt // 2):
                        key = ("mo", l, c, h)
                        wait_ready(act, *key)
                        f(mo_tok[:, 2 * h:2 * h + 2, 2 * c:2 * c + 2, :],
                          bank(*key)[:, :].rearrange("p (t g d) -> p t g d", t=2, g=2), ACT.Copy if c else ACT.Sigmoid)\
                            .then_inc(drained_of(*key), 1)

                values(0)
                act.wait_ge(gate_x, l + 1)
                link(f(grow[0:64, 2, :], grow[0:64, 1, :], ACT.Exp))
                f(grow[0:64, 3, :], grow[0:64, 2, :], ACT.Ln, bias=1.0).then_inc(gate_l, 1)
                values(1)
                act.wait_ge(gate_m, l + 1)
                f(grow[0:64, 6, :], grow[0:64, 4, :], ACT.Exp, scale=-1.0).then_inc(gate_em, 1)
                wait_drained(act, "mean", l)
                f(sq[:, :, 0:n], convT[:, :, 0:n], ACT.Square).then_inc(sq_ready, 1)
                act.wait_ge(rows_used, 2 * l + 1)
                output_gates(0)
                for u in range(2):
                    act.wait_ge(y_stored[u], 16)
                wait_ready(act, "var", l)
                f(yab[:, 0, 0:n], bank("var", l)[:, 0:n], ACT.Sqrt, bias=eps[:, :]).then_inc(drained_of("var", l), 1)
                act.wait_ge(scaled_ready, l + 1)
                for j in range(CT):
                    f(yab[:, j, 0:n], convT[:, j, 0:n], ACT.Silu, bias=smallT[:, l, N_MOD + 8 + j:N_MOD + 9 + j],
                      scale=smallT[:, l, N_MOD + 4 + j:N_MOD + 5 + j]).then_inc(ya_ready, 1)
                units = attention_units(l)

                def probs(i):
                    qt, h = units[i]
                    k0, k1 = key_range(qt)
                    act.wait_ge(s_ready, n_att[l] + i + 1)
                    f(s_buf[:, i % 3, k0:k1], s_buf[:, i % 3, k0:k1], ACT.Exp, bias=a_max[:, i % 3, 1:2],
                      accum_out=a_sum[:, i % 3, 0:1])
                    f(a_sum[:, i % 3, 1:2], sink[:, l, h:h + 1], ACT.Exp, bias=a_max[:, i % 3, 1:2])\
                        .then_inc(p_exp, 1)

                probs(0)
                probs(1)
                output_gates(1)
                modulation(later, 0)
                for i in range(len(units) + 2):
                    if 0 <= i - 2 < len(units):
                        m = i - 2
                        k0, k1 = key_range(units[m][0])
                        wait_ready(act, "PT", l, m)
                        if m >= 2:
                            wait_ready(act, "PV", l, m - 2)
                        f(s_buf[:, 3 + m % 2, k0:k1], bank("PT", l, m)[:, k0:k1], ACT.Copy)\
                            .then_inc(drained_of("PT", l, m), 1)
                    if 2 <= i < len(units):
                        probs(i)
                    if 0 < i < len(units):
                        modulation(later, i)

                for h in range(nt // 2):
                    wait_drained(act, "mo", l, 1, h)
                f(mo_tok[:, 0:nt, 2:4, :], mo_tok[:, 0:nt, 2:4, :], ACT.Sigmoid).then_inc(out_gates_ready, 1)
                for t in range(nt):
                    wait_ready(act, "yb_rows", l, t)
                    f(yab[:, 4:8, t * P:(t + 1) * P], bank("yb_rows", l, t)[:, :].rearrange("p (c q) -> p c q", c=4),
                      ACT.Copy).then_inc(drained_of("yb_rows", l, t), 1)

                for i in range(len(UNITS)):
                    h, d = UNITS[i]
                    r = 32 * d + h
                    act.wait_ge(tri_ready, len(UNITS) * l + i + 1)
                    if i >= 2:
                        wait_ready(act, "hv", l, i - 2, nt // 2 - 1)
                    for s in range(TT):
                        if s < nt:
                            last = f(w_buf[:, 4 * (i % 2) + s, s * P:(s + 1) * P], tri_buf[:, i % 2, s, :], ACT.Exp)
                        for t0, t1 in scan_ranges(s, d, n):
                            last = f(w_buf[:, 4 * (i % 2) + s, t0:t1], bank("bm", l, i)[:, t0:t1], ACT.Exp,
                                     bias=gate_cols[:, s, r:r + 1])
                    last.then_inc(drained_of("bm", l, i), 1)
                    modulation(later, len(units) + i)
                act.wait_ge(hc_ready, l + 1)
                f(hsq[:, 0:nt], hacc[:, 0:nt], ACT.Square).then_inc(hsq_ready, 1)
                act.wait_ge(hvar, l + 1)
                f(hstat[:, 2, 0:NH * nt], hstat[:, 1, 0:NH * nt], ACT.Sqrt, bias=eps[:, :], scale=1.0 / MH)\
                    .then_inc(hstd, 1)
                for h in range(NH):
                    wait_ready(act, "yc", l, h)
                    f(yc[:, h, 0:n], bank("yc", l, h)[:, 0:n], ACT.Copy).then_inc(drained_of("yc", l, h), 1)

                for j in range(KD):
                    if j >= 2:
                        wait_drained(act, "yc_", l, j - 2)
                    for b, key in enumerate(("bga", "bgb", "bgc")):
                        wait_ready(act, key, l, j)
                        f(sig[:, 3 * (j % 2) + b, 0:n], bank(key, l, j)[:, 0:n], ACT.Sigmoid)\
                            .then_inc(drained_of(key, l, j), 1)

                def gate_rows(which):
                    for c in range(nt // 2 * 2):
                        key = ("g1" if which == 0 else "g2", l, c)
                        wait_ready(act, *key)
                        f(g_rows[c // 2][:, (c % 2) * 512:(c % 2 + 1) * 512], bank(*key)[:, :], ACT.Copy)\
                            .then_inc(drained_of(*key), 1)

                def rows_and_scores(h):
                    wait_ready(act, "router", l, h)
                    f(router_rows[:, h * 256:(h + 1) * 256], bank("router", l, h)[:, 0:256], ACT.Copy)\
                        .then_inc(drained_of("router", l, h), 1)
                    if h == nt // 2 - 1:
                        wait_ready(act, "scores", l)
                        f(r_sc[:, 0:nt, :], bank("scores", l)[:, 0:nt * NE].rearrange("p (t e) -> p t e", t=nt),
                          ACT.Sigmoid).then_inc(drained_of("scores", l), 1)
                    for t in (2 * h, 2 * h + 1):
                        for c in range(2):
                            wait_ready(act, "nat", l, t, c)
                            f(u_nat[:, t, c * 512:(c + 1) * 512], bank("nat", l, t, c)[:, :], ACT.Copy)\
                                .then_inc(drained_of("nat", l, t, c), 1)

                gate_rows(0)
                norm_and_modulate(1, rows_and_scores)
                for h in range(nt // 2):
                    for c in range(4):
                        wait_drained(act, "out", l, c, h)
                gate_rows(1)
                for s in range(len(last_modulation(l))):
                    modulation(last_modulation(l), s)

                def x_copy(b, u):
                    act.wait_ge(blk_ready["x0"], b + (xblk_base[l] + 1))
                    f(xT_blk[:, u, 0:4, :], psum[ROLE["x0"]][:, :].rearrange("p (k t) -> p k t", k=4), ACT.Copy)\
                        .then_inc(blk_drained["x0"], 1)

                def silu(b, u):
                    act.wait_ge(blk_ready["g"], b + (blk_base[l] + 1))
                    f(silu_blk[:, u, :], psum[ROLE["g"]][:, :], ACT.Silu).then_inc(blk_drained["g"], 1)

                def output(b, u, nth):
                    act.wait_ge(blk_ready["d0"], b + (blk_base[l] + 1))
                    act.wait_ge(y_stored[u], nth * 16 + 16 * stores_before(l, u))
                    f(y_blk[:, u, 0:512], psum[ROLE["d0"]][:, :], ACT.Copy).then_inc(blk_drained["d0"], 1)

                nb = n_blocks[l]
                act.wait_ge(rows_used, 2 * l + 2)
                x_copy(0, 0)
                x_copy(1, 1)
                silu(0, 0)
                with act.Fori(0, (nb - 1) // 2) as i:
                    for first in (1, 2):
                        x_copy(i * 2 + first + 1, (first + 1) % 2)
                        silu(i * 2 + first, first % 2)
                        output(i * 2 + first - 1, (first - 1) % 2, i)
                output(nb - 1, (nb - 1) % 2, (nb - 1) // 2)
                act.wait_ge(counted, l + 1)
                for t in range(nt):
                    act.wait_ge(gathered[t], 32 * (l + 1))
                    f(y_first[:, t, :], y_first[:, t, :], ACT.Copy, scale=r_w[:, 0, t:t + 1]).then_inc(first_scaled, 1)
            norm_std(2 * DEPTH, 0)

        @block.vector
        def _(dve):
            v = nc.vector
            chain = [0]

            def link(ins):
                chain[0] += 1
                ins.then_inc(dve_chain, 1)
                dve.wait_ge(dve_chain, chain[0])

            v.memset(wrouter[:, :, NE:], 0.0)
            v.memset(eps[:, :], EPS)
            v.memset(gate_bias[:, :], 0.0)
            v.memset(ones_mean[:, :], 1.0 / D_CONV).then_inc(consts_set, 1)
            v.memset(wgate[:, :, :], 0.0).then_inc(wgate_cleared, 1)
            v.memset(mv_tok[:, :, :, MH:MH + 1], 1.0)
            v.memset(zeros, 0.0).then_inc(zeros_set, 1)
            v.memset(ones_blk[:, :], 1.0)
            link(v.memset(ones_row[:, :], 1.0))
            link(v.memset(cT[:, :, :], 0.0))
            wait_ready(dve, "c")
            v.tensor_copy(cT[:, :, 0:2], bank("c")[:, 0:16].rearrange("p (c k) -> p k c", c=2))\
                .then_inc(drained_of("c"), 1)

            def norm_half(w, h):
                pair = (2 * h, 2 * h + 1)
                for t in pair:
                    v.bn_stats(st[:, t, 0:6], H[:, t, 0:512])
                    link(v.bn_stats(st[:, t, 6:12], H[:, t, 512:1024]))
                    last = v.bn_aggr(mv[:, t, :], st[:, t, :])
                last.then_inc(ln_var, 1)
                dve.wait_ge(ln_std, norm_halves(w) + h + 1)
                link(v.reciprocal(rstd[:, 2 * h:2 * h + 2], sd[:, 2 * h:2 * h + 2]))
                for t in pair:
                    ins = v.tensor_scalar(H[:, t, :], H[:, t, :], mv[:, t, 0:1], rstd[:, t:t + 1], ALU.subtract, ALU.mult)
                    if w == 2 * DEPTH:
                        link(ins)
                        dve.wait_ge(ln_loaded, 32 * (w + 1))
                        link(v.tensor_tensor(H[:, t, :], H[:, t, :], ln_g, ALU.mult))
                        ins = v.tensor_tensor(H[:, t, :], H[:, t, :], ln_b, ALU.add)
                    ins.then_inc(h_ready, 1)

            def gain_and_bias(w):
                l, which = divmod(w, 2)
                dve.wait_ge(ln_loaded, 32 * (w + 1))
                for t in range(NORM_TILES[w]):
                    if t % 2 == 0:
                        wait_ready(dve, "tr2" if which else "tr1", l, t // 2, KD // 2 - 1)
                        dve.wait_ge(h_ready, 2 * (norm_halves(w) + t // 2 + 1))
                    link(v.scalar_tensor_tensor(H[:, t, :], H[:, t, :], ALPHA, ln_g, ALU.mult, ALU.mult))
                    ins = v.scalar_tensor_tensor(H[:, t, :], ln_b, ALPHA, H[:, t, :], ALU.mult, ALU.add)
                    if t < NORM_TILES[w] - 1:
                        link(ins)
                ins.then_inc(rows_used, 1)
                dve.wait_ge(rows_used, w + 1)

            def fold_norm(w):
                l, which = divmod(w, 2)
                sh, sc = (SH1, SC1) if which == 0 else (SH2, SC2)
                scale, shift = modT[:, l, sc:sc + KD, :], modT[:, l, sh:sh + KD, :]
                g, b = (lnT[:, w, i, :].unsqueeze(2).broadcast_to([P, KD, 2]) for i in range(2))
                v.tensor_tensor(fold[:, w, 0, :, :], scale, g, ALU.mult)
                link(v.tensor_tensor(fold[:, w, 1, :, :], scale, b, ALU.mult))
                v.tensor_tensor(fold[:, w, 1, :, :], fold[:, w, 1, :, :], shift, ALU.add).then_inc(folded, 1)

            def wait_modulation(slots):
                uses = {}
                for x in slots:
                    bk, use = place[("modt",) + x]
                    uses[bk] = use + 1
                for bk, use in uses.items():
                    dve.wait_ge(drained[bk], use)

            for h in range(TT // 2):
                dve.wait_ge(x_loaded[h], 16)
                norm_half(0, h)

            wait_ready(dve, "prep")
            prep = bank("prep")
            v.tensor_copy(lnT[:, :, :, :], prep[:, 384:384 + 32 * DEPTH].rearrange("p (w i k) -> p w i k", w=2 * DEPTH, i=2))
            v.tensor_copy(smallT[:, :, :], prep[:, 0:120].rearrange("p (l c) -> p l c", l=DEPTH))
            v.tensor_copy(cwT[:, :, :, :], prep[:, 136:136 + 8 * TAPS].rearrange("p (l j w) -> p l j w", l=DEPTH, j=CT))\
                .then_inc(drained_of("prep"), 1)
            wait_drained(dve, "prep")
            for sc in (SC1, SC2):
                last = v.tensor_scalar(smallT[:, :, sc:sc + KD], smallT[:, :, sc:sc + KD], 1.0, None, ALU.add)
            link(last)

            for l in range(DEPTH):
                nt = token_tiles(l)
                n = nt * P
                streams = nt // 2

                def modulation(slots, s):
                    if 1 <= s <= len(slots):
                        m, x = slots[s - 1]
                        wait_ready(dve, "modt", m, x)
                        v.tensor_tensor(modT[:, m, 2 * x:2 * x + 2, :],
                                        bank("modt", m, x)[:, 0:4].rearrange("p (m c) -> p m c", c=2),
                                        smallT[:, m, 2 * x:2 * x + 2].unsqueeze(2).broadcast_to([P, 2, 2]), ALU.add)\
                            .then_inc(drained_of("modt", m, x), 1)

                if l == 0:
                    for s in range(1, MOD_FIRST + 1):
                        modulation(first_modulation(), s)
                later = later_modulation(l)
                if l == 0:
                    wait_modulation(first_modulation())
                    fold_norm(0)

                def modulate(which):
                    dve.wait_ge(folded, 2 * l + which + 1)
                    tiles = nt if which else TT
                    for h in range(tiles // 2):
                        for k in range(KD // 2):
                            if on_scalar(which, h, k, tiles):
                                continue
                            key = ("tr2" if which else "tr1", l, h, k)
                            wait_ready(dve, *key)
                            for c in range(2):
                                x = 2 * k + c
                                last = v.tensor_scalar(uT[:, x, h * 256:(h + 1) * 256], bank(*key)[:, c * 256:(c + 1) * 256],
                                                       fold[:, 2 * l + which, 0, x, h:h + 1],
                                                       fold[:, 2 * l + which, 1, x, h:h + 1], ALU.mult, ALU.add)
                            last.then_inc(drained_of(*key), 1)

                modulate(0)

                link(v.memset(upad[:, :, :, :], 0.0))
                for j in range(CT):
                    wait_ready(dve, "val", l, j)
                    wait_drained(dve, "gate", l, j)
                    v.tensor_tensor(upad[:, j, 0:streams, PAD:PAD + S_LAT],
                                    bank("val", l, j)[:, 0:n].rearrange("p (s t) -> p s t", s=streams),
                                    arena[:, 4 + j % 2, 0:n].rearrange("p (s t) -> p s t", s=streams), ALU.mult)\
                        .then_inc(drained_of("val", l, j), 1)
                    wait_drained(dve, "val", l, j)
                gain_and_bias(2 * l)
                wait_ready(dve, "ig", l)
                v.tensor_scalar(grow[:, 7, :], bank("ig", l)[:, :], gate_bias[:, l:l + 1], None, ALU.add)\
                    .then_inc(drained_of("ig", l), 1)
                wait_drained(dve, "ig", l)
                cv = convT[:, :, :].rearrange("p j (s t) -> p j s t", s=2)
                for w in range(TAPS):
                    for j in range(CT):
                        src = upad[:, j, 0:streams, w:w + S_LAT]
                        if w == 0:
                            last = v.tensor_scalar(cv[:, j, 0:streams], src, cwT[:, l, j, 0:1],
                                                   smallT[:, l, N_MOD + j:N_MOD + j + 1], ALU.mult, ALU.add)
                        else:
                            last = v.scalar_tensor_tensor(cv[:, j, 0:streams], src, cwT[:, l, j, w:w + 1],
                                                          cv[:, j, 0:streams], ALU.mult, ALU.add)
                    if w < TAPS - 1:
                        link(last)
                last.then_inc(conv_ready, 1)

                for t in range(6):
                    wait_drained(dve, "perm", l, t)
                    partner = arena[:, t // 2, (t % 2) * S_LAT:(t % 2 + 1) * S_LAT]
                    v.tensor_tensor(partner, partner, rope[:, 1, :], ALU.mult)
                    link(v.tensor_tensor(qkT[:, t, 0:S_LAT], qkT[:, t, 0:S_LAT], rope[:, 0, :], ALU.mult))
                    v.tensor_tensor(qkT[:, t, 0:S_LAT], qkT[:, t, 0:S_LAT], partner, ALU.add).then_inc(rope_ready, 1)
                dve.wait_ge(rope_ready, 6 * (l + 1))
                link(v.tensor_copy(grow[0:64, 0, :], grow[64:128, 7, :]))
                link(v.tensor_scalar(grow[0:64, 1, :], grow[0:64, 0, :], -1.0, None, ALU.mult))
                v.tensor_tensor(grow[0:64, 1, :], grow[0:64, 0, :], grow[0:64, 1, :], ALU.min).then_inc(gate_x, 1)
                dve.wait_ge(gate_l, l + 1)
                link(v.scalar_tensor_tensor(grow[0:64, 0, :], grow[0:64, 0, :], 0.0, grow[0:64, 3, :],
                                            ALU.min, ALU.subtract))

                def reorder(dst, src, back):
                    lat, ctx_ = (slice(0, S_LAT), slice(S_LAT, T))
                    rev_lat, rev_ctx = slice(S_LAT - 1, None, -1), slice(T - 1, S_LAT - 1, -1)
                    if back:
                        v.tensor_copy(dst[0:32, lat], src[0:32, ctx_])
                        v.tensor_copy(dst[0:32, ctx_], src[0:32, lat])
                        v.tensor_copy(dst[32:64, lat], src[32:64, rev_ctx])
                        return v.tensor_copy(dst[32:64, ctx_], src[32:64, rev_lat])
                    v.tensor_copy(dst[0:32, lat], src[0:32, ctx_])
                    v.tensor_copy(dst[0:32, ctx_], src[0:32, lat])
                    v.tensor_copy(dst[32:64, lat], src[32:64, rev_ctx])
                    return v.tensor_copy(dst[32:64, ctx_], src[32:64, rev_lat])

                reorder(grow[0:64, 1, :], grow[0:64, 0, :], False)
                link(reorder(grow[0:64, 2, :], grow[0:64, 7, :], False))
                link(v.tensor_tensor_scan(grow[0:64, 3, :], ones_row[:, :], grow[0:64, 1, :], 0.0, ALU.mult, ALU.add))
                link(v.tensor_tensor(grow[0:64, 2, :], grow[0:64, 2, :], grow[0:64, 3, :], ALU.subtract))
                link(v.tensor_tensor_scan(grow[0:64, 0, :], grow[0:64, 2, :], grow[0:64, 2, :], 0.0, ALU.max, ALU.max))
                link(v.tensor_tensor(grow[0:64, 3, :], grow[0:64, 3, :], grow[0:64, 0, :], ALU.add))
                link(v.tensor_scalar(grow[0:64, 0, :], grow[0:64, 0, :], -1.0, None, ALU.mult))
                reorder(negM_tok[:, :], grow[0:64, 0, :], True)
                reorder(grow[0:64, 5, :], grow[0:64, 2, :], True)
                reorder(grow[0:64, 4, :], grow[0:64, 3, :], True).then_inc(gate_m, 1)
                dve.wait_ge(gate_m, l + 1)
                wait_ready(dve, "mean", l)
                v.tensor_tensor(convT[:, :, 0:n], convT[:, :, 0:n],
                                bank("mean", l)[:, 0:n].unsqueeze(1).broadcast_to([P, CT, n]), ALU.subtract)\
                    .then_inc(drained_of("mean", l), 1)
                wait_drained(dve, "var", l)
                link(v.reciprocal(yab[:, 0, 0:n], yab[:, 0, 0:n]))
                v.tensor_tensor(convT[:, :, 0:n], convT[:, :, 0:n],
                                yab[:, 0:1, 0:n].broadcast_to([P, CT, n]), ALU.mult).then_inc(scaled_ready, 1)

                units = attention_units(l)
                def denominator(m):
                    b = m % 3
                    k0, k1 = key_range(units[m][0])
                    dve.wait_ge(p_exp, n_att[l] + m + 1)
                    link(v.tensor_tensor(a_sum[:, b, 2:3], a_sum[:, b, 0:1], a_sum[:, b, 1:2], ALU.add))
                    v.reciprocal(a_rden[:, m % 4, :], a_sum[:, b, 2:3]).then_inc(p_ready, 1)

                for i in range(len(units) + 3):
                    if i == 2:
                        denominator(1)
                    if i < len(units):
                        qt, h = units[i]
                        k0, k1 = key_range(qt)
                        b = i % 3
                        wait_ready(dve, "S", l, i)
                        if i >= 3:
                            wait_ready(dve, "PT", l, i - 3)
                        if k0 == 0:
                            ins = v.scalar_tensor_tensor(s_buf[:, b, :], bank("S", l, i)[:, :], A_SCALE, band[:, qt, :],
                                                         ALU.mult, ALU.add)
                        else:
                            ins = v.tensor_scalar(s_buf[:, b, k0:k1], bank("S", l, i)[:, k0:k1], A_SCALE, None, ALU.mult)
                        ins.then_inc(drained_of("S", l, i), 1)
                        wait_drained(dve, "S", l, i)
                        link(v.tensor_reduce(a_max[:, b, 0:1], s_buf[:, b, k0:k1], AX_X, ALU.max))
                        v.tensor_scalar(a_max[:, b, 1:2], a_max[:, b, 0:1], sink[:, l, h:h + 1], -1.0,
                                        ALU.max, ALU.mult).then_inc(s_ready, 1)
                    if 0 <= i - 1 < len(units) and i != 2:
                        denominator(i - 1)
                    if 0 <= i - 3 < len(units):
                        m = i - 3
                        qt, h = units[m]
                        wait_ready(dve, "PV", l, m)
                        dve.wait_ge(p_ready, n_att[l] + m + 1)
                        if m == 0:
                            dve.wait_ge(ya_ready, CT * (l + 1))
                        v.tensor_scalar(convT[:, qt, h * DH:(h + 1) * DH], bank("PV", l, m)[:, 0:DH],
                                        a_rden[:, m % 4, :], None, ALU.mult).then_inc(drained_of("PV", l, m), 1)
                    if i < len(units):
                        modulation(later, i)
                wait_ready(dve, "cols", l)
                v.tensor_copy(gate_cols[:, :, :], bank("cols", l)[:, :].rearrange("p (i r) -> p i r", i=8))\
                    .then_inc(drained_of("cols", l), 1)
                wait_drained(dve, "cols", l)


                def triangles(i):
                    h, d = UNITS[i]
                    r = 32 * d + h
                    wait_ready(dve, "bm", l, i)
                    if i >= 2:
                        wait_drained(dve, "bm", l, i - 2)
                    for s in range(nt):
                        last = v.scalar_tensor_tensor(tri_buf[:, i % 2, s, :], bank("bm", l, i)[:, s * P:(s + 1) * P],
                                                      gate_cols[:, s, r:r + 1], tri[:, d, :], ALU.add, ALU.add)
                    last.then_inc(tri_ready, 1)

                def weights(i):
                    h, d = UNITS[i]
                    wait_drained(dve, "bm", l, i)
                    for s in range(TT):
                        wait_ready(dve, "st", l, i, s)
                        own = [(s * P, (s + 1) * P)] if s < nt else []
                        for t0, t1 in joined(scan_ranges(s, d, n) + own):
                            w = w_buf[:, 4 * (i % 2) + s, t0:t1]
                            last = v.tensor_tensor(w, bank("st", l, i, s)[:, t0:t1], w, ALU.mult)
                        last.then_inc(drained_of("st", l, i, s), 1)

                def outputs(i):
                    h, d = UNITS[i]
                    r = 32 * d + h
                    for half in range(nt // 2):
                        b = bank("hv", l, i, half)
                        wait_ready(dve, "hv", l, i, half)
                        raw = b[:, MH:2 * MH + 2:MH + 1]
                        link(v.scalar_tensor_tensor(den[:, 0, :], raw, -1.0, gate_cols[:, 4 + 2 * half:6 + 2 * half, r],
                                                    ALU.mult, ALU.max))
                        link(v.tensor_tensor(den[:, 1, :], raw, den[:, 0, :], ALU.max))
                        link(v.reciprocal(den[:, 2, :], den[:, 1, :]))
                        for t in range(2):
                            dst = hacc[:, 2 * half + t, h, :]
                            src = b[:, t * (MH + 1):t * (MH + 1) + MH]
                            if d == 0:
                                last = v.tensor_scalar(dst, src, den[:, 2, t:t + 1], None, ALU.mult)
                            else:
                                last = v.scalar_tensor_tensor(dst, src, den[:, 2, t:t + 1], dst, ALU.mult, ALU.add)
                        last.then_inc(drained_of("hv", l, i, half), 1)
                        wait_drained(dve, "hv", l, i, half)

                for i in range(len(UNITS) + 2):
                    if i < len(UNITS):
                        triangles(i)
                    if 0 <= i - 2 < len(UNITS):
                        outputs(i - 2)
                    if 0 <= i - 1 < len(UNITS):
                        weights(i - 1)
                    modulation(later, len(units) + i)

                if l == 0:
                    wait_modulation(later)
                    for w in range(1, 2 * DEPTH):
                        fold_norm(w)

                hs = hstat[:, :, 0:NH * nt].rearrange("p a (t h) -> p a t h", t=nt)
                hv = hacc[:, 0:nt]
                link(v.tensor_reduce(hs[:, 0], hv, AX_X, ALU.add))
                link(v.tensor_scalar(hs[:, 0], hs[:, 0], 1.0 / MH, None, ALU.mult))
                v.tensor_tensor(hv, hv, hs[:, 0].unsqueeze(3).broadcast_to([P, nt, NH, MH]), ALU.subtract)\
                    .then_inc(hc_ready, 1)
                dve.wait_ge(hsq_ready, l + 1)
                v.tensor_reduce(hs[:, 1], hsq[:, 0:nt], AX_X, ALU.add).then_inc(hvar, 1)
                dve.wait_ge(hstd, l + 1)
                link(v.reciprocal(hs[:, 3], hs[:, 2]))
                link(v.tensor_tensor(hv, hv, hs[:, 3].unsqueeze(3).broadcast_to([P, nt, NH, MH]), ALU.mult))
                gain = norm_g[:, l, :].rearrange("p (h d) -> p h d", h=NH)
                link(v.tensor_tensor(hv, hv, gain.unsqueeze(1).broadcast_to([P, nt, NH, MH]), ALU.mult))
                wait_drained(dve, "mo", l, 0, nt // 2 - 1)
                dve.wait_ge(out_gates_ready, l + 1)
                v.tensor_tensor(hv, hv, mo_tok[:, 0:nt], ALU.mult).then_inc(hn_ready, 1)

                for j in range(KD):
                    for b, (key, gkey) in enumerate((("ya", "bga"), ("yb", "bgb"), ("yc_", "bgc"))):
                        wait_ready(dve, key, l, j)
                        wait_drained(dve, gkey, l, j)
                        dst = merged[:, j, 0:n] if b == 0 else sig[:, 6, 0:n]
                        v.tensor_tensor(dst, bank(key, l, j)[:, 0:n], sig[:, 3 * (j % 2) + b, 0:n], ALU.mult)\
                            .then_inc(drained_of(key, l, j), 1)
                        wait_drained(dve, key, l, j)
                        if b == 1:
                            link(v.tensor_tensor(merged[:, j, 0:n], merged[:, j, 0:n], sig[:, 6, 0:n], ALU.add))
                        if b == 2:
                            v.tensor_tensor(merged[:, j, 0:n], merged[:, j, 0:n], sig[:, 6, 0:n], ALU.add)\
                                .then_inc(merged_ready, 1)
                            dve.wait_ge(merged_ready, l * KD + j + 1)

                for h in range(nt // 2):
                    for c in range(4):
                        if (c, h) == (0, 0):
                            for x in range(nt):
                                wait_drained(dve, "g1", l, x)
                        key = ("out", l, c, h)
                        wait_ready(dve, *key)
                        tmp = sig[:, 6, :].rearrange("p (t d) -> p t d", t=2)
                        hh = H[:, 2 * h:2 * h + 2, c * 256:(c + 1) * 256]
                        g = g_rows[h][:, c * 256:(c + 1) * 256].unsqueeze(1).broadcast_to([P, 2, 256])
                        v.tensor_tensor(tmp, bank(*key)[:, :].rearrange("p (t d) -> p t d", t=2), g, ALU.mult)\
                            .then_inc(drained_of(*key), 1)
                        wait_drained(dve, *key)
                        link(v.tensor_tensor(hh, hh, tmp, ALU.add))
                    norm_half(2 * l + 1, h)
                modulate(1)

                wait_drained(dve, "scores", l)
                rs = r_sel[:, 0:nt, :].rearrange("p t (g e) -> p t g e", g=NG)
                rk = r_rank[:, 0:nt, :].rearrange("p t (g e) -> p t g e", g=NG)
                rc = r_cmp[:, 0:nt, :].rearrange("p t (g e) -> p t g e", g=NG)
                link(v.tensor_tensor(r_sel[:, 0:nt, :], r_sc[:, 0:nt, :],
                                     b_router[:, :].unsqueeze(1).broadcast_to([P, nt, NE]), ALU.add))
                hi = r_hi[:, 0:nt]
                v.tensor_tensor(hi[:, :, :, 0:2], rs[:, :, :, 0:3:2], rs[:, :, :, 1:4:2], ALU.max)
                link(v.tensor_tensor(hi[:, :, :, 2:4], rs[:, :, :, 0:3:2], rs[:, :, :, 1:4:2], ALU.min))
                gs, gc, gr = r_gs[:, 0:nt], r_gcmp[:, 0:nt], r_grank[:, 0:nt]
                v.tensor_tensor(gs, hi[:, :, :, 0], hi[:, :, :, 1], ALU.max)
                v.tensor_tensor(gc, hi[:, :, :, 0], hi[:, :, :, 1], ALU.min)
                link(v.tensor_tensor(gr, hi[:, :, :, 2], hi[:, :, :, 3], ALU.max))
                link(v.tensor_tensor(gc, gc, gr, ALU.max))
                link(v.tensor_tensor(gs, gs, gc, ALU.add))
                for e in range(4):
                    v.memset(r_grank[:, :, e:e + 1], float(3 - e))
                    last = v.memset(r_rank[:, :, :].rearrange("p t (g e) -> p t g e", g=NG)[:, :, :, e:e + 1], float(3 - e))
                link(last)
                for sft in range(1, 4):
                    k = 4 - sft
                    link(v.tensor_tensor(gc[:, :, 0:k], gs[:, :, 0:k], gs[:, :, sft:4], ALU.is_ge))
                    link(v.tensor_tensor(gr[:, :, sft:4], gr[:, :, sft:4], gc[:, :, 0:k], ALU.add))
                    link(v.tensor_tensor(gr[:, :, 0:k], gr[:, :, 0:k], gc[:, :, 0:k], ALU.subtract))
                    link(v.tensor_tensor(rc[:, :, :, 0:k], rs[:, :, :, 0:k], rs[:, :, :, sft:4], ALU.is_ge))
                    link(v.tensor_tensor(rk[:, :, :, sft:4], rk[:, :, :, sft:4], rc[:, :, :, 0:k], ALU.add))
                    link(v.tensor_tensor(rk[:, :, :, 0:k], rk[:, :, :, 0:k], rc[:, :, :, 0:k], ALU.subtract))
                first, second = r_pick[:, 0, 0:nt], r_pick[:, 1, 0:nt]
                fg = first.rearrange("p t (g e) -> p t g e", g=NG)
                link(v.tensor_scalar(gr, gr, 0.5, None, ALU.is_lt))
                in_group = gr.unsqueeze(3).broadcast_to([P, nt, NG, EPG])
                v.tensor_scalar(fg, rk, 0.5, None, ALU.is_lt)
                link(v.tensor_scalar(rk, rk, 1.5, None, ALU.is_lt))
                v.tensor_tensor(fg, fg, in_group, ALU.mult)
                v.tensor_tensor(rk, rk, in_group, ALU.mult).then_inc(picked, 1)
                dve.wait_ge(picked, l + 1)
                v.tensor_tensor(second, r_rank[:, 0:nt, :], first, ALU.subtract)
                link(v.tensor_tensor(r_sel[:, 0:nt, :], r_rank[:, 0:nt, :], r_sc[:, 0:nt, :], ALU.mult))
                link(v.tensor_reduce(r_sum[:, 0:nt], r_sel[:, 0:nt, :], AX_X, ALU.add))
                link(v.reciprocal(r_sum[:, 0:nt], r_sum[:, 0:nt]))
                link(v.tensor_tensor(gates[:, 0:nt, :], r_sel[:, 0:nt, :],
                                     r_sum[:, 0:nt].unsqueeze(2).broadcast_to([P, nt, NE]), ALU.mult))

                wait_ready(dve, "count", l)
                v.tensor_scalar(r_cnt[:, 0:(nt + 1) * NE], bank("count", l)[:, 0:(nt + 1) * NE], float(D_CONV), None,
                                ALU.mult).then_inc(drained_of("count", l), 1)
                wait_drained(dve, "count", l)
                total = r_cnt[:, nt * NE:(nt + 1) * NE]
                link(v.tensor_scalar(r_blk[:, 0, :], total, 0.0, None, ALU.is_gt))
                for j in range(1, nt * P // CAP):
                    link(v.scalar_tensor_tensor(r_blk[:, 0, :], total, float(j * CAP), r_blk[:, 0, :], ALU.is_gt, ALU.add))
                link(v.tensor_tensor_scan(r_blk[:, 1, :], ones_blk[:, :], r_blk[:, 0, :], 0.0, ALU.mult, ALU.add))
                link(v.tensor_tensor(r_blk[:, 2, :], r_blk[:, 1, :], r_blk[:, 0, :], ALU.subtract))
                link(v.tensor_scalar(r_blk[:, 2, :], r_blk[:, 2, :], float(CAP), None, ALU.mult))
                cnt = r_cnt[:, 0:nt * NE].rearrange("p (t e) -> p t e", t=nt)
                link(v.tensor_tensor(cnt, cnt, r_blk[:, 2:3, :].broadcast_to([P, nt, NE]), ALU.add))
                for c in range(2):
                    pick = r_pick[:, c, 0:nt]
                    v.tensor_tensor(r_cmp[:, 0:nt], pick, cnt, ALU.mult)
                    link(v.tensor_tensor(r_sel[:, 0:nt], pick, gates[:, 0:nt], ALU.mult))
                    v.tensor_reduce(r_slot[:, c, 0:nt], r_cmp[:, 0:nt], AX_X, ALU.add)
                    link(v.tensor_reduce(r_w[:, c, 0:nt], r_sel[:, 0:nt], AX_X, ALU.add))
                if l:
                    for t in range(TT):
                        dve.wait_ge(gathered[t], 32 * l)
                v.tensor_copy(slot_id[:, :, 0:nt], r_slot[:, :, 0:nt])
                link(v.tensor_tensor(r_cover[:, :, :], block_row[0:1, 0:24].unsqueeze(2).broadcast_to([1, 24, NE]),
                                     r_blk[0:1, 1:2, :].broadcast_to([1, 24, NE]), ALU.is_ge))
                link(v.tensor_reduce(r_expert[:, :], r_cover[:, :, :], AX_X, ALU.add))
                link(v.tensor_scalar(r_expert[:, :], r_expert[:, :], float(NE - 1), None, ALU.min))
                v.tensor_copy(expert_id[:, :], r_expert[:, :]).then_inc(counted, 1)

                for s in range(1, len(last_modulation(l)) + 1):
                    modulation(last_modulation(l), s)
                gain_and_bias(2 * l + 1)

                def x_copy(b, u):
                    dve.wait_ge(blk_ready["x1"], b + (xblk_base[l] + 1))
                    v.tensor_copy(xT_blk[:, u, 4:8, :], psum[ROLE["x1"]][:, :].rearrange("p (k t) -> p k t", k=4))\
                        .then_inc(blk_drained["x1"], 1)

                def hidden(b, u):
                    dve.wait_ge(blk_drained["g"], b + (blk_base[l] + 1))
                    dve.wait_ge(blk_ready["u"], b + (blk_base[l] + 1))
                    v.tensor_tensor(hid_blk[:, u, :], psum[ROLE["u"]][:, :], silu_blk[:, u, :], ALU.mult)\
                        .then_inc(blk_drained["u"], 1)

                def hidden_copy(b, u):
                    dve.wait_ge(blk_ready["h"], b + (blk_base[l] + 1))
                    v.tensor_copy(hT_blk[:, u, :], psum[ROLE["h"]][:, :]).then_inc(blk_drained["h"], 1)

                def output(b, u, nth):
                    dve.wait_ge(blk_ready["d1"], b + (blk_base[l] + 1))
                    dve.wait_ge(y_stored[u], nth * 16 + 16 * stores_before(l, u))
                    v.tensor_copy(y_blk[:, u, 512:1024], psum[ROLE["d1"]][:, :]).then_inc(blk_drained["d1"], 1)

                nb = n_blocks[l]
                x_copy(0, 0)
                x_copy(1, 1)
                hidden(0, 0)
                with dve.Fori(0, (nb - 1) // 2) as i:
                    for first in (1, 2):
                        u = first % 2
                        x_copy(i * 2 + first + 1, 1 - u)
                        hidden_copy(i * 2 + first - 1, 1 - u)
                        hidden(i * 2 + first, u)
                        output(i * 2 + first - 1, 1 - u, i)
                hidden_copy(nb - 1, (nb - 1) % 2)
                output(nb - 1, (nb - 1) % 2, (nb - 1) // 2)

                for x in range(nt):
                    wait_drained(dve, "g2", l, x)
                for h in range(nt // 2):
                    for t in (2 * h, 2 * h + 1):
                        dve.wait_ge(gathered[t], 32 * (l + 1))
                        dve.wait_ge(first_scaled, sum(token_tiles(x) for x in range(l)) + t + 1)
                        link(v.scalar_tensor_tensor(y_first[:, t, :], y_second[:, t, :], r_w[:, 1, t:t + 1],
                                                    y_first[:, t, :], ALU.mult, ALU.add))
                        link(v.tensor_tensor(y_first[:, t, :], y_first[:, t, :], g_rows[t // 2], ALU.mult))
                        link(v.tensor_tensor(H[:, t, :], H[:, t, :], y_first[:, t, :], ALU.add))
                    norm_half(2 * l + 2, h)


INPUTS = ["x", "c", "ctx", "c_ctx", "ln_in_g", "ln_in_b", "w_router", "b_router", "w_mod", "b_mod", "w_in", "conv_w",
          "conv_b", "conv_ln_g", "conv_ln_b", "w_a_out", "attn_sink", "w_b_out", "mlstm_gate_b", "mlstm_norm_g",
          "w_c_out", "w_out", "ln1_g", "ln1_b", "moe_w_gu", "moe_w_dn", "ln2_g", "ln2_b"]


def kernel(**inputs):
    import concourse.bacc as bacc
    from concourse.bass_utils import run_bass_kernel_spmd

    nc = bacc.Bacc("TRN2", target_bir_lowering=False, num_devices=1)
    arrays, aps = {}, {}
    host = {name: np.ascontiguousarray(inputs[name]) for name in INPUTS}
    host.update(host_constants())
    for name, value in host.items():
        arrays[f"in_{name}"] = value
        aps[name] = nc.dram_tensor(f"in_{name}", value.shape, mybir.dt.from_np(value.dtype), kind="ExternalInput").ap()
    out = nc.dram_tensor("out", (1, S_LAT, D), F32, kind="ExternalOutput").ap()
    build(nc, aps, out)
    result = run_bass_kernel_spmd(nc, [arrays], core_ids=[0])
    return result.results[0]["out"]
```
